# Optimizing a Trainium2 kernel written in Bass

```python
import jax, jax.numpy as jnp
from jax import lax
import numpy as np
import math, functools

D_MODEL = 1024
BATCH = 1
SEQ = 512
DEPTH = 2

POOL_GROUPS = 4
POOL_WINDOWS = (2, 4, 8, 16)
POOL_WIDTH = 3 * D_MODEL // 8
POOL_GROUP_DIM = POOL_WIDTH // POOL_GROUPS
CONV_WIDTH = 3 * D_MODEL // 8
HEAD_DIM = 64
DIL_CONFIGS = ((128, 1), (512, 4), (2048, 16))
HEADS_PER_GROUP = 4
ATTN_HEADS = HEADS_PER_GROUP * len(DIL_CONFIGS)
ATTN_WIDTH = ATTN_HEADS * HEAD_DIM
ATTN_OUT_WIDTH = HEADS_PER_GROUP * HEAD_DIM
ROT_DIM = HEAD_DIM // 4
ROPE_THETA = 500000.0
QUERY_BLOCK = 128
N_BRANCHES = 3
IN_SPLITS = (POOL_WIDTH, CONV_WIDTH, CONV_WIDTH, CONV_WIDTH, ATTN_WIDTH, ATTN_WIDTH, ATTN_WIDTH, N_BRANCHES * D_MODEL)
IN_WIDTH = POOL_WIDTH + 3 * CONV_WIDTH + 3 * ATTN_WIDTH + N_BRANCHES * D_MODEL
MEM_LEN = 256
MEM_HEADS = 4
MEM_HEAD_DIM = D_MODEL // 8
MEM_WIDTH = MEM_HEADS * MEM_HEAD_DIM
D_FF = ((8 * D_MODEL // 3 + 127) // 128) * 128
CONV_K = 3
RMS_EPS = 1e-6


def rmsnorm(x, g):
    xf = x.astype(jnp.float32)
    y = xf * lax.rsqrt(jnp.mean(xf * xf, axis=-1, keepdims=True) + RMS_EPS)
    return (y * g.astype(jnp.float32)).astype(x.dtype)

def split_cols(u, sizes):
    outs, start = [], 0
    for s in sizes:
        outs.append(u[..., start:start + s])
        start += s
    return outs

def causal_dwconv(u, w):
    k, c = w.shape
    return lax.conv_general_dilated(
        u, w[:, None, :].astype(u.dtype), window_strides=(1,), padding=((k - 1, 0),),
        dimension_numbers=("NWC", "WIO", "NWC"), feature_group_count=c)

def rope_tables(positions):
    inv = ROPE_THETA ** (-jnp.arange(0, ROT_DIM, 2, dtype=jnp.float32) / ROT_DIM)
    ang = positions.astype(jnp.float32)[..., None] * inv
    return jnp.cos(ang)[:, :, None, :], jnp.sin(ang)[:, :, None, :]

def apply_partial_rope(u, cos, sin):
    half = ROT_DIM // 2
    uf = u[..., :ROT_DIM].astype(jnp.float32)
    u1, u2 = uf[..., :half], uf[..., half:]
    rot = jnp.concatenate([u1 * cos - u2 * sin, u2 * cos + u1 * sin], axis=-1).astype(u.dtype)
    return jnp.concatenate([rot, u[..., ROT_DIM:]], axis=-1)

def multiscale_pool(u, pool_w, pool_scale):
    b, s, _ = u.shape
    ug = u.reshape(b, s, POOL_GROUPS, POOL_GROUP_DIM).astype(jnp.float32)
    cs = jnp.cumsum(ug, axis=1)
    t = jnp.arange(s)
    outs = []
    for g, w in enumerate(POOL_WINDOWS):
        c = cs[:, :, g]
        prev = jnp.pad(c, ((0, 0), (w, 0), (0, 0)))[:, :s]
        cnt = jnp.minimum(t + 1, w).astype(jnp.float32)[None, :, None]
        outs.append((c - prev) / cnt - ug[:, :, g])
    pooled = jnp.stack(outs, axis=2)
    mixed = jnp.einsum("bsgc,gcd->bsgd", pooled, pool_w.astype(jnp.float32))
    return (mixed.reshape(b, s, POOL_WIDTH) * pool_scale.astype(jnp.float32)).astype(u.dtype)

def dilated_attention(q, k, v):
    b, s, _, hd = q.shape
    ng = len(DIL_CONFIGS)
    def grp(u):
        return u.reshape(b, s, ng, HEADS_PER_GROUP, hd).transpose(2, 0, 3, 1, 4)
    qg, kg, vg = grp(q), grp(k), grp(v)
    scale = hd ** -0.5

    def block(bi):
        start = bi * QUERY_BLOCK
        t = start + jnp.arange(QUERY_BLOCK)
        qb = lax.dynamic_slice_in_dim(qg, start, QUERY_BLOCK, axis=3)
        outs, lses = [], []
        for g, (window, dil) in enumerate(DIL_CONFIGS):
            offs = jnp.arange(window // dil + 1) * dil
            idx = t[:, None] - offs[None, :]
            valid = idx >= 0
            idx = jnp.maximum(idx, 0)
            kk = jnp.take(kg[g], idx, axis=2)
            vv = jnp.take(vg[g], idx, axis=2)
            sc = jnp.einsum("bhqd,bhqkd->bhqk", qb[g], kk).astype(jnp.float32) * scale
            sc = jnp.where(valid, sc, -jnp.inf)
            m = jnp.max(sc, axis=-1, keepdims=True)
            p = jnp.exp(sc - m)
            den = jnp.sum(p, axis=-1, keepdims=True)
            o = jnp.einsum("bhqk,bhqkd->bhqd", p, vv.astype(jnp.float32)) / den
            outs.append(o)
            lses.append(m + jnp.log(den))
        wts = jax.nn.softmax(jnp.stack(lses, axis=0), axis=0)
        return jnp.sum(wts * jnp.stack(outs, axis=0), axis=0).astype(q.dtype)

    out = lax.map(block, jnp.arange(s // QUERY_BLOCK))
    return out.transpose(1, 0, 3, 2, 4).reshape(b, s, ATTN_OUT_WIDTH)

def memory_cross_attention(h, mem_n, w_q, w_kv, w_o):
    b, s, _ = h.shape
    q = (h @ w_q).reshape(b, s, MEM_HEADS, MEM_HEAD_DIM)
    kv = mem_n @ w_kv
    k = kv[..., :MEM_WIDTH].reshape(b, -1, MEM_HEADS, MEM_HEAD_DIM)
    v = kv[..., MEM_WIDTH:].reshape(b, -1, MEM_HEADS, MEM_HEAD_DIM)
    sc = jnp.einsum("bshd,bmhd->bhsm", q, k).astype(jnp.float32) * (MEM_HEAD_DIM ** -0.5)
    p = jax.nn.softmax(sc, axis=-1)
    o = jnp.einsum("bhsm,bmhd->bshd", p, v.astype(jnp.float32)).astype(h.dtype)
    return o.reshape(b, s, MEM_WIDTH) @ w_o

def first_inputs(seed: int = 0) -> dict:
    key = jax.random.key(seed)
    ks = jax.random.split(key, 32)
    f32 = jnp.float32

    def nrm(k, shape, fan_in):
        return jax.random.normal(k, shape, f32) * (fan_in ** -0.5)

    def gain(k, n):
        return 1.0 + 0.05 * jax.random.normal(k, (DEPTH, n), f32)

    return {
        "x": jax.random.normal(ks[0], (BATCH, SEQ, D_MODEL), f32),
        "mem": jax.random.normal(ks[1], (BATCH, MEM_LEN, D_MODEL), f32),
        "positions": jnp.broadcast_to(jnp.arange(SEQ, dtype=jnp.int32), (BATCH, SEQ)),
        "norm_mix_pre": gain(ks[2], D_MODEL),
        "norm_mix_post": gain(ks[3], D_MODEL),
        "w_in": nrm(ks[4], (DEPTH, D_MODEL, IN_WIDTH), D_MODEL),
        "pool_w": nrm(ks[5], (DEPTH, POOL_GROUPS, POOL_GROUP_DIM, POOL_GROUP_DIM), POOL_GROUP_DIM),
        "pool_scale": 1.0 + 0.1 * jax.random.normal(ks[6], (DEPTH, POOL_WIDTH), f32),
        "conv_b_w": nrm(ks[7], (DEPTH, CONV_K, CONV_WIDTH), CONV_K),
        "w_branch_a": nrm(ks[8], (DEPTH, POOL_WIDTH, D_MODEL), POOL_WIDTH),
        "w_branch_b": nrm(ks[9], (DEPTH, CONV_WIDTH, D_MODEL), CONV_WIDTH),
        "w_branch_c": nrm(ks[10], (DEPTH, ATTN_OUT_WIDTH, D_MODEL), ATTN_OUT_WIDTH),
        "w_out": nrm(ks[11], (DEPTH, D_MODEL, D_MODEL), D_MODEL),
        "norm_mem_pre": gain(ks[12], D_MODEL),
        "norm_mem_post": gain(ks[13], D_MODEL),
        "norm_memkv": gain(ks[14], D_MODEL),
        "w_mq": nrm(ks[15], (DEPTH, D_MODEL, MEM_WIDTH), D_MODEL),
        "w_mkv": nrm(ks[16], (DEPTH, D_MODEL, 2 * MEM_WIDTH), D_MODEL),
        "w_mo": nrm(ks[17], (DEPTH, MEM_WIDTH, D_MODEL), MEM_WIDTH),
        "norm_ffn_pre": gain(ks[18], D_MODEL),
        "norm_ffn_post": gain(ks[19], D_MODEL),
        "w_up": nrm(ks[20], (DEPTH, D_MODEL, 2 * D_FF), D_MODEL),
        "conv_ffn_w": nrm(ks[21], (DEPTH, CONV_K, D_FF), CONV_K),
        "w_down": nrm(ks[22], (DEPTH, D_FF, D_MODEL), D_FF),
    }

def first_block(x, mem, positions, norm_mix_pre, norm_mix_post, w_in, pool_w, pool_scale, conv_b_w,
              w_branch_a, w_branch_b, w_branch_c, w_out, norm_mem_pre, norm_mem_post, norm_memkv,
              w_mq, w_mkv, w_mo, norm_ffn_pre, norm_ffn_post, w_up, conv_ffn_w, w_down):
    b, s, d = x.shape
    cos, sin = rope_tables(positions)
    cos, sin = cos.astype(x.dtype), sin.astype(x.dtype)
    for l in range(DEPTH):
        h = rmsnorm(x, norm_mix_pre[l])
        a_in, b_x, b_b, b_c, q, k, v, gate_in = split_cols(h @ w_in[l], IN_SPLITS)
        br_a = multiscale_pool(a_in, pool_w[l], pool_scale[l]) @ w_branch_a[l]
        br_b = (b_b * causal_dwconv(b_c * b_x, conv_b_w[l])) @ w_branch_b[l]
        q = apply_partial_rope(q.reshape(b, s, ATTN_HEADS, HEAD_DIM), cos, sin)
        k = apply_partial_rope(k.reshape(b, s, ATTN_HEADS, HEAD_DIM), cos, sin)
        v = v.reshape(b, s, ATTN_HEADS, HEAD_DIM)
        br_c = dilated_attention(q, k, v) @ w_branch_c[l]
        gates = jax.nn.sigmoid(gate_in.astype(jnp.float32)).astype(x.dtype).reshape(b, s, N_BRANCHES, d)
        merged = gates[:, :, 0] * br_a + gates[:, :, 1] * br_b + gates[:, :, 2] * br_c
        x = x + rmsnorm(merged @ w_out[l], norm_mix_post[l])
        h = rmsnorm(x, norm_mem_pre[l])
        mem_n = rmsnorm(mem, norm_memkv[l])
        x = x + rmsnorm(memory_cross_attention(h, mem_n, w_mq[l], w_mkv[l], w_mo[l]), norm_mem_post[l])
        h = rmsnorm(x, norm_ffn_pre[l])
        u = h @ w_up[l]
        ua, ub = u[..., :D_FF], u[..., D_FF:]
        y = (jax.nn.silu(causal_dwconv(ua, conv_ffn_w[l])) * ub) @ w_down[l]
        x = x + rmsnorm(y, norm_ffn_post[l])
    return x


GRID_W = 64
CTX_LEN = 256
ROPE_THETA_2 = 10000.0
ROPE_FREQS = HEAD_DIM // 4
Q_BLOCK = 128
A_HEADS = 8
A_KV_HEADS = 2
B_HEADS = 4
B_V_DIM = 2 * HEAD_DIM
C_HEADS = 8
C_KV_HEADS = 2
C_WINDOW = 128
D_HEADS = 8
NA_ROWS = 8
NA_COLS = 16
EVEN_SPLITS = (A_HEADS * HEAD_DIM, A_KV_HEADS * HEAD_DIM, A_KV_HEADS * HEAD_DIM,
               2 * B_HEADS * HEAD_DIM, 2 * B_HEADS * HEAD_DIM, B_HEADS * B_V_DIM)
ODD_SPLITS = (C_HEADS * HEAD_DIM, C_KV_HEADS * HEAD_DIM, C_KV_HEADS * HEAD_DIM,
              D_HEADS * HEAD_DIM, D_HEADS * HEAD_DIM, D_HEADS * HEAD_DIM)
IN_WIDTH_2 = sum(EVEN_SPLITS)
MIX_WIDTH = A_HEADS * HEAD_DIM + B_HEADS * B_V_DIM
D_FF_2 = 4 * D_MODEL
N_EVEN = (DEPTH + 1) // 2
N_ODD = DEPTH // 2
EPS = 1e-6
NEG = -1e30


def split_cols_2(p, sizes):
    return jnp.split(p, np.cumsum(sizes)[:-1].tolist(), axis=-1)

def rms_norm(x, g):
    xf = x.astype(jnp.float32)
    y = xf * lax.rsqrt(jnp.mean(jnp.square(xf), axis=-1, keepdims=True) + EPS)
    return (y * g.astype(jnp.float32)).astype(x.dtype)

def modulate(h, shift, scale):
    return h * (1 + scale) + shift

def lambda_init(layer):
    return 0.8 - 0.6 * math.exp(-0.3 * layer)

def axial_rope_tables(T, dtype):
    t = jnp.arange(T, dtype=jnp.int32)
    pos = jnp.stack([t // GRID_W, t % GRID_W], axis=-1).astype(jnp.float32)
    inv = ROPE_THETA_2 ** (-jnp.arange(ROPE_FREQS, dtype=jnp.float32) / ROPE_FREQS)
    ang = pos[..., None] * inv
    return jnp.cos(ang).astype(dtype), jnp.sin(ang).astype(dtype)

def apply_axial_rope(x, cos, sin):
    xs = x.reshape(x.shape[:-1] + (2, 2, ROPE_FREQS))
    x1, x2 = xs[..., 0, :], xs[..., 1, :]
    c, s = cos[:, None], sin[:, None]
    return jnp.stack([x1 * c - x2 * s, x2 * c + x1 * s], axis=-2).reshape(x.shape)

def map_query_blocks(fn, *qs):
    B, T = qs[0].shape[:2]
    nb = T // Q_BLOCK
    blocks = tuple(jnp.moveaxis(a.reshape((B, nb, Q_BLOCK) + a.shape[2:]), 1, 0) for a in qs)
    out = lax.map(lambda args: fn(*args), blocks)
    return jnp.moveaxis(out, 0, 1).reshape((B, T) + out.shape[3:])

def gqa_attend(q, k, v):
    s = jnp.einsum('bqkgd,bskd->bkgqs', q, k).astype(jnp.float32)
    p = jax.nn.softmax(s, axis=-1).astype(v.dtype)
    return jnp.einsum('bkgqs,bskd->bqkgd', p, v)

def diff_attend(q, k, v, lam):
    s = jnp.einsum('bqhjd,bshjd->bhjqs', q, k).astype(jnp.float32)
    p = jax.nn.softmax(s, axis=-1)
    a = (p[:, :, 0] - lam * p[:, :, 1]).astype(v.dtype)
    return jnp.einsum('bhqs,bshe->bqhe', a, v)

def sink_attend(q, k, v, sink):
    s = jnp.einsum('bqkgd,bskd->bkgqs', q, k).astype(jnp.float32)
    sk = jnp.broadcast_to(sink.astype(jnp.float32)[None, :, :, None, None], s.shape[:-1] + (1,))
    p = jax.nn.softmax(jnp.concatenate([sk, s], axis=-1), axis=-1)[..., 1:].astype(v.dtype)
    return jnp.einsum('bkgqs,bskd->bqkgd', p, v)

def windowed_attend(q, k, v, k_ctx, v_ctx, sink):
    B, T = q.shape[:2]
    L = k_ctx.shape[1]
    nb = T // C_WINDOW

    def band(a):
        ap = jnp.pad(a, ((0, 0), (C_WINDOW, C_WINDOW), (0, 0), (0, 0)))
        ap = ap.reshape((B, nb + 2, C_WINDOW) + a.shape[2:])
        return jnp.concatenate([ap[:, :-2], ap[:, 1:-1], ap[:, 2:]], axis=2)

    kb, vb = band(k), band(v)
    qb = q.reshape((B, nb, C_WINDOW) + q.shape[2:])
    i = jnp.arange(C_WINDOW)[:, None]
    j = jnp.arange(3 * C_WINDOW)[None, :]
    kpos = jnp.arange(nb)[:, None, None] * C_WINDOW - C_WINDOW + j
    valid = (jnp.abs(j - C_WINDOW - i) <= C_WINDOW)[None] & (kpos >= 0) & (kpos < T)
    s_loc = jnp.einsum('bnqkgd,bnskd->bnkgqs', qb, kb).astype(jnp.float32)
    s_loc = jnp.where(valid[None, :, None, None], s_loc, NEG)
    s_ctx = jnp.einsum('bnqkgd,bskd->bnkgqs', qb, k_ctx).astype(jnp.float32)
    sk = jnp.broadcast_to(sink.astype(jnp.float32)[None, None, :, :, None, None], s_ctx.shape[:-1] + (1,))
    p = jax.nn.softmax(jnp.concatenate([sk, s_ctx, s_loc], axis=-1), axis=-1)
    p_ctx = p[..., 1:1 + L].astype(v.dtype)
    p_loc = p[..., 1 + L:].astype(v.dtype)
    o = (jnp.einsum('bnkgqs,bskd->bnqkgd', p_ctx, v_ctx)
         + jnp.einsum('bnkgqs,bnskd->bnqkgd', p_loc, vb))
    return o.reshape(q.shape)

def neighborhood_attend(q, k, v, k_ctx, v_ctx, rpb):
    B, T, H, Dh = q.shape
    rows = T // GRID_W
    kh = min(NA_ROWS, rows)
    kw = NA_COLS
    L = k_ctx.shape[1]
    r = jnp.arange(rows)
    rs = jnp.clip(r - kh // 2, 0, rows - kh)
    row_idx = rs[:, None] + jnp.arange(kh)[None, :]

    def gather_rows(a):
        return a.reshape(B, rows, GRID_W, H, Dh)[:, row_idx].reshape(B, rows, kh * GRID_W, H, Dh)

    kg, vg = gather_rows(k), gather_rows(v)
    qg = q.reshape(B, rows, GRID_W, H, Dh)
    cq = jnp.arange(GRID_W)
    cs = jnp.clip(cq - kw // 2, 0, GRID_W - kw)
    ck = jnp.tile(jnp.arange(GRID_W), kh)
    col_valid = (ck[None] >= cs[:, None]) & (ck[None] < cs[:, None] + kw)
    dr = jnp.repeat(row_idx - r[:, None], GRID_W, axis=1)
    dc = jnp.clip(ck[None] - cq[:, None], -(kw - 1), kw - 1)
    bias = rpb[:, dr[:, None, :] + NA_ROWS - 1, dc[None] + NA_COLS - 1]
    bias = jnp.moveaxis(bias, 0, 1).astype(jnp.float32)
    s_loc = jnp.einsum('brqhd,brshd->brhqs', qg, kg).astype(jnp.float32) + bias
    s_loc = jnp.where(col_valid, s_loc, NEG)
    s_ctx = jnp.einsum('brqhd,bshd->brhqs', qg, k_ctx).astype(jnp.float32)
    p = jax.nn.softmax(jnp.concatenate([s_ctx, s_loc], axis=-1), axis=-1)
    p_ctx = p[..., :L].astype(v.dtype)
    p_loc = p[..., L:].astype(v.dtype)
    o = (jnp.einsum('brhqs,bshd->brqhd', p_ctx, v_ctx)
         + jnp.einsum('brhqs,brshd->brqhd', p_loc, vg))
    return o.reshape(B, T, H * Dh)

def even_mixer(h_x, h_c, w_in, w_out, qk_g, lam_p, subln_g, lam0, cos, sin, with_ctx):
    scale = HEAD_DIM ** -0.5
    g_a = A_HEADS // A_KV_HEADS

    def project(h, rope):
        n, s = h.shape[:2]
        qa, ka, va, qb, kb, vb = split_cols_2(h @ w_in, EVEN_SPLITS)
        qa = rms_norm(qa.reshape(n, s, A_HEADS, HEAD_DIM), qk_g[0])
        ka = rms_norm(ka.reshape(n, s, A_KV_HEADS, HEAD_DIM), qk_g[1])
        qb = qb.reshape(n, s, 2 * B_HEADS, HEAD_DIM)
        kb = kb.reshape(n, s, 2 * B_HEADS, HEAD_DIM)
        if rope:
            qa, ka = apply_axial_rope(qa, cos, sin), apply_axial_rope(ka, cos, sin)
            qb, kb = apply_axial_rope(qb, cos, sin), apply_axial_rope(kb, cos, sin)
        return ((qa * scale).reshape(n, s, A_KV_HEADS, g_a, HEAD_DIM), ka,
                va.reshape(n, s, A_KV_HEADS, HEAD_DIM),
                (qb * scale).reshape(n, s, B_HEADS, 2, HEAD_DIM),
                kb.reshape(n, s, B_HEADS, 2, HEAD_DIM),
                vb.reshape(n, s, B_HEADS, B_V_DIM))

    lam = (jnp.exp(jnp.sum(lam_p[0] * lam_p[1]).astype(jnp.float32))
           - jnp.exp(jnp.sum(lam_p[2] * lam_p[3]).astype(jnp.float32)) + lam0)
    qa_x, ka_x, va_x, qb_x, kb_x, vb_x = project(h_x, True)
    qa_c, ka_c, va_c, qb_c, kb_c, vb_c = project(h_c, False)
    ka_all = jnp.concatenate([ka_c, ka_x], axis=1)
    va_all = jnp.concatenate([va_c, va_x], axis=1)
    kb_all = jnp.concatenate([kb_c, kb_x], axis=1)
    vb_all = jnp.concatenate([vb_c, vb_x], axis=1)
    B, T = h_x.shape[:2]
    o_a = map_query_blocks(lambda q: gqa_attend(q, ka_all, va_all), qa_x).reshape(B, T, -1)
    o_b = map_query_blocks(lambda q: diff_attend(q, kb_all, vb_all, lam), qb_x)
    o_b = (rms_norm(o_b, subln_g) * (1 - lam0)).reshape(B, T, -1)
    out_x = jnp.concatenate([o_a, o_b], axis=-1) @ w_out
    out_c = None
    if with_ctx:
        n, L = h_c.shape[:2]
        oa_c = gqa_attend(qa_c, ka_c, va_c).reshape(n, L, -1)
        ob_c = (rms_norm(diff_attend(qb_c, kb_c, vb_c, lam), subln_g) * (1 - lam0)).reshape(n, L, -1)
        out_c = jnp.concatenate([oa_c, ob_c], axis=-1) @ w_out
    return out_x, out_c

def odd_mixer(h_x, h_c, w_in, w_out, sink, rpb, cos, sin, with_ctx):
    scale = HEAD_DIM ** -0.5
    g_c = C_HEADS // C_KV_HEADS
    sink = sink.reshape(C_KV_HEADS, g_c)

    def project(h, rope):
        n, s = h.shape[:2]
        qc, kc, vc, qd, kd, vd = split_cols_2(h @ w_in, ODD_SPLITS)
        qc = qc.reshape(n, s, C_HEADS, HEAD_DIM)
        kc = kc.reshape(n, s, C_KV_HEADS, HEAD_DIM)
        if rope:
            qc, kc = apply_axial_rope(qc, cos, sin), apply_axial_rope(kc, cos, sin)
        return ((qc * scale).reshape(n, s, C_KV_HEADS, g_c, HEAD_DIM), kc,
                vc.reshape(n, s, C_KV_HEADS, HEAD_DIM),
                qd.reshape(n, s, D_HEADS, HEAD_DIM) * scale,
                kd.reshape(n, s, D_HEADS, HEAD_DIM),
                vd.reshape(n, s, D_HEADS, HEAD_DIM))

    qc_x, kc_x, vc_x, qd_x, kd_x, vd_x = project(h_x, True)
    qc_c, kc_c, vc_c, qd_c, kd_c, vd_c = project(h_c, False)
    B, T = h_x.shape[:2]
    o_c = windowed_attend(qc_x, kc_x, vc_x, kc_c, vc_c, sink).reshape(B, T, -1)
    o_d = neighborhood_attend(qd_x, kd_x, vd_x, kd_c, vd_c, rpb)
    out_x = jnp.concatenate([o_c, o_d], axis=-1) @ w_out
    out_c = None
    if with_ctx:
        n, L = h_c.shape[:2]
        oc_c = sink_attend(qc_c, kc_c, vc_c, sink).reshape(n, L, -1)
        od_c = gqa_attend(qd_c[:, :, :, None], kd_c, vd_c).reshape(n, L, -1)
        out_c = jnp.concatenate([oc_c, od_c], axis=-1) @ w_out
    return out_x, out_c

def squared_relu_mlp(h, w1, w2):
    return jnp.square(jax.nn.relu(h @ w1)) @ w2

def second_inputs(seed: int = 0) -> dict:
    key = jax.random.key(seed)
    ks = jax.random.split(key, 16)
    f32 = jnp.float32

    def nrm(k, shape, s):
        return jax.random.normal(k, shape, f32) * s

    return {
        "x": nrm(ks[0], (BATCH, SEQ, D_MODEL), 1.0),
        "c": nrm(ks[1], (BATCH, D_MODEL), 1.0),
        "ctx": nrm(ks[2], (BATCH, CTX_LEN, D_MODEL), 1.0),
        "c_ctx": nrm(ks[3], (D_MODEL,), 1.0),
        "w_mod": nrm(ks[4], (DEPTH, D_MODEL, 6 * D_MODEL), D_MODEL ** -0.5),
        "b_mod": nrm(ks[5], (DEPTH, 6 * D_MODEL), 0.02),
        "norm_g": 1.0 + nrm(ks[6], (DEPTH, 4, D_MODEL), 0.02),
        "w_in": nrm(ks[7], (DEPTH, D_MODEL, IN_WIDTH_2), D_MODEL ** -0.5),
        "w_out": nrm(ks[8], (DEPTH, MIX_WIDTH, D_MODEL), MIX_WIDTH ** -0.5),
        "w_mlp_in": nrm(ks[9], (DEPTH, D_MODEL, D_FF_2), D_MODEL ** -0.5),
        "w_mlp_out": nrm(ks[10], (DEPTH, D_FF_2, D_MODEL), D_FF_2 ** -0.5),
        "qk_norm_a": 1.0 + nrm(ks[11], (N_EVEN, 2, HEAD_DIM), 0.02),
        "diff_lambda": nrm(ks[12], (N_EVEN, 4, HEAD_DIM), 0.1),
        "diff_subln": 1.0 + nrm(ks[13], (N_EVEN, B_V_DIM), 0.02),
        "sink_c": nrm(ks[14], (N_ODD, C_HEADS), 0.5),
        "rpb_d": nrm(ks[15], (N_ODD, D_HEADS, 2 * NA_ROWS - 1, 2 * NA_COLS - 1), 0.1),
    }

def second_block(x, c, ctx, c_ctx, w_mod, b_mod, norm_g, w_in, w_out, w_mlp_in, w_mlp_out,
              qk_norm_a, diff_lambda, diff_subln, sink_c, rpb_d):
    T = x.shape[1]
    cos, sin = axial_rope_tables(T, x.dtype)
    s_x = jax.nn.silu(c)
    s_c = jax.nn.silu(c_ctx)
    for l in range(DEPTH):
        last = l == DEPTH - 1
        mod_x = (s_x @ w_mod[l] + b_mod[l])[:, None, :]
        mod_c = s_c @ w_mod[l] + b_mod[l]
        sh1_x, sc1_x, g1_x, sh2_x, sc2_x, g2_x = jnp.split(mod_x, 6, axis=-1)
        sh1_c, sc1_c, g1_c, sh2_c, sc2_c, g2_c = jnp.split(mod_c, 6, axis=-1)
        h_x = modulate(rms_norm(x, norm_g[l, 0]), sh1_x, sc1_x)
        h_c = modulate(rms_norm(ctx, norm_g[l, 0]), sh1_c, sc1_c)
        if l % 2 == 0:
            i = l // 2
            m_x, m_c = even_mixer(h_x, h_c, w_in[l], w_out[l], qk_norm_a[i], diff_lambda[i],
                                  diff_subln[i], lambda_init(l), cos, sin, not last)
        else:
            i = l // 2
            m_x, m_c = odd_mixer(h_x, h_c, w_in[l], w_out[l], sink_c[i], rpb_d[i],
                                 cos, sin, not last)
        x = x + g1_x * rms_norm(m_x, norm_g[l, 1])
        f_x = squared_relu_mlp(modulate(rms_norm(x, norm_g[l, 2]), sh2_x, sc2_x), w_mlp_in[l], w_mlp_out[l])
        x = x + g2_x * rms_norm(f_x, norm_g[l, 3])
        if not last:
            ctx = ctx + g1_c * rms_norm(m_c, norm_g[l, 1])
            f_c = squared_relu_mlp(modulate(rms_norm(ctx, norm_g[l, 2]), sh2_c, sc2_c), w_mlp_in[l], w_mlp_out[l])
            ctx = ctx + g2_c * rms_norm(f_c, norm_g[l, 3])
    return x


def setup_inputs(seed=0):
    out = dict(first_inputs(seed))
    for name, value in second_inputs(seed + 1).items():
        if name != "x":
            out[name + "_2"] = value
    return out


def reference(
    x, mem, positions, norm_mix_pre, norm_mix_post, w_in, pool_w, pool_scale, conv_b_w,
    w_branch_a, w_branch_b, w_branch_c, w_out, norm_mem_pre, norm_mem_post, norm_memkv, w_mq,
    w_mkv, w_mo, norm_ffn_pre, norm_ffn_post, w_up, conv_ffn_w, w_down, c_2, ctx_2, c_ctx_2,
    w_mod_2, b_mod_2, norm_g_2, w_in_2, w_out_2, w_mlp_in_2, w_mlp_out_2, qk_norm_a_2,
    diff_lambda_2, diff_subln_2, sink_c_2, rpb_d_2,
):
    x = first_block(
        x, mem, positions, norm_mix_pre, norm_mix_post, w_in, pool_w, pool_scale, conv_b_w,
        w_branch_a, w_branch_b, w_branch_c, w_out, norm_mem_pre, norm_mem_post, norm_memkv,
        w_mq, w_mkv, w_mo, norm_ffn_pre, norm_ffn_post, w_up, conv_ffn_w, w_down,
    )
    return second_block(
        x, c_2, ctx_2, c_ctx_2, w_mod_2, b_mod_2, norm_g_2, w_in_2, w_out_2, w_mlp_in_2,
        w_mlp_out_2, qk_norm_a_2, diff_lambda_2, diff_subln_2, sink_c_2, rpb_d_2,
    )


_drawn_inputs = setup_inputs


def setup_inputs(seed=0):
    import zlib

    import numpy as np

    out = dict(_drawn_inputs(seed))
    spreads = {}
    factors = {'b_mod_2': 2.853,
     'norm_g_2': 4.641,
     'qk_norm_a_2': 8.0,
     'diff_lambda_2': 5.485,
     'diff_subln_2': 8.0,
     'sink_c_2': 8.0,
     'rpb_d_2': 8.0}
    for name, (base, spread) in spreads.items():
        noise = np.random.default_rng([zlib.crc32(name.encode()), seed]).standard_normal(out[name].shape)
        drawn = base * np.exp(spread * noise) if base else spread * noise
        out[name] = __import__('jax').numpy.asarray(drawn.astype(out[name].dtype))
    for name, factor in factors.items():
        out[name] = (out[name] * factor).astype(out[name].dtype)
    return out
```

```python
from contextlib import ExitStack, contextmanager

import concourse.bass as bass
from concourse import mybir

ALU = mybir.AluOpType
ACT = mybir.ActivationFunctionType
AX = mybir.AxisListType
F32 = mybir.dt.float32
F32R = mybir.dt.float32r
I32 = mybir.dt.int32

P = 128
DEPTH = 2
D = 1024
KB = D // P
T = 512
TC = 256
TA = T + TC
HD = 64
EPS = 1e-6

POOL = 3
HEADS = 4
QKV = 6
MIX_IN = 4 * POOL + 3 * QKV
FF = 2816 // P
DOWN_UNITS = -(-FF // KB)
C_BX, C_BB, C_BC, C_Q, C_K, C_V = POOL, 2 * POOL, 3 * POOL, 4 * POOL, 4 * POOL + QKV, 4 * POOL + 2 * QKV
G_MIX, G_MIXP, G_MEM, G_MEMP, G_KV, G_FFN, G_FFNP = (KB * i for i in range(7))
C_SCALE = 7 * KB
C_CONVB = C_SCALE + POOL
C_CONVF = C_CONVB + 3 * POOL
NPAR = C_CONVF + 3 * FF
UNITS_1 = MIX_IN + 4 * KB + KB + KB + 4 + 4 + 2 * FF + DOWN_UNITS * KB

IN2 = 18
QUARTERS = 4
UNITS_2 = IN2 + KB + QUARTERS * 2 * KB
MODS = 6 * KB
MOD_UNITS = DEPTH * MODS
LAMBDA0 = 0.8 - 0.6
NEG = -1e30
TWO_PI = 6.283185307179586
TURN_PARTS = (6.28125, 0.0019350051879882812, 3.0199159819e-07)
MAGIC = 1.5 * 2 ** 23
PI_IN = 3.1415925
DR = 14
BW = DR * HD

RAW_SLOTS = 4
SLOTS = 2


class Marks:

    def __init__(self, *names):
        self.n = {name: 0 for name in names}
        self.var = {name: 0 for name in names}

    def at(self, name, more=0):
        return self.n[name] + more + self.var[name]

    def add(self, name, k=1):
        self.n[name] += k

    @contextmanager
    def loop(self, eng, count, **per):
        n0, v0 = dict(self.n), dict(self.var)
        with eng.Fori(0, count) as i:
            for name, k in per.items():
                self.var[name] = i * k + self.var[name]
            yield i
        for name in self.n:
            moved = self.n[name] - n0[name]
            assert moved == per.get(name, 0), (name, moved, per)
            self.n[name] = n0[name] + count * moved
            self.var[name] = v0[name]


def build(nc, stream, x, mem, params1, positions, consts, poolw, masks, ctx, params2, cvec, small2, rope2, band, rpb, out):
    with ExitStack() as stack:
        def sem(name):
            return stack.enter_context(nc.semaphore(name))

        top = [0]

        def place(name, shape, dt=F32, at=None):
            size = 1
            for s in shape[1:]:
                size *= s
            if at is None:
                at = top[0]
                top[0] += -(-size // 8) * 8
            return nc.alloc_sbuf_tensor_at(name, shape, dt, offset=base0 + 4 * at)

        base0 = -(-nc.sbuf_base // 32) * 32
        RAW = place("RAW", [P, RAW_SLOTS, D])
        WH = place("WH", [P, SLOTS, D], F32R)
        WL = place("WL", [P, SLOTS, D], F32R)
        IDENT = place("IDENT", [P, P])
        ONES = place("ONES", [P, P])
        COL = place("COL", [P, 16])
        PAR = place("PAR", [P, DEPTH, NPAR])
        PL = place("PL", [P, NPAR])
        INV16 = place("INV16", [P, POOL, 16])
        DEN = place("DEN", [P, 2])
        MX = place("MX", [P, 8])
        MR = place("MR", [P, TC])
        X = place("X", [P, KB, T])
        S0 = top[0]
        SCR_N = 4608
        top[0] += SCR_N
        SQ = place("SQ", [P, 2, TA], at=S0)
        ACC = place("ACC", [P, TA], at=S0 + 2 * TA)
        RS = place("RS", [P, TA], at=S0 + 3 * TA)
        TMP = place("TMP", [P, 2, TA], at=S0 + 4 * TA)
        Z = top[0]

        HHI = place("HHI", [P, KB, T], F32R, at=Z)
        HLO = place("HLO", [P, KB, T], F32R, at=Z + KB * T)
        Y = place("Y", [P, KB, T], at=Z)
        ZU = Z + 2 * KB * T
        U = place("U", [P, MIX_IN, T], at=ZU)
        ZB = ZU + MIX_IN * T
        BHI = place("BHI", [P, KB, T], F32R, at=ZB)
        BLO = place("BLO", [P, KB, T], F32R, at=ZB + KB * T)
        ZT = ZB + 2 * KB * T
        MASK0 = place("MASK0", [P, T + 3], at=ZT)
        MASK12 = place("MASK12", [P, 2 * P], at=ZT + T + 8)
        COS = place("COS", [P, T], at=ZT + T + 8 + 2 * P)
        SIN = place("SIN", [P, T], at=ZT + 2 * T + 8 + 2 * P)
        top1 = ZT + 3 * T + 8 + 2 * P
        PU = place("PU", [P, 5, T + 16], at=S0)
        CB = place("CB", [P, 2, T + 2], at=S0 + 5 * (T + 16))
        RT = place("RT", [P, T], at=S0 + 5 * (T + 16) + 2 * (T + 8))
        PTS = place("PTS", [P, 2, TA], at=S0)
        PB = place("PB", [P, 2, TA], at=S0 + 2 * TA)
        OTOK = place("OTOK", [P, 4, 2 * P], at=S0 + 4 * TA)
        GATE = place("GATE", [P, 3, T], at=S0)
        MT = place("MT", [P, 2, T], at=S0 + 3 * T)
        POOLW = place("POOLW", [P, 7, P], at=ZB + 2 * POOL * T)
        MHI = place("MHI", [P, KB, T], F32R, at=ZU)
        MLO = place("MLO", [P, KB, T], F32R, at=ZU + KB * T)
        MEM = place("MEM", [P, KB, TC], at=ZU + 2 * KB * T)
        NHI = place("NHI", [P, KB, TC], F32R, at=ZU + 2 * KB * T + KB * TC)
        NLO = place("NLO", [P, KB, TC], F32R, at=ZU + 2 * KB * T + 2 * KB * TC)
        KV = place("KV", [P, KB, TC], at=ZB)
        VM = place("VM", [P, 2, HEADS * P], at=ZB + KB * TC)
        QM = place("QM", [P, HEADS, T], at=ZB + KB * TC + 2 * HEADS * P)
        OM = place("OM", [P, 4, HEADS * P], at=ZU + 2 * KB * T)
        OMHI = place("OMHI", [P, HEADS, T], F32R, at=ZU)
        OMLO = place("OMLO", [P, HEADS, T], F32R, at=ZU + HEADS * T)
        FHI = place("FHI", [P, FF, T], F32R, at=ZU)
        FLO = place("FLO", [P, FF, T], F32R, at=ZU + FF * T)
        UA = place("UA", [P, 2, T + 8], at=S0 + 6 * TA - 2 * (T + 8) + 0 * T)
        FT = place("FT", [P, 2, T], at=S0)
        FC = place("FC", [P, 2, T], at=S0 + 2 * T)
        assert ZU + 2 * FF * T <= ZT and ZU + 2 * KB * T + 3 * KB * TC <= ZB
        limit = (nc.sbuf_usable_end - base0) // 4
        assert top1 <= limit, (top1, limit)

        at2 = [Z]

        def place2(name, shape, dt=F32):
            size = 1
            for n in shape[1:]:
                size *= n
            here = at2[0]
            at2[0] += -(-size // 8) * 8
            return place(name, shape, dt, at=here)

        CTX = place2("CTX", [P, KB, TC])
        PAR2 = place2("PAR2", [P, 2 * KB * 4 + MOD_UNITS + 8 + P])
        NG = PAR2[:, 0:2 * KB * 4].rearrange("p (l g k) -> p l g k", l=DEPTH, g=4)
        BMOD = PAR2[:, 2 * KB * 4:2 * KB * 4 + MOD_UNITS]
        QKG = PAR2[:, 2 * KB * 4 + MOD_UNITS:2 * KB * 4 + MOD_UNITS + 8]
        HEAD_ONES = PAR2[:, 2 * KB * 4 + MOD_UNITS + 8:2 * KB * 4 + MOD_UNITS + 8 + P]
        SK = place2("SK", [P, 4])
        MOD = place2("MOD", [P, MOD_UNITS, 2])
        CV = place2("CV", [P, KB, 2])
        SM = place2("SM", [P, 4 * HD + 8])
        LM = place2("LM", [P, 8])
        SINK8 = place2("SINK8", [P, 8])
        ES = place2("ES", [P, 8])
        SS = place2("SS", [P, 8])
        H2HI = place2("H2HI", [P, KB, TA], F32R)
        H2LO = place2("H2LO", [P, KB, TA], F32R)
        at_u2 = at2[0]
        U2 = place2("U2", [P, IN2, TA])
        C2 = place2("C2", [P, T])
        S2 = place2("S2", [P, T])
        OT2 = place2("OT2", [P, TA // P, P])
        RT2 = place2("RT2", [P, T])
        BIAS = place2("BIAS", [P, 2, BW])
        BAND = place2("BAND", [P, BW])
        ZERO = place2("ZERO", [P, TC])
        CMASK = place2("CMASK", [P, HD])
        assert at2[0] <= limit, (at2[0], limit)
        GHI = place("GHI", [P, KB, TA], F32R, at=at_u2)
        GLO = place("GLO", [P, KB, TA], F32R, at=at_u2 + KB * TA)
        Y2 = place("Y2", [P, KB, TA], at=at_u2 + 2 * KB * TA)
        assert at_u2 + 3 * KB * TA <= limit
        QST = place("QST", [P, TA], at=S0 + 4 * TA)
        KST = place("KST", [P, TA], at=S0 + 5 * TA)
        bias_rows = nc.dram_tensor("bias_rows", (2 * HEADS * (DR + 1), HD, 2 * HD - 1), F32).ap()

        def skewed(half):
            row = HD * (2 * HD - 1)
            return bass.AP(tensor=bias_rows.tensor, offset=(1 - half) * row + HD - 1,
                           ap=[[(DR + 1) * row, 2 * HEADS], [2 * HD - 2, HD], [row, DR], [1, HD]])


        PS = stack.enter_context(nc.psum_tensor("PS", [P, 8, T], F32))
        FLAT = PS[:].rearrange("p b n -> p (b n)")

        def bank(b, n=T):
            return PS[:, b, 0:n]

        landed = [sem(f"landed{s}") for s in range(RAW_SLOTS)]
        raw_used = [sem(f"raw_used{s}") for s in range(RAW_SLOTS)]
        split_ready, units_done = sem("split_ready"), sem("units_done")
        taken = [sem("taken0"), sem("taken1")]
        consts_in, mem_in, pool_in, stored = sem("consts_in"), sem("mem_in"), sem("pool_in"), sem("stored")
        passed = sem("passed")
        tables_ready, sin_ready, ang_ready = sem("tables_ready"), sem("sin_ready"), sem("ang_ready")
        x_ready, sq_ready, sq_taken = sem("x_ready"), sem("sq_ready"), sem("sq_taken")
        stat_done, root_ready = sem("stat_done"), sem("root_ready")
        val_ready, hi_ready, lo_ready = sem("val_ready"), sem("hi_ready"), sem("lo_ready")
        pooled, pool_mixed = sem("pooled"), sem("pool_mixed")
        vt_done, vt_ready, roped = sem("vt_done"), sem("vt_ready"), sem("roped")
        s_done, max_ready, exp_done = sem("s_done"), sem("max_ready"), sem("exp_done")
        pt_done, pts_ready, o_done, o_taken, ot_done = sem("pt_done"), sem("pts_ready"), sem("o_done"), sem("o_taken"), sem("ot_done")
        mem_ready, layer_ready = sem("mem_ready"), sem("layer_ready")
        merge_done = sem("merge_done")
        conv_ready, silu_ready = sem("conv_ready"), sem("silu_ready")
        rows_in, in2, bias_in, sv_ready = sem("rows_in"), sem("in2"), sem("bias_in"), sem("sv_ready")
        mod_done, mod_taken, lam_ready, y_ready = sem("mod_done"), sem("mod_taken"), sem("lam_ready"), sem("y_ready")
        relu_ready, ss_ready, root_row, hsq_ready = sem("relu_ready"), sem("ss_ready"), sem("root_row"), sem("hsq_ready")
        bias_used, sub_ready, root_sub = sem("bias_used"), sem("sub_ready"), sem("root_sub")
        MARKS = ("raw", "modd", "modt", "relu", "ss", "rr", "y", "hsq", "bias", "in2", "units", "use0", "use1", "consts", "mem", "pool", "x", "sq", "sqt", "stat", "root", "val", "hi", "lo", "pooled", "mixed",
                 "vt", "vtr", "roped", "s", "max", "exp", "pt", "pts", "o", "ot", "otk", "gate", "merge", "conv", "silu", "layer", "otd")
        steps = 4 + 16 + 2
        uses = MIX_IN // 2 + 2 * KB + KB // 2 + KB // 2 + HEADS // 2 + HEADS // 2 + FF + KB // 2
        LAYER = {
            "pe": dict(units=UNITS_1, use0=uses, use1=uses, lo=3 * KB + 2 * POOL + 2 + KB + HEADS + FF, sqt=6 * (KB - 1), pool=16,
                       pooled=POOL, vtr=QKV + 2, roped=2 * QKV, exp=32, pts=32, otk=32, mem=KB),
            "act": dict(units=UNITS_1, use0=uses, use1=uses, sqt=6 * (KB - 1), stat=6, x=3 * KB, val=3 * KB + POOL + KB, mixed=POOL,
                        vt=QKV + 2, max=32, pt=32, otd=2 + HEADS, merge=KB, conv=FF, layer=1),
            "dve": dict(units=UNITS_1, use0=uses, use1=uses, sq=3 * KB + KB // 2, root=6, hi=3 * KB + 2 * POOL + 2 + 2 * KB + HEADS + FF,
                        o=32, s=32, mem=16, silu=FF, layer=1),
        }

        block = stack.enter_context(nc.Block())
        n_units = DEPTH * UNITS_1 + MOD_UNITS + DEPTH * UNITS_2
        first_mod = DEPTH * UNITS_1 // RAW_SLOTS
        after_mod = first_mod + MOD_UNITS // RAW_SLOTS

        @block.sync
        def _(sp):
            sp.dma_start(X[:], x).then_inc(consts_in, 16)
            sp.dma_start(PAR[:], params1).then_inc(consts_in, 16)
            sp.dma_start(IDENT[:], consts[:, 0:P]).then_inc(consts_in, 16)
            sp.dma_start(ONES[:], consts[:, P:2 * P]).then_inc(consts_in, 16)
            sp.dma_start(COL[:], consts[:, 2 * P:2 * P + 16]).then_inc(consts_in, 16)
            sp.dma_start(INV16[:].rearrange("p a b -> p (a b)"), consts[:, 2 * P + 16:2 * P + 64]).then_inc(consts_in, 16)
            sp.dma_start(MASK0[:], masks[:, 0:T + 3]).then_inc(consts_in, 16)
            sp.dma_start(MASK12[:], masks[:, T + 3:T + 3 + 2 * P]).then_inc(consts_in, 16)
            sp.dma_start(SIN[:].bitcast(I32), positions.partition_broadcast(P)).then_inc(consts_in, 16)
            sp.dma_start(bias_rows, rpb.rearrange("h d w -> (h d) w").unsqueeze(1).to_broadcast([2 * HEADS * (DR + 1), HD, 2 * HD - 1])).then_inc(rows_in, 16)
            for s in range(RAW_SLOTS):
                sp.dma_start(RAW[:, s, :], stream[s, :, :]).then_inc(landed[s], 16)
            with sp.Fori(1, n_units // RAW_SLOTS) as i:
                for s in range(RAW_SLOTS):
                    sp.wait_ge(raw_used[s], i)
                    sp.dma_start(RAW[:, s:s + 1, :], stream[bass.ds(i * RAW_SLOTS + s, 1), :, :].rearrange("u p n -> p u n")).then_inc(landed[s], 16)
            sp.wait_ge(x_ready, DEPTH * 3 * KB + DEPTH * 2 * KB)
            sp.dma_start(out.rearrange("(k p) t -> p k t", p=P), X[:]).then_inc(stored, 16)
            sp.wait_ge(stored, 16)

        @block.gpsimd
        def _(pool):
            def split(i, s, skipped=0):
                d = s % SLOTS
                pool.wait_ge(landed[s], 16 * i + 16)
                if s >= SLOTS or not isinstance(i, int):
                    pool.wait_ge(units_done, i * RAW_SLOTS + (s - SLOTS + 1 - skipped))
                nc.gpsimd.sem_inc(passed, 1)
                nc.gpsimd.tensor_tensor(WH[:, d, :].rearrange("p (b n) -> p b n", n=P), RAW[:, s, :].rearrange("p (b n) -> p b n", n=P),
                                        ONES[:].unsqueeze(1).to_broadcast([P, KB, P]), ALU.mult)
                pool.drain()
                nc.gpsimd.tensor_tensor(WL[:, d, :], RAW[:, s, :], WH[:, d, :].bitcast(F32), ALU.subtract).then_inc(split_ready, 1)
                pool.drain()
                nc.gpsimd.sem_inc(raw_used[s], 1)

            pool.wait_ge(consts_in, 16 * 9)
            for s in range(RAW_SLOTS):
                split(0, s)
            with pool.Fori(1, first_mod) as i:
                for s in range(RAW_SLOTS):
                    split(i, s)
            with pool.Fori(after_mod, n_units // RAW_SLOTS) as i:
                for s in range(RAW_SLOTS):
                    split(i, s, MOD_UNITS)

        @block.tensor
        def _(pe):
            m = Marks(*MARKS)

            def products(out, slot, b, hi, lo, start, stop):
                nc.tensor.matmul(out, WH[:, slot, b * P:(b + 1) * P], hi, start=start, stop=False)
                nc.tensor.matmul(out, WH[:, slot, b * P:(b + 1) * P], lo, start=False, stop=False)
                return nc.tensor.matmul(out, WL[:, slot, b * P:(b + 1) * P], hi, start=False, stop=stop)

            def unit_in():
                pe.wait_ge(split_ready, m.at("units", 1))
                return m.n["units"] % SLOTS

            def unit_out(last):
                last.then_inc(units_done, 1)
                m.add("units")

            def set_in(p):
                pe.wait_ge(taken[p], m.at(f"use{p}", 1))
                m.add(f"use{p}")

            def sets_idle():
                for p in range(2):
                    pe.wait_ge(taken[p], m.at(f"use{p}", 1))

            def chunk(hi, lo, n=T, ready=False):
                slot = unit_in()
                set_in(slot)
                for k in range(KB):
                    if ready:
                        m.add("lo")
                        pe.wait_ge(lo_ready, m.at("lo"))
                    last = products(bank(3 * slot, n), slot, k, hi[:, k, 0:n], lo[:, k, 0:n], k == 0, k == KB - 1)
                unit_out(last)

            def statistics(n):
                m.add("sqt", KB - 1)
                pe.wait_ge(sq_taken, m.at("sqt"))
                for c0 in range(0, n, T):
                    c1 = min(c0 + T, n)
                    last = nc.tensor.matmul(FLAT[:, 6 * T + c0:6 * T + c1], ONES[:], ACC[:, c0:c1], start=True, stop=True)
                last.then_inc(stat_done, 1)

            def attention(count, kblocks, scores, values):
                scores(0)
                scores(1)
                for n in range(count):
                    m.add("exp")
                    pe.wait_ge(exp_done, m.at("exp"))
                    for b in range(kblocks):
                        last = nc.tensor.transpose(FLAT[:, 4 * T + b * P:4 * T + (b + 1) * P], PB[:, n % 2, b * P:(b + 1) * P], IDENT[:])
                    last.then_inc(pt_done, 1)
                    if n + 2 < count:
                        scores(n + 2)
                    m.add("pts")
                    pe.wait_ge(pts_ready, m.at("pts"))
                    m.add("otk")
                    if n >= 2:
                        pe.wait_ge(o_taken, m.at("otk", -2))
                    values(n)

            pe.wait_ge(consts_in, 16 * 9)
            statistics(TC)
            statistics(T)
            with m.loop(pe, DEPTH, **LAYER["pe"]):
                chunk(HHI, HLO, ready=True)
                chunk(HHI, HLO)
                with m.loop(pe, (MIX_IN - 2) // 2, units=2, use0=1, use1=1):
                    chunk(HHI, HLO)
                    chunk(HHI, HLO)
                sets_idle()
                m.add("pool", 16)
                pe.wait_ge(pool_in, m.at("pool"))
                m.add("pooled", POOL)
                pe.wait_ge(pooled, m.at("pooled"))
                b = 0
                for c, ks in enumerate(((0, 1), (0, 1, 2), (1, 2))):
                    for k in ks:
                        last = nc.tensor.matmul(bank(c), POOLW[:, b, :], U[:, k, :], start=k == ks[0], stop=k == ks[-1])
                        b += 1
                    last.then_inc(pool_mixed, 1)
                for c in range(QKV):
                    if c == 5:
                        pe.wait_ge(vt_ready, m.at("vtr", 1))
                    for b in range(4):
                        v = U[:, C_V + c, :]
                        src = v[:, b * P:(b + 1) * P] if c < 2 else v.rearrange("p (i r) -> p r i", r=4)[:, b, :]
                        last = nc.tensor.transpose(PS[:, (3, 4, 5, 6, 7, 3)[c], b * P:(b + 1) * P], src, IDENT[:])
                    last.then_inc(vt_done, 1)
                m.add("vtr", QKV)
                pe.wait_ge(vt_ready, m.at("vtr"))
                m.add("roped", 2 * QKV)
                pe.wait_ge(roped, m.at("roped"))
                m.add("lo", 2 * POOL)
                pe.wait_ge(lo_ready, m.at("lo"))

                def head(n):
                    jj, r, half = n // 8, n // 2 % 4, n % 2
                    return jj, r, slice(half * HD, half * HD + HD)

                def scores(n):
                    jj, r, rows = head(n)
                    for g in range(3):
                        q = U[rows, C_Q + 2 * g + jj, :].rearrange("p (i r) -> p r i", r=4)[:, r, :]
                        k = U[rows, C_K + 2 * g + jj, :]
                        c0 = 2 * (n % 2) * T
                        if g == 0:
                            o = FLAT[:, c0:c0 + T]
                        else:
                            k = k.rearrange("p (i r) -> p r i", r=4)[:, r, :]
                            o = FLAT[:, c0 + T + (g - 1) * P:c0 + T + g * P]
                        last = nc.tensor.matmul(o, q, k, start=True, stop=True)
                    last.then_inc(s_done, 1)

                def values(n):
                    jj, r, rows = head(n)
                    for b in range(6):
                        g = max(b - 3, 0)
                        vb = b if b < 4 else r
                        v = U[:, C_V + 2 * g + jj, vb * P + rows.start:vb * P + rows.stop]
                        last = nc.tensor.matmul(PS[:, 6 + n % 2, 0:HD], PTS[:, n % 2, b * P:(b + 1) * P], v, start=b == 0, stop=b == 5)
                    last.then_inc(o_done, 1)

                attention(16, 6, scores, values)
                pe.wait_ge(o_taken, m.at("otk"))
                for jj in range(2):
                    for r in range(4):
                        last = nc.tensor.transpose(PS[:, jj, r * P:(r + 1) * P], OTOK[:, r, jj * P:(jj + 1) * P], IDENT[:])
                    last.then_inc(ot_done, 1)
                m.add("lo", 2)
                pe.wait_ge(lo_ready, m.at("lo"))
                pe.sem_inc(passed, 1)
                with m.loop(pe, KB, units=4, use0=2, use1=2):
                    for g in range(3):
                        chunk(HHI, HLO)
                    slot = unit_in()
                    set_in(1)
                    for b, (bk, first, end) in enumerate(((3, 1, 0), (3, 0, 0), (3, 0, 1), (4, 1, 0), (4, 0, 0), (4, 0, 1), (5, 1, 0), (5, 0, 1))):
                        last = products(bank(bk), slot, b, BHI[:, b, :], BLO[:, b, :], bool(first), bool(end))
                    unit_out(last)
                chunk(MHI, MLO, ready=True)
                for _ in range(KB - 1):
                    chunk(MHI, MLO)
                statistics(T)
                m.add("mem", KB)
                pe.wait_ge(mem_ready, m.at("mem"))
                for _ in range(KB):
                    chunk(NHI, NLO, TC)
                statistics(T)
                chunk(HHI, HLO, ready=True)
                for _ in range(HEADS - 1):
                    chunk(HHI, HLO)
                sets_idle()
                for c in range(2):
                    for hh in range(HEADS):
                        last = nc.tensor.transpose(PS[:, 4 + c, hh * P:(hh + 1) * P], KV[:, HEADS + hh, c * P:(c + 1) * P], IDENT[:])
                    last.then_inc(vt_done, 1)
                m.add("vtr", 2)
                pe.wait_ge(vt_ready, m.at("vtr"))

                def scores_m(n):
                    hh, qb = n // 4, n % 4
                    nc.tensor.matmul(FLAT[:, 2 * (n % 2) * T:2 * (n % 2) * T + TC], QM[:, hh, qb * P:(qb + 1) * P], KV[:, hh, :],
                                     start=True, stop=True).then_inc(s_done, 1)

                def values_m(n):
                    hh = n // 4
                    for b in range(2):
                        last = nc.tensor.matmul(PS[:, 6 + n % 2, 0:P], PTS[:, n % 2, b * P:(b + 1) * P], VM[:, b, hh * P:(hh + 1) * P],
                                                start=b == 0, stop=b == 1)
                    last.then_inc(o_done, 1)

                attention(16, 2, scores_m, values_m)
                pe.wait_ge(o_taken, m.at("otk"))
                for hh in range(HEADS):
                    for qb in range(4):
                        last = nc.tensor.transpose(PS[:, hh, qb * P:(qb + 1) * P], OM[:, qb, hh * P:(hh + 1) * P], IDENT[:])
                    last.then_inc(ot_done, 1)
                m.add("lo", HEADS)
                pe.wait_ge(lo_ready, m.at("lo"))
                for _ in range(HEADS):
                    slot = unit_in()
                    set_in(slot)
                    for b in range(KB):
                        last = products(bank(3 * slot + b // 4), slot, b, OMHI[:, b % 4, :], OMLO[:, b % 4, :], b % 4 == 0, b % 4 == 3)
                    unit_out(last)
                statistics(T)
                statistics(T)
                chunk(HHI, HLO, ready=True)
                chunk(HHI, HLO)
                with m.loop(pe, FF - 1, units=2, use0=1, use1=1):
                    chunk(HHI, HLO)
                    chunk(HHI, HLO)
                m.add("lo", FF)
                pe.wait_ge(lo_ready, m.at("lo"))
                pe.sem_inc(passed, 1)
                with m.loop(pe, KB // 2, units=2 * DOWN_UNITS, use0=1, use1=1):
                    for p in range(2):
                        set_in(p)
                        for k in range(FF):
                            if k % KB == 0:
                                slot = unit_in()
                            last = products(bank(3 * p), slot, k % KB, FHI[:, k, :], FLO[:, k, :], k == 0, k == FF - 1)
                            if k % KB == KB - 1 or k == FF - 1:
                                unit_out(last)
                statistics(T)
                statistics(T)

            pe.wait_ge(sv_ready, 1)
            with m.loop(pe, MOD_UNITS // KB, raw=2, modt=1) as i:
                pe.wait_ge(mod_taken, m.at("modt", 1))
                m.add("modt")
                for u in range(KB):
                    s = u % RAW_SLOTS
                    if s == 0:
                        m.add("raw")
                    pe.wait_ge(landed[s], 16 * first_mod + m.at("raw") * 16)
                    for k in range(KB):
                        last = nc.tensor.matmul(PS[:, 6, 2 * u:2 * u + 2], RAW[:, s, k * P:(k + 1) * P], CV[:, k, :], start=k == 0, stop=k == KB - 1)
                    last.then_inc(raw_used[s], 1)
                nc.tensor.matmul(PS[:, 7, 0:2], IDENT[:], CV[:, 0, :], start=True, stop=True).then_inc(mod_done, 1)

            def chunk2(hi, lo, full, ready=False):
                slot = unit_in()
                set_in(slot)
                parts = ((bank(3 * slot), slice(0, T)), (bank(3 * slot + 1, TC), slice(T, TA)))[:2 if full else 1]
                for k in range(KB):
                    if ready:
                        m.add("lo")
                        pe.wait_ge(lo_ready, m.at("lo"))
                    w = slice(k * P, (k + 1) * P)
                    for o, c in parts:
                        nc.tensor.matmul(o, WH[:, slot, w], hi[:, k, c], start=k == 0, stop=False, skip_group_check=True)
                        nc.tensor.matmul(o, WH[:, slot, w], lo[:, k, c], start=False, stop=False, skip_group_check=True)
                    for o, c in parts:
                        last = nc.tensor.matmul(o, WL[:, slot, w], hi[:, k, c], start=False, stop=k == KB - 1, skip_group_check=True)
                unit_out(last)

            def chunks2(count, hi, lo, full):
                with m.loop(pe, count // 2, units=2, use0=1, use1=1):
                    chunk2(hi, lo, full)
                    chunk2(hi, lo, full)

            def attention2(count, blocks, scores, values):
                scores(0)
                scores(1)
                for n in range(count):
                    m.add("exp")
                    pe.wait_ge(exp_done, m.at("exp"))
                    for b in range(len(blocks(n))):
                        last = nc.tensor.transpose(FLAT[:, 4 * T + b * P:4 * T + (b + 1) * P], PB[:, n % 2, b * P:(b + 1) * P], IDENT[:])
                    last.then_inc(pt_done, 1)
                    if n + 2 < count:
                        scores(n + 2)
                    m.add("pts")
                    pe.wait_ge(pts_ready, m.at("pts"))
                    m.add("otk")
                    if n >= 2:
                        pe.wait_ge(o_taken, m.at("otk", -2))
                    values(n)

            def to_features(blocks):
                pe.wait_ge(o_taken, m.at("otk"))
                m.add("ss")
                pe.wait_ge(ss_ready, m.at("ss"))
                for b in range(blocks):
                    last = nc.tensor.transpose(FLAT[:, 4 * T + b * P:4 * T + (b + 1) * P], OT2[:, b, :], IDENT[:])
                last.then_inc(ot_done, 1)
                m.add("lo")
                pe.wait_ge(lo_ready, m.at("lo"))

            def heads(full, interleaved, wide, v_chunk):
                nq = 6 if full else 4
                m.add("roped")
                pe.wait_ge(roped, m.at("roped"))

                def unit(n):
                    half, qb = (n % 2, n // 2) if interleaved else (n // nq, n % nq)
                    return half, qb, range(6) if qb < 4 else range(4, 6)

                def scores(n):
                    half, qb, keys = unit(n)
                    rows = slice(half * HD, half * HD + HD)
                    c0 = 2 * (n % 2) * T
                    q = QST[rows, qb * P:(qb + 1) * P]
                    if len(keys) == 6:
                        nc.tensor.matmul(FLAT[:, c0:c0 + T], q, KST[rows, 0:T], start=True, stop=True)
                        c0 += T
                    nc.tensor.matmul(FLAT[:, c0:c0 + TC], q, KST[rows, T:TA], start=True, stop=True).then_inc(s_done, 1)

                def values(n):
                    half, qb, keys = unit(n)
                    dv = P if wide else HD
                    for b, kb in enumerate(keys):
                        v = v_chunk(kb, slice(0, P) if wide else slice(half * HD, half * HD + HD))
                        last = nc.tensor.matmul(PS[:, 6 + n % 2, 0:dv], PTS[:, n % 2, b * P:(b + 1) * P], v, start=b == 0, stop=b == len(keys) - 1)
                    last.then_inc(o_done, 1)

                attention2(2 * nq, lambda n: unit(n)[2], scores, values)
                to_features(nq)

            def v_to_tokens(chunks_):
                for n, c in enumerate(chunks_):
                    if n:
                        m.add("vtr")
                        pe.wait_ge(vt_ready, m.at("vtr"))
                    for b in range(6):
                        last = nc.tensor.transpose(FLAT[:, b * P:(b + 1) * P], U2[:, c, b * P:(b + 1) * P], IDENT[:])
                    last.then_inc(vt_done, 1)
                m.add("vtr")
                pe.wait_ge(vt_ready, m.at("vtr"))

            for l in range(DEPTH):
                full = l == 0
                statistics(TA)
                chunk2(H2HI, H2LO, True, ready=True)
                chunk2(H2HI, H2LO, True)
                chunks2(IN2 - 2, H2HI, H2LO, True)
                sets_idle()
                if l == 0:
                    with m.loop(pe, 5, hsq=1):
                        m.add("hsq")
                        pe.wait_ge(hsq_ready, m.at("hsq"))
                        for c0, c1 in ((0, T), (T, TA)):
                            last = nc.tensor.matmul(FLAT[:, 6 * T + c0:6 * T + c1], HEAD_ONES, SQ[:, 0, c0:c1], start=True, stop=True)
                        last.then_inc(stat_done, 1)
                    v_to_tokens([5] + list(range(14, 18)))
                    with m.loop(pe, 4, exp=12, pts=12, otk=12, lo=1, roped=1, ss=1):
                        heads(True, False, False, lambda kb, cols: U2[:, 5, kb * P + cols.start:kb * P + cols.stop])
                    with m.loop(pe, 4, exp=12, pts=12, otk=12, lo=1, roped=1, ss=1) as j:
                        heads(True, True, True, lambda kb, cols: U2[:, bass.ds(j + 14, 1), kb * P:(kb + 1) * P])
                else:
                    v_to_tokens([5] + list(range(14, 18)))
                    with m.loop(pe, 4, exp=8, pts=8, otk=8, lo=1, roped=1, ss=1):
                        heads(False, False, False, lambda kb, cols: U2[:, 5, kb * P + cols.start:kb * P + cols.stop])
                    with m.loop(pe, 4, exp=8, pts=8, otk=8, lo=1, roped=1, ss=1) as j:
                        heads(False, False, False, lambda kb, cols: U2[:, bass.ds(j + 14, 1), kb * P + cols.start:kb * P + cols.stop])
                chunks2(KB, H2HI, H2LO, full)
                statistics(TA if full else T)
                statistics(TA if full else T)
                m.add("lo", KB)
                pe.wait_ge(lo_ready, m.at("lo"))
                pe.sem_inc(passed, 1)
                with m.loop(pe, QUARTERS, units=2 * KB, use0=KB, use1=KB, lo=KB):
                    chunks2(KB, H2HI, H2LO, full)
                    m.add("lo", KB)
                    pe.wait_ge(lo_ready, m.at("lo"))
                    pe.sem_inc(passed, 1)
                    chunks2(KB, GHI, GLO, full)
                statistics(TA if full else T)

        @block.scalar
        def _(act):
            m = Marks(*MARKS)
            A = nc.scalar.activation

            def unit_wait():
                m.add("units")
                act.wait_ge(units_done, m.at("units"))
                return (m.n["units"] - 1) % SLOTS

            def take(dst, n=T):
                p = unit_wait()
                m.add(f"use{p}")
                A(dst, PS[:, 3 * p:3 * p + 1, 0:n], ACT.Copy).then_inc(taken[p], 1)

            def square_slot(k):
                if k >= 2:
                    act.wait_ge(sq_taken, m.at("sqt", max(1, k - 2)))
                elif k == 0 and not first[0]:
                    act.wait_ge(sq_taken, m.at("sqt"))
                return SQ[:, k % 2, :]

            first = [True]

            def squares(src, n):
                for k in range(KB):
                    dst = square_slot(k)
                    src(k, dst, n)
                first[0] = False
                m.add("sqt", KB - 1)

            def root(n):
                m.add("stat")
                act.wait_ge(stat_done, m.at("stat"))
                A(RS[:, 0:n], FLAT[:, 6 * T:6 * T + n], ACT.Sqrt, bias=COL[:, 0:1], scale=1.0 / D).then_inc(root_ready, 1)

            def of_y(k, dst, n):
                p = unit_wait()
                m.add(f"use{p}")
                A(Y[:, k, :], bank(3 * p), ACT.Copy)
                A(dst[:, 0:n], bank(3 * p), ACT.Square).then_inc(taken[p], 1)

            def of_x(k, dst, n):
                m.add("x")
                act.wait_ge(x_ready, m.at("x"))
                A(dst[:, 0:n], X[:, k, :], ACT.Square).then_inc(sq_ready, 1)

            def high(dst, src, sem_=None):
                m.add("val")
                act.wait_ge(val_ready, m.at("val"))
                A(dst, src, ACT.Copy).then_inc(hi_ready, 1)

            def norm_high(n=T):
                for k in range(KB):
                    high(HHI[:, k, :], TMP[:, k % 2, 0:n])

            def attention(count, kblocks, source, scale):
                n_keys = kblocks * P

                def exps(n):
                    m.add("max")
                    act.wait_ge(max_ready, m.at("max"))
                    A(PB[:, n % 2, 0:n_keys], source(n), ACT.Exp, bias=MX[:, 2 + n % 2:3 + n % 2], scale=scale,
                      accum_out=DEN[:, n % 2:n % 2 + 1]).then_inc(exp_done, 1)

                exps(0)
                for n in range(count):
                    if n + 1 < count:
                        exps(n + 1)
                    m.add("pt")
                    act.wait_ge(pt_done, m.at("pt"))
                    A(PTS[:, n % 2, 0:n_keys], FLAT[:, 4 * T:4 * T + n_keys], ACT.Copy).then_inc(pts_ready, 1)

            act.dma_start(MEM[:], mem).then_inc(mem_in, 16)
            act.wait_ge(consts_in, 16 * 9)
            act.wait_ge(ang_ready, 1)
            A(RT[:], SIN[:], ACT.Sin, scale=0.5).then_inc(sin_ready, 1)
            A(COS[:], SIN[:], ACT.Sin).then_inc(sin_ready, 1)
            act.wait_ge(mem_in, 16)
            act.wait_ge(tables_ready, 1)

            def of_mem(k, dst, n):
                A(dst[:, 0:n], MEM[:, k, :], ACT.Square).then_inc(sq_ready, 1)

            squares(of_mem, TC)
            root(TC)

            def of_x0(k, dst, n):
                A(dst[:, 0:n], X[:, k, :], ACT.Square).then_inc(sq_ready, 1)

            squares(of_x0, T)
            root(T)
            m.add("mem", 16)
            with m.loop(act, DEPTH, **LAYER["act"]):
                m.add("layer")
                act.wait_ge(layer_ready, m.at("layer"))
                act.dma_start(POOLW[:], poolw[bass.ds(m.at("layer", -1), 1), :, :, :].rearrange("l p b n -> p (l b) n")).then_inc(pool_in, 16)
                norm_high()
                with m.loop(act, MIX_IN // 2, units=2, use0=1, use1=1) as i:
                    take(U[:, bass.ds(2 * i, 1), :])
                    take(U[:, bass.ds(2 * i + 1, 1), :])
                for c in range(POOL):
                    high(BHI[:, POOL + c, :], U[:, C_BX + c, :])
                for c in range(POOL):
                    m.add("mixed")
                    act.wait_ge(pool_mixed, m.at("mixed"))
                    A(BHI[:, c, :], bank(c), ACT.Identity, scale=PL[:, C_SCALE + c:C_SCALE + c + 1]).then_inc(hi_ready, 1)
                for c in range(QKV):
                    m.add("vt")
                    act.wait_ge(vt_done, m.at("vt"))
                    A(U[:, C_V + c, :], bank((3, 4, 5, 6, 7, 3)[c]), ACT.Copy).then_inc(vt_ready, 1)
                attention(16, 6, lambda n: PB[:, n % 2, :], HD ** -0.5)
                for jj in range(2):
                    m.add("otd")
                    act.wait_ge(ot_done, m.at("otd"))
                    A(BHI[:, 2 * POOL + jj, :].rearrange("p (i r) -> p r i", r=4), bank(jj).rearrange("p (r i) -> p r i", r=4),
                      ACT.Copy).then_inc(hi_ready, 1)
                act.dma_start(MEM[:], mem).then_inc(mem_in, 16)
                for k in range(KB):
                    high(NHI[:, k, :], MEM[:, k, :])
                with m.loop(act, KB, units=4, use0=2, use1=2, merge=1) as i:
                    for g in range(3):
                        p = unit_wait()
                        m.add(f"use{p}")
                        A(GATE[:, g, :], bank(3 * p), ACT.Sigmoid).then_inc(taken[p], 1)
                    unit_wait()
                    m.add("use1")
                    m.add("merge")
                    act.wait_ge(merge_done, m.at("merge"))
                    A(MHI[:, bass.ds(i, 1), :], MT[:, 0:1, :], ACT.Copy).then_inc(hi_ready, 1)
                squares(of_y, T)
                root(T)
                squares(of_x, T)
                for c in range(KB):
                    take(KV[:, c:c + 1, :], TC)
                root(T)
                norm_high()
                for c in range(HEADS):
                    take(QM[:, c:c + 1, :])
                for c in range(2):
                    m.add("vt")
                    act.wait_ge(vt_done, m.at("vt"))
                    A(VM[:, c, :], bank(4 + c), ACT.Copy).then_inc(vt_ready, 1)
                attention(16, 2, lambda n: FLAT[:, 2 * (n % 2) * T:2 * (n % 2) * T + TC], P ** -0.5)
                for hh in range(HEADS):
                    m.add("otd")
                    act.wait_ge(ot_done, m.at("otd"))
                    A(OMHI[:, hh, :], bank(hh), ACT.Copy).then_inc(hi_ready, 1)

                def of_mo(k, dst, n):
                    if k % 2 == 0:
                        p = unit_wait()
                        m.add(f"use{p}")
                    p = (m.n["units"] - 1) % SLOTS
                    A(Y[:, k, :], bank(3 * p + k % 2), ACT.Copy)
                    sq = A(dst[:, 0:n], bank(3 * p + k % 2), ACT.Square)
                    sq.then_inc(taken[p] if k % 2 else sq_ready, 1)

                squares(of_mo, T)
                root(T)
                squares(of_x, T)
                root(T)
                norm_high()
                with m.loop(act, FF, units=2, use0=1, use1=1, conv=1) as i:
                    take(UA[:, 0:1, 8:8 + T])
                    m.add("conv")
                    act.wait_ge(conv_ready, m.at("conv"))
                    A(FC[:, 0, :], FC[:, 0, :], ACT.Silu).then_inc(silu_ready, 1)
                    m.add("units")
                    m.add("use1")
                    act.wait_ge(taken[1], m.at("use1", 1))
                    A(FHI[:, bass.ds(i, 1), :], FT[:, 0:1, :], ACT.Copy).then_inc(hi_ready, 1)

                def of_down(k, dst, n):
                    m.add("units", DOWN_UNITS)
                    act.wait_ge(units_done, m.at("units"))
                    m.add(f"use{k % 2}")
                    A(Y[:, k, :], bank(3 * (k % 2)), ACT.Copy)
                    A(dst[:, 0:n], bank(3 * (k % 2)), ACT.Square).then_inc(taken[k % 2], 1)

                squares(of_down, T)
                root(T)
                squares(of_x, T)
                root(T)

            act.dma_start(CTX[:], ctx).then_inc(in2, 16)
            act.dma_start(PAR2[:], params2).then_inc(in2, 16)
            act.dma_start(CV[:], cvec).then_inc(in2, 16)
            act.dma_start(SM[:], small2.partition_broadcast(P)).then_inc(in2, 16)
            act.wait_ge(in2, 64)
            A(CV[:], CV[:], ACT.Silu).then_inc(sv_ready, 1)
            act.wait_ge(lam_ready, 1)
            A(LM[:, 2:4], LM[:, 0:2], ACT.Exp).then_inc(lam_ready, 1)

            def spans(full):
                return ((0, slice(0, T)), (1, slice(T, TA)))[:2 if full else 1]

            def squares_x(full, wait):
                for k in range(KB):
                    dst = square_slot(k)
                    if wait:
                        m.add("x")
                        act.wait_ge(x_ready, m.at("x"))
                    for v, c in spans(full):
                        last = A(dst[:, c], (CTX if v else X)[:, k, :], ACT.Square)
                    last.then_inc(sq_ready, 1)
                m.add("sqt", KB - 1)

            def norm_high2(l, part, full):
                for k in range(KB):
                    m.add("val")
                    act.wait_ge(val_ready, m.at("val"))
                    for v, c in spans(full):
                        last = A(H2HI[:, k, c], TMP[:, k % 2, c], ACT.Identity, bias=MOD[:, l * MODS + part * KB + k, v:v + 1])
                    last.then_inc(hi_ready, 1)

            def take2(dst, full):
                n = TA if full else T
                p = unit_wait()
                m.add(f"use{p}")
                A(dst, FLAT[:, 3 * p * T:3 * p * T + n].unsqueeze(1), ACT.Copy).then_inc(taken[p], 1)

            def heads(full, interleaved, masked, sink=None):
                nq = 6 if full else 4

                def n_keys(n):
                    qb = n // 2 if interleaved else n % nq
                    return TA if qb < 4 else TC

                def exps(n):
                    m.add("max")
                    act.wait_ge(max_ready, m.at("max"))
                    if sink is not None:
                        A(ES[:, n % 2:n % 2 + 1], sink(n // nq), ACT.Exp, bias=MX[:, 2 + n % 2:3 + n % 2])
                    src = PB[:, n % 2, 0:n_keys(n)] if masked else FLAT[:, 2 * (n % 2) * T:2 * (n % 2) * T + n_keys(n)]
                    A(PB[:, n % 2, 0:n_keys(n)], src, ACT.Exp, bias=MX[:, 2 + n % 2:3 + n % 2], scale=HD ** -0.5,
                      accum_out=DEN[:, n % 2:n % 2 + 1]).then_inc(exp_done, 1)

                exps(0)
                for n in range(2 * nq):
                    if n + 1 < 2 * nq:
                        exps(n + 1)
                    m.add("pt")
                    act.wait_ge(pt_done, m.at("pt"))
                    A(PTS[:, n % 2, 0:n_keys(n)], FLAT[:, 4 * T:4 * T + n_keys(n)], ACT.Copy).then_inc(pts_ready, 1)

            def features_high(j, full, scale=1.0):
                n = TA if full else T
                m.add("otd")
                act.wait_ge(ot_done, m.at("otd"))
                A(H2HI[:, bass.ds(j, 1), 0:n], FLAT[:, 4 * T:4 * T + n].unsqueeze(1), ACT.Identity, scale=scale).then_inc(hi_ready, 1)

            def v_to_tokens(chunks_):
                for c in chunks_:
                    m.add("vt")
                    act.wait_ge(vt_done, m.at("vt"))
                    A(U2[:, c, :], FLAT[:, 0:TA], ACT.Copy).then_inc(vt_ready, 1)

            for l in range(DEPTH):
                full = l == 0
                if l == 0:
                    squares_x(True, False)
                else:
                    squares_x(True, True)
                root(TA)
                norm_high2(l, 0, True)
                act.dma_start(C2[:], rope2[:, 0:T]).then_inc(in2, 16)
                act.dma_start(S2[:], rope2[:, T:2 * T]).then_inc(in2, 16)
                if l:
                    act.dma_start(BAND[:], band[:, 0:BW]).then_inc(in2, 16)
                    act.dma_start(CMASK[:], band[:, BW:BW + HD]).then_inc(in2, 16)
                with m.loop(act, IN2 // 2, units=2, use0=1, use1=1) as i:
                    take2(U2[:, bass.ds(2 * i, 1), :], True)
                    take2(U2[:, bass.ds(2 * i + 1, 1), :], True)
                if l == 0:
                    with m.loop(act, 5, stat=1, rr=1) as c:
                        act.wait_ge(root_row, m.at("rr", 1))
                        m.add("rr")
                        A(SQ[:, 0:1, :], U2[:, bass.ds(c, 1), :], ACT.Square).then_inc(hsq_ready, 1)
                        m.add("stat")
                        act.wait_ge(stat_done, m.at("stat"))
                        A(RS[:], FLAT[:, 6 * T:6 * T + TA], ACT.Sqrt, bias=COL[:, 0:1], scale=1.0 / HD).then_inc(root_ready, 1)
                    v_to_tokens([5] + list(range(14, 18)))
                    with m.loop(act, 4, max=12, pt=12, otd=1) as j:
                        heads(True, False, False)
                        features_high(j, True)
                    with m.loop(act, 4, max=12, pt=12, otd=1, ss=1) as j:
                        heads(True, True, False)
                        m.add("ss")
                        act.wait_ge(sub_ready, m.at("ss"))
                        A(SS[:, 0:6], SS[:, 0:6], ACT.Sqrt, bias=COL[:, 0:1], scale=1.0 / P).then_inc(root_sub, 1)
                        features_high(j + 4, True, QKG[:, 2:3])
                else:
                    act.wait_ge(rows_in, 16)
                    v_to_tokens([5] + list(range(14, 18)))
                    with m.loop(act, 4, max=8, pt=8, otd=1) as j:
                        heads(False, False, True, lambda half: SK[:, half:half + 1])
                        features_high(j, False)
                    with m.loop(act, 4, max=8, pt=8, otd=1, bias=1) as j:
                        act.wait_ge(bias_used, m.at("bias", 1))
                        m.add("bias")
                        for h in range(2):
                            for half in range(2):
                                act.dma_start(BIAS[half * HD:(half + 1) * HD, h, :].rearrange("p (d c) -> p d c", c=HD),
                                              skewed(half)[bass.ds(2 * j + h, 1), :, :, :].rearrange("h q d c -> (h q) d c")).then_inc(bias_in, 16)
                        heads(False, False, True)
                        features_high(j + 4, False)

                def of_y2(k, dst, n):
                    p = unit_wait()
                    m.add(f"use{p}")
                    A(Y2[:, k, 0:n], FLAT[:, 3 * p * T:3 * p * T + n], ACT.Copy)
                    A(dst[:, 0:n], FLAT[:, 3 * p * T:3 * p * T + n], ACT.Square).then_inc(taken[p], 1)

                n2 = TA if full else T
                squares(of_y2, n2)
                root(n2)
                squares_x(full, True)
                root(n2)
                norm_high2(l, 3, full)
                with m.loop(act, QUARTERS, units=2 * KB, use0=KB, use1=KB, val=KB):
                    with m.loop(act, KB // 2, units=2, use0=1, use1=1, val=2) as i:
                        for p in range(2):
                            unit_wait()
                            m.add(f"use{p}")
                            A(TMP[:, p, 0:n2], FLAT[:, 3 * p * T:3 * p * T + n2], ACT.Relu).then_inc(relu_ready, 1)
                            m.add("val")
                            act.wait_ge(val_ready, m.at("val"))
                            A(GHI[:, bass.ds(2 * i + p, 1), 0:n2], TMP[:, p:p + 1, 0:n2], ACT.Copy).then_inc(hi_ready, 1)
                    m.add("units", KB)
                    m.add("use0", KB // 2)
                    m.add("use1", KB // 2)

                def of_y3(k, dst, n):
                    if k == 0:
                        m.add("y", 1)
                        act.wait_ge(y_ready, m.at("y"))
                    A(dst[:, 0:n], Y2[:, k, 0:n], ACT.Square).then_inc(sq_ready, 1)

                squares(of_y3, n2)
                root(n2)

        @block.vector
        def _(dve):
            m = Marks(*MARKS)
            TT = nc.vector.tensor_tensor
            def TTR(out, in0, in1, scale, init, op0, op1, accum):
                nc.vector.tensor_tensor_reduce(out=out, in0=in0, in1=in1, scale=scale, scalar=init, op0=op0, op1=op1, accum_out=accum)
            TS = nc.vector.tensor_scalar
            STT = nc.vector.scalar_tensor_tensor

            def par(c):
                return PL[:, c:c + 1]

            def add_squares(k, n, arrived):
                if k == 0:
                    return
                if k > 1:
                    dve.drain()
                arrived(k)
                if k == 1:
                    TT(ACC[:, 0:n], SQ[:, 0, 0:n], SQ[:, 1, 0:n], ALU.add).then_inc(sq_taken, 1)
                else:
                    TT(ACC[:, 0:n], ACC[:, 0:n], SQ[:, k % 2, 0:n], ALU.add).then_inc(sq_taken, 1)

            def sq_arrived(k):
                m.add("sq", 2 if k == 1 else 1)
                dve.wait_ge(sq_ready, m.at("sq"))

            def y_arrived(k):
                for j in ((0, 1) if k == 1 else (k,)):
                    m.add(f"use{j % 2}")
                for p in range(2) if k == 1 else (k % 2,):
                    dve.wait_ge(taken[p], m.at(f"use{p}", 1))

            def root_inverse(n):
                m.add("root")
                dve.wait_ge(root_ready, m.at("root"))
                nc.vector.reciprocal(RS[:, 0:n], RS[:, 0:n])
                dve.drain()

            def low(dst, src, hi):
                m.add("hi")
                dve.wait_ge(hi_ready, m.at("hi"))
                TT(dst, src, hi.bitcast(F32), ALU.subtract).then_inc(lo_ready, 1)

            def norm_apply(gain):
                for k in range(KB + 1):
                    if k < KB:
                        dve.drain()
                        STT(TMP[:, k % 2, 0:T], X[:, k, :], par(gain + k), RS[:, 0:T], ALU.mult, ALU.mult).then_inc(val_ready, 1)
                    if k:
                        low(HLO[:, k - 1, :], TMP[:, (k - 1) % 2, 0:T], HHI[:, k - 1, :])

            def residual(gain):
                for k in range(KB + 1):
                    if k < KB:
                        STT(TMP[:, k % 2, 0:T], Y[:, k, :], par(gain + k), RS[:, 0:T], ALU.mult, ALU.mult)
                        dve.drain()
                        TT(X[:, k, :], X[:, k, :], TMP[:, k % 2, 0:T], ALU.add).then_inc(x_ready, 1)
                    if k >= 1:
                        add_squares(k - 1, T, sq_arrived)

            def attention(count, keys, maximum, scale, dv, dst):
                def outputs(n):
                    m.add("o")
                    dve.wait_ge(o_done, m.at("o"))
                    nc.vector.reciprocal(MX[:, 4 + n % 2:5 + n % 2], DEN[:, n % 2:n % 2 + 1])
                    dve.drain()
                    TS(dst(n), PS[:, 6 + n % 2, 0:dv], MX[:, 4 + n % 2:5 + n % 2], None, ALU.mult).then_inc(o_taken, 1)

                for n in range(count):
                    m.add("s")
                    dve.wait_ge(s_done, m.at("s"))
                    dve.sem_inc(passed, 1)
                    maximum(n)
                    dve.drain()
                    TS(MX[:, 2 + n % 2:3 + n % 2], MX[:, 1:2], -scale, None, ALU.mult).then_inc(max_ready, 1)
                    dve.drain()
                    if n:
                        outputs(n - 1)
                outputs(count - 1)

            nc.vector.memset(MX[:], 0.0).then_inc(taken[0], 1)
            nc.vector.memset(DEN[:], 0.0).then_inc(taken[1], 1)
            dve.wait_ge(consts_in, 16 * 9)
            POS, ANG, TURN = COS[:], PU[:, 0, 0:T], PU[:, 1, 0:T]
            nc.vector.tensor_copy(POS, SIN[:].bitcast(I32))
            dve.drain()
            TS(ANG, POS, COL[:, 1:2], None, ALU.mult)
            dve.drain()
            TS(TURN, ANG, 1.0 / TWO_PI, MAGIC, ALU.mult, ALU.add)
            dve.drain()
            TS(TURN, TURN, -MAGIC, None, ALU.add)
            dve.drain()
            for part in TURN_PARTS:
                STT(ANG, TURN, -part, ANG, ALU.mult, ALU.add)
                dve.drain()
            TS(SIN[:], ANG, PI_IN, -PI_IN, ALU.min, ALU.max).then_inc(ang_ready, 1)
            dve.wait_ge(sin_ready, 2)
            TS(SIN[:], COS[:], COL[:, 2:3], None, ALU.mult)
            TT(RT[:], RT[:], RT[:], ALU.mult)
            dve.drain()
            TS(COS[:], RT[:], -2.0, 1.0, ALU.mult, ALU.add).then_inc(tables_ready, 1)
            dve.drain()
            for k in range(KB):
                add_squares(k, TC, sq_arrived)
            m.add("root")
            dve.wait_ge(root_ready, m.at("root"))
            nc.vector.reciprocal(MR[:], RS[:, 0:TC])
            dve.drain()
            for k in range(KB):
                add_squares(k, T, sq_arrived)
            root_inverse(T)
            m.add("layer")
            with m.loop(dve, DEPTH, **LAYER["dve"]):
                nc.vector.tensor_copy(PL[:], PAR[:, bass.ds(m.at("layer", -1), 1), :]).then_inc(layer_ready, 1)
                m.add("layer")
                dve.drain()
                norm_apply(G_MIX)
                use = {0: m.n["use0"], 1: m.n["use1"]}

                def chunk_in(c):
                    m.n[f"use{c % 2}"] = use[c % 2] + c // 2 + 1
                    dve.wait_ge(taken[c % 2], m.at(f"use{c % 2}", 1))

                dve.drain()
                nc.vector.memset(PU[:, :, 0:16], 0.0)
                nc.vector.memset(CB[:, :, 0:2], 0.0)
                for c in range(POOL):
                    chunk_in(c)
                    nc.vector.tensor_copy(PU[:, 0, 16:], U[:, c, :])
                    dve.drain()
                    for w in range(c + 2):
                        s = 1 << w
                        TT(PU[:, w + 1, 16:], PU[:, w, 16:], PU[:, w, 16 - s:16 - s + T], ALU.add)
                        dve.drain()
                    edge = (96, 64, 32)[c]
                    rows = ((slice(0, 96), c + 1), (slice(96, P), c + 2)) if edge == 96 else \
                        ((slice(0, 64), c + 1), (slice(64, P), c + 2)) if edge == 64 else \
                        ((slice(0, P), c + 2), (slice(0, 32), c + 1))
                    for r, w in rows:
                        STT(U[r, c, :], PU[r, w, 16:], COL[r, 4 + c:5 + c], PU[r, 0, 16:], ALU.mult, ALU.subtract)
                        dve.drain()
                        TT(PU[r, w, 16:32], PU[r, w, 16:32], INV16[r, c, :], ALU.mult)
                        dve.drain()
                        TT(U[r, c, 0:16], PU[r, w, 16:32], PU[r, 0, 16:32], ALU.subtract)
                        dve.drain()
                    dve.drain().then_inc(pooled, 1)
                for c in range(POOL):
                    chunk_in(C_BC + c)
                    TT(CB[:, 0, 2:], U[:, C_BC + c, :], U[:, C_BX + c, :], ALU.mult)
                    dve.drain()
                    TS(CB[:, 1, 2:], CB[:, 0, 2:], par(C_CONVB + 2 * POOL + c), None, ALU.mult)
                    for tap in (1, 0):
                        dve.drain()
                        STT(CB[:, 1, 2:], CB[:, 0, tap:tap + T], par(C_CONVB + tap * POOL + c), CB[:, 1, 2:], ALU.mult, ALU.add)
                    dve.drain()
                    TT(U[:, C_BX + c, :], CB[:, 1, 2:], U[:, C_BB + c, :], ALU.mult).then_inc(val_ready, 1)
                    dve.drain()
                swap = [(i + 8) % 16 for i in range(16)] + list(range(16, 32))
                for c in range(2 * QKV):
                    chunk_in(C_Q + c)
                    dve.sem_inc(passed, 1)
                    u = U[:, C_Q + c, :]
                    nc.vector.stream_shuffle(RT[:], u, swap)
                    dve.drain()
                    TT(RT[:], RT[:], SIN[:], ALU.mult)
                    TT(u, u, COS[:], ALU.mult)
                    dve.drain()
                    TT(u, u, RT[:], ALU.add).then_inc(roped, 1)
                    dve.drain()
                for p in range(2):
                    m.n[f"use{p}"] = use[p] + MIX_IN // 2
                m.add("units", MIX_IN)
                for c in range(POOL):
                    low(BLO[:, POOL + c, :], U[:, C_BX + c, :], BHI[:, POOL + c, :])
                for c in range(POOL):
                    m.add("hi")
                    dve.wait_ge(hi_ready, m.at("hi"))
                    STT(BLO[:, c, :], bank(c), par(C_SCALE + c), BHI[:, c, :].bitcast(F32), ALU.mult, ALU.subtract).then_inc(lo_ready, 1)

                def maximum(n):
                    r = n // 2 % 4
                    c0 = 2 * (n % 2) * T
                    TTR(PB[:, n % 2, 0:T], FLAT[:, c0:c0 + T], MASK0[:, 3 - r:3 - r + T], 1.0, NEG, ALU.add, ALU.max, MX[:, 0:1])
                    dve.drain()
                    TTR(PB[:, n % 2, T:TA], FLAT[:, c0 + T:c0 + TA], MASK12[:], 1.0, MX[:, 0:1], ALU.add, ALU.max, MX[:, 1:2])

                attention(16, 6, maximum, HD ** -0.5, HD,
                          lambda n: OTOK[:, n // 2 % 4, (n // 8) * P + n % 2 * HD:(n // 8) * P + n % 2 * HD + HD])
                for jj in range(2):
                    low(BLO[:, 2 * POOL + jj, :].rearrange("p (i r) -> p r i", r=4), bank(jj).rearrange("p (r i) -> p r i", r=4),
                        BHI[:, 2 * POOL + jj, :].rearrange("p (i r) -> p r i", r=4))
                m.add("mem", 16)
                dve.wait_ge(mem_in, m.at("mem", 16))
                for k in range(KB):
                    STT(MEM[:, k, :], MEM[:, k, :], par(G_KV + k), MR[:], ALU.mult, ALU.mult).then_inc(val_ready, 1)
                for k in range(KB):
                    m.add("hi")
                    dve.wait_ge(hi_ready, m.at("hi"))
                    TT(NLO[:, k, :], MEM[:, k, :], NHI[:, k, :].bitcast(F32), ALU.subtract).then_inc(mem_ready, 1)
                with m.loop(dve, KB, use0=2, use1=2, units=4, hi=1) as i:
                    m.add("use0", 2)
                    m.add("use1")
                    dve.wait_ge(taken[0], m.at("use0", 1))
                    dve.wait_ge(taken[1], m.at("use1", 1))
                    m.add("units", 4)
                    dve.wait_ge(units_done, m.at("units"))
                    TT(MT[:, 0, :], bank(3), GATE[:, 0, :], ALU.mult)
                    TT(MT[:, 1, :], bank(4), GATE[:, 1, :], ALU.mult)
                    dve.drain()
                    TT(MT[:, 0, :], MT[:, 0, :], MT[:, 1, :], ALU.add)
                    dve.drain()
                    TT(MT[:, 1, :], bank(5), GATE[:, 2, :], ALU.mult).then_inc(taken[1], 1)
                    m.add("use1")
                    dve.drain()
                    TT(MT[:, 0, :], MT[:, 0, :], MT[:, 1, :], ALU.add).then_inc(merge_done, 1)
                    low(MLO[:, bass.ds(i, 1), :], MT[:, 0:1, :], MHI[:, bass.ds(i, 1), :])
                    dve.drain()
                def post(gain, next_gain):
                    root_inverse(T)
                    residual(gain)
                    root_inverse(T)
                    if next_gain is not None:
                        norm_apply(next_gain)

                def y_squares():
                    for k in range(KB):
                        add_squares(k, T, y_arrived)

                y_squares()
                root_inverse(T)
                residual(G_MIXP)
                m.add("use0", 4)
                m.add("use1", 4)
                m.add("units", KB + KB)
                root_inverse(T)
                norm_apply(G_MEM)
                m.add("use0", 2)
                m.add("use1", 2)
                m.add("units", HEADS)

                def maximum_m(n):
                    c0 = 2 * (n % 2) * T
                    nc.vector.reduce_max(MX[:, 1:2], FLAT[:, c0:c0 + TC], AX.X)

                attention(16, 2, maximum_m, P ** -0.5, P, lambda n: OM[:, n % 4, (n // 4) * P:(n // 4 + 1) * P])
                for hh in range(HEADS):
                    low(OMLO[:, hh, :], bank(hh), OMHI[:, hh, :])

                def mo_arrived(k):
                    if k == 1:
                        m.add("sq")
                        dve.wait_ge(sq_ready, m.at("sq"))
                    if k % 2:
                        m.add(f"use{k // 2 % 2}")
                        dve.wait_ge(taken[k // 2 % 2], m.at(f"use{k // 2 % 2}", 1))
                    else:
                        m.add("sq")
                        dve.wait_ge(sq_ready, m.at("sq"))

                for k in range(KB):
                    add_squares(k, T, mo_arrived)
                m.add("units", HEADS)
                post(G_MEMP, G_FFN)
                dve.drain()
                nc.vector.memset(UA[:, 0, 0:8], 0.0)
                with m.loop(dve, FF, use0=1, use1=1, units=2, silu=1, hi=1) as i:
                    m.add("use0")
                    dve.wait_ge(taken[0], m.at("use0", 1))
                    TS(FC[:, 0, :], UA[:, 0, 8:8 + T], PL[:, bass.ds(i + C_CONVF + 2 * FF, 1)], None, ALU.mult)
                    dve.drain()
                    STT(FC[:, 0, :], UA[:, 0, 7:7 + T], PL[:, bass.ds(i + C_CONVF + FF, 1)], FC[:, 0, :], ALU.mult, ALU.add)
                    dve.drain()
                    STT(FC[:, 0, :], UA[:, 0, 6:6 + T], PL[:, bass.ds(i + C_CONVF, 1)], FC[:, 0, :], ALU.mult, ALU.add).then_inc(conv_ready, 1)
                    m.add("silu")
                    dve.wait_ge(silu_ready, m.at("silu"))
                    m.add("units", 2)
                    dve.wait_ge(units_done, m.at("units"))
                    TT(FT[:, 0, :], FC[:, 0, :], bank(3), ALU.mult).then_inc(taken[1], 1)
                    m.add("use1")
                    low(FLO[:, bass.ds(i, 1), :], FT[:, 0:1, :], FHI[:, bass.ds(i, 1), :])
                    dve.drain()
                m.add("units", DOWN_UNITS * KB)
                y_squares()
                post(G_FFNP, None)

            dve.drain()
            dve.wait_ge(in2, 64)
            for p in range(2):
                TTR(RT2[:, 0:HD], SM[:, 2 * p * HD:(2 * p + 1) * HD], SM[:, (2 * p + 1) * HD:(2 * p + 2) * HD], 1.0, 0.0, ALU.mult, ALU.add, LM[:, p:p + 1])
                dve.drain()
            TS(SINK8[:], SM[:, 4 * HD:4 * HD + 8], HD ** 0.5, None, ALU.mult)
            TS(QKG[:, 2:3], QKG[:, 2:3], 1.0 - LAMBDA0, None, ALU.mult)
            nc.vector.memset(ZERO[:], 0.0)
            dve.drain().then_inc(lam_ready, 1)
            dve.wait_ge(lam_ready, 2)
            TT(LM[:, 4:5], LM[:, 3:4], LM[:, 2:3], ALU.subtract)
            dve.drain()
            TS(LM[:, 4:5], LM[:, 4:5], -LAMBDA0, None, ALU.add)
            nc.vector.memset(DEN[:], 0.0).then_inc(mod_taken, 1)
            with m.loop(dve, MOD_UNITS // KB, modd=1) as i:
                m.add("modd")
                dve.wait_ge(mod_done, m.at("modd"))
                TT(MOD[:, bass.ds(i * KB, KB), :], PS[:, 6, 0:2 * KB].rearrange("p (k v) -> p k v", v=2),
                   BMOD[:, bass.ds(i * KB, KB)].unsqueeze(2).to_broadcast([P, KB, 2]), ALU.add).then_inc(mod_taken, 1)
            dve.drain()
            for l in range(DEPTH):
                for part, g, shift in ((1, 0, 1.0), (2, 1, 0.0), (4, 2, 1.0), (5, 3, 0.0)):
                    mod = MOD[:, l * MODS + part * KB:l * MODS + (part + 1) * KB, :]
                    STT(mod, mod, shift, NG[:, l, g, :].unsqueeze(2).to_broadcast([P, KB, 2]), ALU.add, ALU.mult)
            dve.drain()

            def spans(full):
                return ((0, slice(0, T)), (1, slice(T, TA)))[:2 if full else 1]

            def xpart(v):
                return CTX if v else X

            def norm_apply2(l, part, full):
                for k in range(KB + 1):
                    if k < KB:
                        dve.drain()
                        for v, c in spans(full):
                            last = STT(TMP[:, k % 2, c], xpart(v)[:, k, :], MOD[:, l * MODS + (part + 1) * KB + k, v:v + 1], RS[:, c], ALU.mult, ALU.mult)
                        last.then_inc(val_ready, 1)
                    if k:
                        m.add("hi")
                        dve.wait_ge(hi_ready, m.at("hi"))
                        for v, c in spans(full):
                            last = STT(H2LO[:, k - 1, c], TMP[:, (k - 1) % 2, c], MOD[:, l * MODS + part * KB + k - 1, v:v + 1],
                                       H2HI[:, k - 1, c].bitcast(F32), ALU.add, ALU.subtract)
                        last.then_inc(lo_ready, 1)

            def residual2(l, part, full, stats=True):
                for k in range(KB + 1):
                    if k < KB:
                        for v, c in spans(full):
                            STT(TMP[:, k % 2, c], Y2[:, k, c], MOD[:, l * MODS + part * KB + k, v:v + 1], RS[:, c], ALU.mult, ALU.mult)
                        dve.drain()
                        for v, c in spans(full):
                            last = TT(xpart(v)[:, k, :], xpart(v)[:, k, :], TMP[:, k % 2, c], ALU.add)
                        last.then_inc(x_ready, 1)
                    if k and stats:
                        add_squares(k - 1, TA if full else T, sq_arrived)
                    else:
                        dve.drain()

            def stage(dst, c, rope):
                nc.vector.tensor_copy(dst[:].unsqueeze(1), c)
                dve.drain()
                if rope:
                    nc.vector.stream_shuffle(RT2[:], dst[:, 0:T], [(i + 16) % 32 for i in range(32)])
                    dve.drain()
                    TT(RT2[:], RT2[:], S2[:], ALU.mult)
                    TT(dst[:, 0:T], dst[:, 0:T], C2[:], ALU.mult)
                    dve.drain()
                    TT(dst[:, 0:T], dst[:, 0:T], RT2[:], ALU.add)
                    dve.drain()

            def heads(full, interleaved, bias=None, sink=None, diff=False):
                nq = 6 if full else 4
                dv = P if diff else HD

                def unit(n):
                    return (n % 2, n // 2) if interleaved else (n // nq, n % nq)

                def outputs(n):
                    half, qb = unit(n)
                    m.add("o")
                    dve.wait_ge(o_done, m.at("o"))
                    r = MX[:, 4 + n % 2:5 + n % 2]
                    if sink is not None:
                        TT(DEN[:, n % 2:n % 2 + 1], DEN[:, n % 2:n % 2 + 1], ES[:, n % 2:n % 2 + 1], ALU.add)
                        dve.drain()
                    nc.vector.reciprocal(r, DEN[:, n % 2:n % 2 + 1])
                    dve.drain()
                    o = PS[:, 6 + n % 2, 0:dv]
                    if diff and half:
                        TS(r, r, LM[:, 4:5], None, ALU.mult)
                        dve.drain()
                        STT(OT2[:, qb, :], o, r, OT2[:, qb, :], ALU.mult, ALU.add).then_inc(o_taken, 1)
                    elif diff:
                        TS(OT2[:, qb, :], o, r, None, ALU.mult).then_inc(o_taken, 1)
                    else:
                        TS(OT2[:, qb, half * HD:(half + 1) * HD], o, r, None, ALU.mult).then_inc(o_taken, 1)

                for n in range(2 * nq):
                    half, qb = unit(n)
                    c0 = 2 * (n % 2) * T
                    m.add("s")
                    dve.wait_ge(s_done, m.at("s"))
                    if bias is None:
                        nc.vector.reduce_max(MX[:, 1:2], FLAT[:, c0:c0 + (TA if qb < 4 else TC)], AX.X)
                    else:
                        dve.sem_inc(passed, 1)
                        TTR(PB[:, n % 2, 0:T], FLAT[:, c0:c0 + T], bias(half, qb), 1.0, NEG, ALU.add, ALU.max, MX[:, 0:1])
                        dve.drain()
                        TTR(PB[:, n % 2, T:TA], FLAT[:, c0 + T:c0 + TA], ZERO[:], 1.0, MX[:, 0:1], ALU.add, ALU.max, MX[:, 1:2])
                    dve.drain()
                    if sink is not None:
                        TT(MX[:, 1:2], MX[:, 1:2], sink(half), ALU.max)
                        dve.drain()
                    TS(MX[:, 2 + n % 2:3 + n % 2], MX[:, 1:2], -HD ** -0.5, None, ALU.mult).then_inc(max_ready, 1)
                    dve.drain()
                    if n:
                        outputs(n - 1)
                outputs(2 * nq - 1)
                dve.drain()

            def features_low(j, full, scale=1.0):
                n = TA if full else T
                m.add("hi")
                dve.wait_ge(hi_ready, m.at("hi"))
                STT(H2LO[:, bass.ds(j, 1), 0:n], FLAT[:, 4 * T:4 * T + n].unsqueeze(1), scale, H2HI[:, bass.ds(j, 1), 0:n].bitcast(F32),
                    ALU.mult, ALU.subtract).then_inc(lo_ready, 1)

            for l in range(DEPTH):
                full = l == 0
                n2 = TA if full else T
                if l == 0:
                    for k in range(KB):
                        add_squares(k, TA, sq_arrived)
                root_inverse(TA)
                norm_apply2(l, 0, True)
                m.add("units", IN2)
                m.add("use0", IN2 // 2)
                m.add("use1", IN2 // 2)
                for p in range(2):
                    dve.wait_ge(taken[p], m.at(f"use{p}", 1))
                m.add("in2", 64 if l else 32)
                dve.wait_ge(in2, m.at("in2", 64))
                if l == 0:
                    nc.vector.memset(MX[:, 6:7], 0.0).then_inc(root_row, 1)
                    with m.loop(dve, 5, root=1) as c:
                        m.add("root")
                        dve.wait_ge(root_ready, m.at("root"))
                        nc.vector.reciprocal(RS[:], RS[:])
                        dve.drain()
                        STT(U2[:, bass.ds(c, 1), :], U2[:, bass.ds(c, 1), :], PAR2[:, bass.ds(c + (2 * KB * 4 + MOD_UNITS + 3), 1)],
                            RS[:].unsqueeze(1), ALU.mult, ALU.mult).then_inc(root_row, 1)
                        dve.drain()
                    stage(KST, U2[:, 4:5, :], True)
                    with m.loop(dve, 4, s=12, o=12, hi=1) as j:
                        stage(QST, U2[:, bass.ds(j, 1), :], True)
                        dve.drain().then_inc(roped, 1)
                        heads(True, False)
                        dve.drain().then_inc(ss_ready, 1)
                        features_low(j, True)
                        dve.drain()
                    with m.loop(dve, 4, s=12, o=12, hi=1, rr=1) as j:
                        stage(QST, U2[:, bass.ds(j + 6, 1), :], True)
                        stage(KST, U2[:, bass.ds(j + 10, 1), :], True)
                        dve.drain().then_inc(roped, 1)
                        heads(True, True, diff=True)
                        for b in range(6):
                            TTR(RT2[:, 0:P], OT2[:, b, :], OT2[:, b, :], 1.0, 0.0, ALU.mult, ALU.add, SS[:, b:b + 1])
                            dve.drain()
                        dve.drain().then_inc(sub_ready, 1)
                        m.add("rr")
                        dve.wait_ge(root_sub, m.at("rr"))
                        nc.vector.reciprocal(SS[:, 0:6], SS[:, 0:6])
                        dve.drain()
                        for b in range(6):
                            TS(OT2[:, b, :], OT2[:, b, :], SS[:, b:b + 1], None, ALU.mult)
                        dve.drain().then_inc(ss_ready, 1)
                        features_low(j + 4, True, QKG[:, 2:3])
                        dve.drain()
                else:
                    stage(KST, U2[:, 4:5, :], True)
                    with m.loop(dve, 4, s=8, o=8, hi=1) as j:
                        stage(QST, U2[:, bass.ds(j, 1), :], True)
                        for half in range(2):
                            nc.vector.tensor_copy(SK[:, half:half + 1], SM[:, bass.ds(j + (4 * HD + 4 * half), 1)])
                            nc.vector.tensor_copy(SK[:, 2 + half:3 + half], SINK8[:, bass.ds(j + 4 * half, 1)])
                        dve.drain().then_inc(roped, 1)
                        heads(False, False, lambda half, qb: BAND[:, (3 - qb) * P:(3 - qb) * P + T],
                              lambda half: SK[:, 2 + half:3 + half])
                        dve.drain().then_inc(ss_ready, 1)
                        features_low(j, False)
                        dve.drain()
                    nc.vector.memset(MX[:, 6:7], 0.0).then_inc(bias_used, 1)
                    with m.loop(dve, 4, s=8, o=8, hi=1, bias=64) as j:
                        stage(QST, U2[:, bass.ds(j + 6, 1), :], False)
                        stage(KST, U2[:, bass.ds(j + 10, 1), :], False)
                        m.add("bias", 64)
                        dve.wait_ge(bias_in, m.at("bias"))
                        for h in range(2):
                            STT(BIAS[:, h, :].rearrange("p (d c) -> p d c", c=HD), BIAS[:, h, :].rearrange("p (d c) -> p d c", c=HD), HD ** 0.5,
                                CMASK[:].unsqueeze(1).to_broadcast([P, DR, HD]), ALU.mult, ALU.add)
                        dve.drain().then_inc(roped, 1)
                        heads(False, False, lambda half, qb: BIAS[:, half, (6 - 2 * qb) * HD:(6 - 2 * qb) * HD + T])
                        dve.drain().then_inc(bias_used, 1)
                        dve.drain().then_inc(ss_ready, 1)
                        features_low(j + 4, False)
                        dve.drain()
                m.add("units", KB)
                for k in range(KB):
                    add_squares(k, n2, y_arrived)
                root_inverse(n2)
                residual2(l, 2, full)
                root_inverse(n2)
                norm_apply2(l, 3, full)
                dve.drain()
                nc.vector.memset(Y2[:], 0.0)
                dve.drain()
                with m.loop(dve, QUARTERS, units=2 * KB, use0=KB, use1=KB, relu=KB, hi=KB):
                    with m.loop(dve, KB // 2, units=2, use0=1, use1=1, relu=2, hi=2) as i:
                        for p in range(2):
                            m.add("units")
                            m.add(f"use{p}")
                            m.add("relu")
                            dve.wait_ge(relu_ready, m.at("relu"))
                            STT(TMP[:, p, 0:n2], FLAT[:, 3 * p * T:3 * p * T + n2], 0.0, TMP[:, p, 0:n2], ALU.max, ALU.mult).then_inc(taken[p], 1)
                            dve.drain().then_inc(val_ready, 1)
                            m.add("hi")
                            dve.wait_ge(hi_ready, m.at("hi"))
                            TT(GLO[:, bass.ds(2 * i + p, 1), 0:n2], TMP[:, p:p + 1, 0:n2], GHI[:, bass.ds(2 * i + p, 1), 0:n2].bitcast(F32),
                               ALU.subtract).then_inc(lo_ready, 1)
                            dve.drain()
                    with m.loop(dve, KB // 2, units=2, use0=1, use1=1) as i:
                        for p in range(2):
                            m.add("units")
                            m.add(f"use{p}")
                            dve.wait_ge(units_done, m.at("units"))
                            y = Y2[:, bass.ds(2 * i + p, 1), 0:n2]
                            TT(y, y, FLAT[:, 3 * p * T:3 * p * T + n2].unsqueeze(1), ALU.add).then_inc(taken[p], 1)
                    dve.drain()
                dve.drain().then_inc(y_ready, 1)
                for k in range(KB):
                    add_squares(k, n2, sq_arrived)
                root_inverse(n2)
                residual2(l, 5, full, stats=l == 0)


def kernel(**inputs):
    import numpy as np
    import concourse.bacc as bacc
    from concourse.bass_utils import run_bass_kernel_spmd

    a = {k: np.asarray(v) for k, v in inputs.items()}
    f4 = np.float32

    def chunks(w):
        k, n = w.shape
        return np.ascontiguousarray(w.reshape(k // P, P, n // P, P).transpose(2, 1, 0, 3))

    units = []
    for l in range(DEPTH):
        w_in = chunks(a["w_in"][l])
        units += [w_in[c] for c in range(MIX_IN)]
        branch = [chunks(a[n][l]) for n in ("w_branch_a", "w_branch_b", "w_branch_c")]
        for c in range(KB):
            units += [w_in[MIX_IN + g * KB + c] for g in range(3)]
            units.append(np.concatenate([w[c] for w in branch], axis=1))
        units += list(chunks(a["w_out"][l])) + list(chunks(a["w_mkv"][l])) + list(chunks(a["w_mq"][l]))
        mo = chunks(a["w_mo"][l])
        units += [np.concatenate([mo[2 * u], mo[2 * u + 1]], axis=1) for u in range(HEADS)]
        up = chunks(a["w_up"][l])
        for j in range(FF):
            units += [up[j], up[FF + j]]
        down = chunks(a["w_down"][l])
        pad = np.zeros((P, DOWN_UNITS * KB - FF, P), f4)
        for c in range(KB):
            padded = np.concatenate([down[c], pad], axis=1)
            units += [padded[:, u * KB:(u + 1) * KB] for u in range(DOWN_UNITS)]
    for l in range(DEPTH):
        units += list(chunks(a["w_mod_2"][l]))
    pairs = np.concatenate([np.r_[j * HD:(j + 1) * HD, (j + 4) * HD:(j + 5) * HD] for j in range(4)])
    order = np.r_[pairs, 4 * P:IN2 * P]
    rows = np.r_[pairs, 4 * P:KB * P]
    for l in range(DEPTH):
        units += list(chunks(a["w_in_2"][l][:, order])) + list(chunks(a["w_out_2"][l][rows]))
        up, down = chunks(a["w_mlp_in_2"][l]), chunks(a["w_mlp_out_2"][l])
        for q in range(QUARTERS):
            units += list(up[q * KB:(q + 1) * KB]) + list(down[:, :, q * KB:(q + 1) * KB])
    stream = np.stack(units).reshape(len(units), P, D)

    def feature_major(v):
        return np.ascontiguousarray(v.T.reshape(-1, P, v.shape[0]).transpose(1, 0, 2))

    def columns(v):
        return v.reshape(-1, P).T

    par = np.stack([np.concatenate([columns(a[n][l]) for n in (
        "norm_mix_pre", "norm_mix_post", "norm_mem_pre", "norm_mem_post", "norm_memkv", "norm_ffn_pre", "norm_ffn_post",
        "pool_scale", "conv_b_w", "conv_ffn_w")], axis=1) for l in range(DEPTH)], axis=1)

    gq, gk = (np.tile(a["qk_norm_a_2"][0, i], 2)[:, None] for i in range(2))
    params2 = np.concatenate([columns(a["norm_g_2"]), columns(a["b_mod_2"]), gq, gk, columns(a["diff_subln_2"]), gq, gq, gq, gq, gk,
                              np.kron(np.eye(2), np.ones((HD, HD))).astype(f4)], axis=1)
    small2 = np.concatenate([a["diff_lambda_2"][0].ravel(), a["sink_c_2"][0]])
    w = 2 * HD - 1
    rpb = np.zeros((2 * HEADS, DR + 1, w), f4)
    rpb[:, :, 48:48 + 31] = a["rpb_d_2"][0]

    gd = 3 * D // 8 // 4
    diag = np.zeros((DEPTH, POOL * P, POOL * P), f4)
    for g in range(4):
        diag[:, g * gd:(g + 1) * gd, g * gd:(g + 1) * gd] = a["pool_w"][:, g]
    poolw = np.stack([diag[:, k * P:(k + 1) * P, c * P:(c + 1) * P] for c, k in (
        (0, 0), (0, 1), (1, 0), (1, 1), (1, 2), (2, 1), (2, 2))], axis=2)

    consts = np.zeros((P, 2 * P + 64), f4)
    consts[:, :P] = np.eye(P)
    consts[:, P:2 * P] = 1.0
    col = consts[:, 2 * P:2 * P + 16]
    col[:, 0] = EPS
    rot = HD // 4
    inv = (f4(500000.0) ** (-np.arange(0, rot, 2, dtype=f4) / f4(rot))).astype(f4)
    for p in range(P):
        d = p % HD
        if d < rot:
            col[p, 1] = inv[d % (rot // 2)]
            col[p, 2] = -1.0 if d < rot // 2 else 1.0
    for c in range(POOL):
        for p in range(P):
            w = (2, 4, 8, 16)[(c * P + p) // gd]
            col[p, 4 + c] = 1.0 / w
            consts[p, 2 * P + 16 + 16 * c:2 * P + 32 + 16 * c] = 1.0 / np.minimum(np.arange(16) + 1, w)
    i = np.arange(P)[:, None]
    j = np.arange(T + 3)[None]
    gap = 4 * i - (j - 3)
    k = np.arange(P)[None]
    masks = np.concatenate([np.where((gap >= 0) & (gap <= 128), 0, NEG), np.where(k <= i, 0, NEG),
                            np.where((k <= i) & ((i - k) % 4 == 0), 0, NEG)], axis=1).astype(f4)

    t = np.arange(T)
    inv2 = (f4(10000.0) ** (-np.arange(16, dtype=f4) / f4(16))).astype(f4)
    d = np.arange(P) % HD
    pos = np.stack([t // 64, t % 64]).astype(f4)[d // 32]
    ang = (pos * inv2[d % 16][:, None]).astype(f4)
    rope2 = np.concatenate([np.cos(ang), np.sin(ang) * np.where(d // 16 % 2, 1, -1)[:, None]], axis=1).astype(f4)
    jj = np.arange(BW)[None]
    cq = (np.arange(P) % 64)[:, None]
    ck = np.arange(64)[None]
    cs = np.clip(cq - 8, 0, 48)
    band = np.concatenate([np.where(abs(jj - 3 * P - i) <= 128, 0, NEG), np.where((ck >= cs) & (ck < cs + 16), 0, NEG)], axis=1).astype(f4)

    ins = {
        "stream": stream, "x": feature_major(a["x"][0]), "ctx": feature_major(a["ctx_2"][0]), "params2": params2,
        "cvec": np.stack([columns(a["c_2"][0]), columns(a["c_ctx_2"])], axis=2), "small2": small2, "rope2": rope2, "band": band, "rpb": rpb, "mem": feature_major(a["mem"][0]),
        "params1": par, "positions": a["positions"][0], "consts": consts, "poolw": poolw, "masks": masks,
    }
    nc = bacc.Bacc("TRN2", target_bir_lowering=False, num_devices=1)
    t = np.arange(T)
    inv2 = (f4(10000.0) ** (-np.arange(16, dtype=f4) / f4(16))).astype(f4)
    d = np.arange(P) % HD
    pos = np.stack([t // 64, t % 64]).astype(f4)[d // 32]
    ang = (pos * inv2[d % 16][:, None]).astype(f4)
    rope2 = np.concatenate([np.cos(ang), np.sin(ang) * np.where(d // 16 % 2, 1, -1)[:, None]], axis=1).astype(f4)
    jj = np.arange(BW)[None]
    cq = (np.arange(P) % 64)[:, None]
    ck = np.arange(64)[None]
    cs = np.clip(cq - 8, 0, 48)
    band = np.concatenate([np.where(abs(jj - 3 * P - i) <= 128, 0, NEG), np.where((ck >= cs) & (ck < cs + 16), 0, NEG)], axis=1).astype(f4)

    ins = {n: np.ascontiguousarray(v) for n, v in ins.items()}
    args = {n: nc.dram_tensor("in_" + n, v.shape, mybir.dt.from_np(v.dtype), kind="ExternalInput").ap() for n, v in ins.items()}
    out = nc.dram_tensor("out", (D, T), F32, kind="ExternalOutput").ap()
    build(nc, out=out, **args)
    r = run_bass_kernel_spmd(nc, [{"in_" + n: v for n, v in ins.items()}], core_ids=[0])
    return np.ascontiguousarray(r.results[0]["out"].T)[None]
```

```python
from contextlib import ExitStack, contextmanager

import concourse.bass as bass
from concourse import mybir

ALU = mybir.AluOpType
ACT = mybir.ActivationFunctionType
AX = mybir.AxisListType
F32 = mybir.dt.float32
F32R = mybir.dt.float32r
I32 = mybir.dt.int32

P = 128
DEPTH = 2
D = 1024
KB = D // P
T = 512
TC = 256
TA = T + TC
HD = 64
EPS = 1e-6

POOL = 3
HEADS = 4
QKV = 6
MIX_IN = 4 * POOL + 3 * QKV
FF = 2816 // P
DOWN_UNITS = -(-FF // KB)
C_BX, C_BB, C_BC, C_Q, C_K, C_V = POOL, 2 * POOL, 3 * POOL, 4 * POOL, 4 * POOL + QKV, 4 * POOL + 2 * QKV
G_MIX, G_MIXP, G_MEM, G_MEMP, G_KV, G_FFN, G_FFNP = (KB * i for i in range(7))
C_SCALE = 7 * KB
C_CONVB = C_SCALE + POOL
C_CONVF = C_CONVB + 3 * POOL
NPAR = C_CONVF + 3 * FF
UNITS_1 = MIX_IN + 4 * KB + KB + KB + 4 + 4 + 2 * FF + DOWN_UNITS * KB

IN2 = 18
QUARTERS = 4
UNITS_2 = IN2 + KB + QUARTERS * 2 * KB
MODS = 6 * KB
MOD_UNITS = DEPTH * MODS
MOD_CHUNK = 5
MOD_LAYER = MOD_CHUNK * KB
MOD_DVE = DEPTH * MOD_LAYER
MOD_PE = MOD_UNITS - MOD_DVE
LAMBDA0 = 0.8 - 0.6
NEG = -1e30
TWO_PI = 6.283185307179586
TURN_PARTS = (6.28125, 0.0019350051879882812, 3.0199159819e-07)
MAGIC = 1.5 * 2 ** 23
PI_IN = 3.1415925
DR = 14
BW = DR * HD

RAW_SLOTS = 4
SLOTS = 2


class Marks:

    def __init__(self, *names):
        self.n = {name: 0 for name in names}
        self.var = {name: 0 for name in names}

    def at(self, name, more=0):
        return self.n[name] + more + self.var[name]

    def add(self, name, k=1):
        self.n[name] += k

    @contextmanager
    def loop(self, eng, count, **per):
        n0, v0 = dict(self.n), dict(self.var)
        with eng.Fori(0, count) as i:
            for name, k in per.items():
                self.var[name] = i * k + self.var[name]
            yield i
        for name in self.n:
            moved = self.n[name] - n0[name]
            assert moved == per.get(name, 0), (name, moved, per)
            self.n[name] = n0[name] + count * moved
            self.var[name] = v0[name]


def build(nc, stream, modw, crow, x, mem, params1, positions, consts, poolw, masks, ctx, params2, cvec, small2, rope2, band, rpb, out):
    with ExitStack() as stack:
        def sem(name):
            return stack.enter_context(nc.semaphore(name))

        top = [0]

        def place(name, shape, dt=F32, at=None):
            size = 1
            for s in shape[1:]:
                size *= s
            if at is None:
                at = top[0]
                top[0] += -(-size // 8) * 8
            return nc.alloc_sbuf_tensor_at(name, shape, dt, offset=base0 + 4 * at)

        base0 = -(-nc.sbuf_base // 32) * 32
        RAW = place("RAW", [P, RAW_SLOTS, D])
        WH = place("WH", [P, SLOTS, D], F32R)
        WL = place("WL", [P, SLOTS, D], F32R)
        IDENT = place("IDENT", [P, P])
        ONES = place("ONES", [P, P])
        COL = place("COL", [P, 16])
        PAR = place("PAR", [P, DEPTH, NPAR])
        PL = place("PL", [P, NPAR])
        INV16 = place("INV16", [P, POOL, 16])
        DEN = place("DEN", [P, 2])
        MX = place("MX", [P, 8])
        MR = place("MR", [P, TC])
        MOD = place("MOD", [P, MOD_UNITS, 2])
        MODL = place("MODL", [P, MOD_LAYER, 2])
        CV = place("CV", [P, KB, 2])
        X = place("X", [P, KB, T])
        S0 = top[0]
        SCR_N = 4608
        top[0] += SCR_N
        SQ = place("SQ", [P, 2, TA], at=S0)
        ACC = place("ACC", [P, TA], at=S0 + 2 * TA)
        RS = place("RS", [P, TA], at=S0 + 3 * TA)
        TMP = place("TMP", [P, 2, TA], at=S0 + 4 * TA)
        Z = top[0]

        HHI = place("HHI", [P, KB, T], F32R, at=Z)
        HLO = place("HLO", [P, KB, T], F32R, at=Z + KB * T)
        Y = place("Y", [P, KB, T], at=Z)
        ZU = Z + 2 * KB * T
        U = place("U", [P, MIX_IN, T], at=ZU)
        ZB = ZU + MIX_IN * T
        BHI = place("BHI", [P, KB, T], F32R, at=ZB)
        BLO = place("BLO", [P, KB, T], F32R, at=ZB + KB * T)
        ZT = ZB + 2 * KB * T
        MASK0 = place("MASK0", [P, T + 3], at=ZT)
        MASK12 = place("MASK12", [P, 2 * P], at=ZT + T + 8)
        COS = place("COS", [P, T], at=ZT + T + 8 + 2 * P)
        SIN = place("SIN", [P, T], at=ZT + 2 * T + 8 + 2 * P)
        CROW = place("CROW", [P, 2, D], at=Z + KB * T)
        MODW = [place(f"MODW{s}", [P, D], at=at) for s, at in enumerate((Z + KB * T + 2 * D, Z + KB * T + 3 * D, ZT - D, ZT + 3 * T + 8 + 2 * P))]
        top1 = ZT + 3 * T + 8 + 2 * P + D
        PU = place("PU", [P, 5, T + 16], at=S0)
        CB = place("CB", [P, 2, T + 2], at=S0 + 5 * (T + 16))
        RT = place("RT", [P, T], at=S0 + 5 * (T + 16) + 2 * (T + 8))
        PTS = place("PTS", [P, 2, TA], at=S0 + 2 * TA)
        PB = place("PB", [P, 2, TA], at=S0)
        OTOK = place("OTOK", [P, 4, 2 * P], at=S0 + 4 * TA)
        GATE = place("GATE", [P, 3, T], at=S0)
        MT = place("MT", [P, 2, T], at=S0 + 3 * T)
        POOLW = place("POOLW", [P, 7, P], at=ZB + 2 * POOL * T)
        MHI = place("MHI", [P, KB, T], F32R, at=ZU)
        MLO = place("MLO", [P, KB, T], F32R, at=ZU + KB * T)
        MEM = place("MEM", [P, KB, TC], at=ZU + 2 * KB * T)
        NHI = place("NHI", [P, KB, TC], F32R, at=ZU + 2 * KB * T + KB * TC)
        NLO = place("NLO", [P, KB, TC], F32R, at=ZU + 2 * KB * T + 2 * KB * TC)
        KV = place("KV", [P, KB, TC], at=ZB)
        VM = place("VM", [P, 2, HEADS * P], at=ZB + KB * TC)
        QM = place("QM", [P, HEADS, T], at=ZB + KB * TC + 2 * HEADS * P)
        OM = place("OM", [P, 4, HEADS * P], at=ZU + 2 * KB * T)
        OMHI = place("OMHI", [P, HEADS, T], F32R, at=ZU)
        OMLO = place("OMLO", [P, HEADS, T], F32R, at=ZU + HEADS * T)
        FHI = place("FHI", [P, FF, T], F32R, at=ZU)
        FLO = place("FLO", [P, FF, T], F32R, at=ZU + FF * T)
        UA = place("UA", [P, 2, T + 8], at=S0 + 6 * TA - 2 * (T + 8) + 0 * T)
        FT = place("FT", [P, 2, T], at=S0)
        FC = place("FC", [P, 2, T], at=S0 + 2 * T)
        assert ZU + 2 * FF * T <= ZT and ZU + 2 * KB * T + 3 * KB * TC <= ZB
        limit = (nc.sbuf_usable_end - base0) // 4
        assert top1 <= limit, (top1, limit)

        at2 = [Z]

        def place2(name, shape, dt=F32):
            size = 1
            for n in shape[1:]:
                size *= n
            here = at2[0]
            at2[0] += -(-size // 8) * 8
            return place(name, shape, dt, at=here)

        CTX = place2("CTX", [P, KB, TC])
        PAR2 = place2("PAR2", [P, 2 * KB * 4 + MOD_UNITS + 8 + P])
        NG = PAR2[:, 0:2 * KB * 4].rearrange("p (l g k) -> p l g k", l=DEPTH, g=4)
        BMOD = PAR2[:, 2 * KB * 4:2 * KB * 4 + MOD_UNITS]
        QKG = PAR2[:, 2 * KB * 4 + MOD_UNITS:2 * KB * 4 + MOD_UNITS + 8]
        HEAD_ONES = PAR2[:, 2 * KB * 4 + MOD_UNITS + 8:2 * KB * 4 + MOD_UNITS + 8 + P]
        SK = place2("SK", [P, 4])
        SM = place2("SM", [P, 4 * HD + 8])
        LM = place2("LM", [P, 8])
        SINK8 = place2("SINK8", [P, 8])
        ES = place2("ES", [P, 8])
        SS = place2("SS", [P, 8])
        H2HI = place2("H2HI", [P, KB, TA], F32R)
        H2LO = place2("H2LO", [P, KB, TA], F32R)
        at_u2 = at2[0]
        U2 = place2("U2", [P, IN2, TA])
        C2 = place2("C2", [P, T])
        S2 = place2("S2", [P, T])
        OT2 = place2("OT2", [P, TA // P, P])
        RT2 = place2("RT2", [P, T])
        BIAS = place2("BIAS", [P, 2, BW])
        BAND = place2("BAND", [P, BW])
        ZERO = place2("ZERO", [P, TC])
        CMASK = place2("CMASK", [P, HD])
        place2("VL_2_", [P, TA])
        assert at2[0] <= limit, (at2[0], limit)
        GHI = place("GHI", [P, KB, TA], F32R, at=at_u2)
        GLO = place("GLO", [P, KB, TA], F32R, at=at_u2 + KB * TA)
        Y2 = place("Y2", [P, KB, TA], at=at_u2 + 2 * KB * TA)
        assert at_u2 + 3 * KB * TA <= limit
        PTH = place("PTH", [P, 2, 6, 2, P], F32R, at=S0 + 2 * TA)
        hi4, lo4 = at_u2 - 12 * TA, at_u2 - 4 * TA
        u4, tail = at_u2 + 4 * TA, at_u2 + IN2 * TA
        FIRST = dict(ptl=place("PTL_1", [P, 2, 6, 2, P], F32R, at=hi4), qh=place("QH_1", [P, TA], F32R, at=lo4),
                     ql=place("QL_1", [P, TA], F32R, at=lo4 + TA), kh=place("KH_1", [P, TA], F32R, at=lo4 + 2 * TA),
                     vh=place("VH_1", [P, TA], F32R, at=lo4 + 3 * TA), kl=place("KL_1", [P, TA], F32R, at=tail),
                     vl=place("VL_1", [P, TA], F32R, at=tail + TA))
        SECOND = dict(ptl=place("PTL_2", [P, 2, 6, 2, P], F32R, at=at_u2), qh=place("QH_2", [P, TA], F32R, at=u4),
                      ql=place("QL_2", [P, TA], F32R, at=u4 + TA), kh=place("KH_2", [P, TA], F32R, at=tail),
                      kl=place("KL_2", [P, TA], F32R, at=tail + TA), vh=place("VH_2", [P, TA], F32R, at=tail + 2 * TA),
                      vl=place("VL_2", [P, TA], F32R, at=at2[0] - TA))
        COMB = place("COMB", [P, 2, TA], at=S0 + 4 * TA)
        OF = place("OF", [P, TA], at=at_u2 + 2 * TA)
        OSQ = place("OSQ", [P, TA], at=at_u2 + 3 * TA)
        bias_rows = nc.dram_tensor("bias_rows", (2 * HEADS * (DR + 1), HD, 2 * HD - 1), F32).ap()

        def skewed(half):
            row = HD * (2 * HD - 1)
            return bass.AP(tensor=bias_rows.tensor, offset=(1 - half) * row + HD - 1,
                           ap=[[(DR + 1) * row, 2 * HEADS], [2 * HD - 2, HD], [row, DR], [1, HD]])


        PS = stack.enter_context(nc.psum_tensor("PS", [P, 8, T], F32))
        FLAT = PS[:].rearrange("p b n -> p (b n)")

        def bank(b, n=T):
            return PS[:, b, 0:n]

        landed = [sem(f"landed{s}") for s in range(RAW_SLOTS)]
        raw_used = [sem(f"raw_used{s}") for s in range(RAW_SLOTS)]
        split_ready, units_done = sem("split_ready"), sem("units_done")
        taken = [sem("taken0"), sem("taken1")]
        consts_in, mem_in, pool_in, stored = sem("consts_in"), sem("mem_in"), sem("pool_in"), sem("stored")
        passed = sem("passed")
        tables_ready, sin_ready, ang_ready = sem("tables_ready"), sem("sin_ready"), sem("ang_ready")
        x_ready, sq_ready, sq_taken = sem("x_ready"), sem("sq_ready"), sem("sq_taken")
        stat_done, root_ready = sem("stat_done"), sem("root_ready")
        val_ready, hi_ready, lo_ready = sem("val_ready"), sem("hi_ready"), sem("lo_ready")
        pooled, pool_mixed = sem("pooled"), sem("pool_mixed")
        vt_done, vt_ready, roped = sem("vt_done"), sem("vt_ready"), sem("roped")
        s_done, max_ready, exp_done = sem("s_done"), sem("max_ready"), sem("exp_done")
        pt_done, pts_ready, o_done, o_taken, ot_done = sem("pt_done"), sem("pts_ready"), sem("o_done"), sem("o_taken"), sem("ot_done")
        mem_ready, layer_ready = sem("mem_ready"), sem("layer_ready")
        merge_done = sem("merge_done")
        conv_ready, silu_ready = sem("conv_ready"), sem("silu_ready")
        rows_in, in2, bias_in, sv_ready = sem("rows_in"), sem("in2"), sem("bias_in"), sem("sv_ready")
        modw_in = [sem(f"modw_in{s}") for s in range(4)]
        crow_in, crow_ready, mod_used = sem("crow_in"), sem("crow_ready"), sem("mod_used")
        mod_done, mod_taken, lam_ready, y_ready = sem("mod_done"), sem("mod_taken"), sem("lam_ready"), sem("y_ready")
        relu_ready, ss_ready, root_row, hsq_ready = sem("relu_ready"), sem("ss_ready"), sem("root_row"), sem("hsq_ready")
        bias_used, sub_ready, root_sub = sem("bias_used"), sem("sub_ready"), sem("root_sub")
        qk_high, qk_staged, v_high, v_staged = sem("qk_high"), sem("qk_staged"), sem("v_high"), sem("v_staged")
        of_taken = sem("of_taken")
        r_ready, scaled, combined, ptl_ready = sem("r_ready"), sem("scaled"), sem("combined"), sem("ptl_ready")
        MARKS = ("of", "qkh", "qks", "vh", "vs", "r", "sc", "comb", "ptl", "modw", "crow", "modu", "raw", "modd", "modt", "relu", "ss", "rr", "y", "hsq", "bias", "in2", "units", "use0", "use1", "consts", "mem", "pool", "x", "sq", "sqt", "stat", "root", "val", "hi", "lo", "pooled", "mixed",
                 "vt", "vtr", "roped", "s", "max", "exp", "pt", "pts", "o", "ot", "otk", "gate", "merge", "conv", "silu", "layer", "otd")
        steps = 4 + 16 + 2
        uses = MIX_IN // 2 + 2 * KB + KB // 2 + KB // 2 + HEADS // 2 + HEADS // 2 + FF + KB // 2
        LAYER = {
            "pe": dict(units=UNITS_1, use0=uses, use1=uses, lo=3 * KB + 2 * POOL + 2 + KB + HEADS + FF, sqt=6 * (KB - 1), pool=16,
                       pooled=POOL, vtr=QKV + 2, roped=2 * QKV, exp=32, pts=32, otk=32, mem=KB),
            "act": dict(units=UNITS_1, use0=uses, use1=uses, sqt=6 * (KB - 1), stat=6, x=3 * KB, val=3 * KB + POOL + KB, mixed=POOL,
                        vt=QKV + 2, max=32, pt=32, otd=2 + HEADS, merge=KB, conv=FF, layer=1, crow=1, modu=MOD_LAYER),
            "dve": dict(units=UNITS_1, use0=uses, use1=uses, sq=3 * KB + KB // 2, root=6, hi=3 * KB + 2 * POOL + 2 + 2 * KB + HEADS + FF,
                        o=32, s=32, mem=16, silu=FF, layer=1, crow=1, modw=MOD_LAYER // 4),
        }

        block = stack.enter_context(nc.Block())
        n_units = DEPTH * UNITS_1 + MOD_PE + DEPTH * UNITS_2
        first_mod = DEPTH * UNITS_1 // RAW_SLOTS
        after_mod = first_mod + MOD_PE // RAW_SLOTS

        @block.sync
        def _(sp):
            sp.dma_start(X[:], x).then_inc(consts_in, 16)
            sp.dma_start(PAR[:], params1).then_inc(consts_in, 16)
            sp.dma_start(CV[:], cvec).then_inc(consts_in, 16)
            sp.dma_start(IDENT[:], consts[:, 0:P]).then_inc(consts_in, 16)
            sp.dma_start(ONES[:], consts[:, P:2 * P]).then_inc(consts_in, 16)
            sp.dma_start(COL[:], consts[:, 2 * P:2 * P + 16]).then_inc(consts_in, 16)
            sp.dma_start(INV16[:].rearrange("p a b -> p (a b)"), consts[:, 2 * P + 16:2 * P + 64]).then_inc(consts_in, 16)
            sp.dma_start(MASK0[:], masks[:, 0:T + 3]).then_inc(consts_in, 16)
            sp.dma_start(MASK12[:], masks[:, T + 3:T + 3 + 2 * P]).then_inc(consts_in, 16)
            sp.dma_start(SIN[:].bitcast(I32), positions.partition_broadcast(P)).then_inc(consts_in, 16)
            sp.dma_start(bias_rows, rpb.rearrange("h d w -> (h d) w").unsqueeze(1).to_broadcast([2 * HEADS * (DR + 1), HD, 2 * HD - 1])).then_inc(rows_in, 16)
            for s in range(RAW_SLOTS):
                sp.dma_start(RAW[:, s, :], stream[s, :, :]).then_inc(landed[s], 16)
            with sp.Fori(1, n_units // RAW_SLOTS) as i:
                for s in range(RAW_SLOTS):
                    sp.wait_ge(raw_used[s], i)
                    sp.dma_start(RAW[:, s:s + 1, :], stream[bass.ds(i * RAW_SLOTS + s, 1), :, :].rearrange("u p n -> p u n")).then_inc(landed[s], 16)
            sp.wait_ge(x_ready, DEPTH * 3 * KB + DEPTH * 2 * KB)
            sp.dma_start(out.rearrange("(k p) t -> p k t", p=P), X[:]).then_inc(stored, 16)
            sp.wait_ge(stored, 16)

        @block.gpsimd
        def _(pool):
            def split(i, s, skipped=0):
                d = s % SLOTS
                pool.wait_ge(landed[s], 16 * i + 16)
                if s >= SLOTS or not isinstance(i, int):
                    pool.wait_ge(units_done, i * RAW_SLOTS + (s - SLOTS + 1 - skipped))
                nc.gpsimd.sem_inc(passed, 1)
                nc.gpsimd.tensor_tensor(WH[:, d, :].rearrange("p (b n) -> p b n", n=P), RAW[:, s, :].rearrange("p (b n) -> p b n", n=P),
                                        ONES[:].unsqueeze(1).to_broadcast([P, KB, P]), ALU.mult)
                pool.drain()
                nc.gpsimd.tensor_tensor(WL[:, d, :], RAW[:, s, :], WH[:, d, :].bitcast(F32), ALU.subtract).then_inc(split_ready, 1)
                pool.drain()
                nc.gpsimd.sem_inc(raw_used[s], 1)

            pool.wait_ge(consts_in, 16 * 10)
            for s in range(RAW_SLOTS):
                split(0, s)
            with pool.Fori(1, first_mod) as i:
                for s in range(RAW_SLOTS):
                    split(i, s)
            with pool.Fori(after_mod, n_units // RAW_SLOTS) as i:
                for s in range(RAW_SLOTS):
                    split(i, s, MOD_PE)

        @block.tensor
        def _(pe):
            m = Marks(*MARKS)

            def products(out, slot, b, hi, lo, start, stop):
                nc.tensor.matmul(out, WH[:, slot, b * P:(b + 1) * P], hi, start=start, stop=False)
                nc.tensor.matmul(out, WH[:, slot, b * P:(b + 1) * P], lo, start=False, stop=False)
                return nc.tensor.matmul(out, WL[:, slot, b * P:(b + 1) * P], hi, start=False, stop=stop)

            def unit_in():
                pe.wait_ge(split_ready, m.at("units", 1))
                return m.n["units"] % SLOTS

            def unit_out(last):
                last.then_inc(units_done, 1)
                m.add("units")

            def set_in(p):
                pe.wait_ge(taken[p], m.at(f"use{p}", 1))
                m.add(f"use{p}")

            def sets_idle():
                for p in range(2):
                    pe.wait_ge(taken[p], m.at(f"use{p}", 1))

            def chunk(hi, lo, n=T, ready=False):
                slot = unit_in()
                set_in(slot)
                for k in range(KB):
                    if ready:
                        m.add("lo")
                        pe.wait_ge(lo_ready, m.at("lo"))
                    last = products(bank(3 * slot, n), slot, k, hi[:, k, 0:n], lo[:, k, 0:n], k == 0, k == KB - 1)
                unit_out(last)

            def statistics(n):
                m.add("sqt", KB - 1)
                pe.wait_ge(sq_taken, m.at("sqt"))
                for c0 in range(0, n, T):
                    c1 = min(c0 + T, n)
                    last = nc.tensor.matmul(FLAT[:, 6 * T + c0:6 * T + c1], ONES[:], ACC[:, c0:c1], start=True, stop=True)
                last.then_inc(stat_done, 1)

            def attention(count, kblocks, scores, values):
                scores(0)
                scores(1)
                for n in range(count):
                    m.add("exp")
                    pe.wait_ge(exp_done, m.at("exp"))
                    for b in range(kblocks):
                        last = nc.tensor.transpose(FLAT[:, 4 * T + b * P:4 * T + (b + 1) * P], PB[:, n % 2, b * P:(b + 1) * P], IDENT[:])
                    last.then_inc(pt_done, 1)
                    if n + 2 < count:
                        scores(n + 2)
                    m.add("pts")
                    pe.wait_ge(pts_ready, m.at("pts"))
                    m.add("otk")
                    if n >= 2:
                        pe.wait_ge(o_taken, m.at("otk", -2))
                    values(n)

            pe.wait_ge(consts_in, 16 * 10)
            statistics(TC)
            statistics(T)
            with m.loop(pe, DEPTH, **LAYER["pe"]):
                chunk(HHI, HLO, ready=True)
                chunk(HHI, HLO)
                with m.loop(pe, (MIX_IN - 2) // 2, units=2, use0=1, use1=1):
                    chunk(HHI, HLO)
                    chunk(HHI, HLO)
                sets_idle()
                m.add("pool", 16)
                pe.wait_ge(pool_in, m.at("pool"))
                m.add("pooled", POOL)
                pe.wait_ge(pooled, m.at("pooled"))
                b = 0
                for c, ks in enumerate(((0, 1), (0, 1, 2), (1, 2))):
                    for k in ks:
                        last = nc.tensor.matmul(bank(c), POOLW[:, b, :], U[:, k, :], start=k == ks[0], stop=k == ks[-1])
                        b += 1
                    last.then_inc(pool_mixed, 1)
                for c in range(QKV):
                    if c == 5:
                        pe.wait_ge(vt_ready, m.at("vtr", 1))
                    for b in range(4):
                        v = U[:, C_V + c, :]
                        src = v[:, b * P:(b + 1) * P] if c < 2 else v.rearrange("p (i r) -> p r i", r=4)[:, b, :]
                        last = nc.tensor.transpose(PS[:, (3, 4, 5, 6, 7, 3)[c], b * P:(b + 1) * P], src, IDENT[:])
                    last.then_inc(vt_done, 1)
                m.add("vtr", QKV)
                pe.wait_ge(vt_ready, m.at("vtr"))
                m.add("roped", 2 * QKV)
                pe.wait_ge(roped, m.at("roped"))
                m.add("lo", 2 * POOL)
                pe.wait_ge(lo_ready, m.at("lo"))

                def head(n):
                    jj, r, half = n // 8, n // 2 % 4, n % 2
                    return jj, r, slice(half * HD, half * HD + HD)

                def scores(n):
                    jj, r, rows = head(n)
                    for g in range(3):
                        q = U[rows, C_Q + 2 * g + jj, :].rearrange("p (i r) -> p r i", r=4)[:, r, :]
                        k = U[rows, C_K + 2 * g + jj, :]
                        c0 = 2 * (n % 2) * T
                        if g == 0:
                            o = FLAT[:, c0:c0 + T]
                        else:
                            k = k.rearrange("p (i r) -> p r i", r=4)[:, r, :]
                            o = FLAT[:, c0 + T + (g - 1) * P:c0 + T + g * P]
                        last = nc.tensor.matmul(o, q, k, start=True, stop=True)
                    last.then_inc(s_done, 1)

                def values(n):
                    jj, r, rows = head(n)
                    for b in range(6):
                        g = max(b - 3, 0)
                        vb = b if b < 4 else r
                        v = U[:, C_V + 2 * g + jj, vb * P + rows.start:vb * P + rows.stop]
                        last = nc.tensor.matmul(PS[:, 6 + n % 2, 0:HD], PTS[:, n % 2, b * P:(b + 1) * P], v, start=b == 0, stop=b == 5)
                    last.then_inc(o_done, 1)

                attention(16, 6, scores, values)
                pe.wait_ge(o_taken, m.at("otk"))
                for jj in range(2):
                    for r in range(4):
                        last = nc.tensor.transpose(PS[:, jj, r * P:(r + 1) * P], OTOK[:, r, jj * P:(jj + 1) * P], IDENT[:])
                    last.then_inc(ot_done, 1)
                m.add("lo", 2)
                pe.wait_ge(lo_ready, m.at("lo"))
                pe.sem_inc(passed, 1)
                with m.loop(pe, KB, units=4, use0=2, use1=2):
                    for g in range(3):
                        chunk(HHI, HLO)
                    slot = unit_in()
                    set_in(1)
                    for b, (bk, first, end) in enumerate(((3, 1, 0), (3, 0, 0), (3, 0, 1), (4, 1, 0), (4, 0, 0), (4, 0, 1), (5, 1, 0), (5, 0, 1))):
                        last = products(bank(bk), slot, b, BHI[:, b, :], BLO[:, b, :], bool(first), bool(end))
                    unit_out(last)
                chunk(MHI, MLO, ready=True)
                for _ in range(KB - 1):
                    chunk(MHI, MLO)
                statistics(T)
                m.add("mem", KB)
                pe.wait_ge(mem_ready, m.at("mem"))
                for _ in range(KB):
                    chunk(NHI, NLO, TC)
                statistics(T)
                chunk(HHI, HLO, ready=True)
                for _ in range(HEADS - 1):
                    chunk(HHI, HLO)
                sets_idle()
                for c in range(2):
                    for hh in range(HEADS):
                        last = nc.tensor.transpose(PS[:, 4 + c, hh * P:(hh + 1) * P], KV[:, HEADS + hh, c * P:(c + 1) * P], IDENT[:])
                    last.then_inc(vt_done, 1)
                m.add("vtr", 2)
                pe.wait_ge(vt_ready, m.at("vtr"))

                def scores_m(n):
                    hh, qb = n // 4, n % 4
                    nc.tensor.matmul(FLAT[:, 2 * (n % 2) * T:2 * (n % 2) * T + TC], QM[:, hh, qb * P:(qb + 1) * P], KV[:, hh, :],
                                     start=True, stop=True).then_inc(s_done, 1)

                def values_m(n):
                    hh = n // 4
                    for b in range(2):
                        last = nc.tensor.matmul(PS[:, 6 + n % 2, 0:P], PTS[:, n % 2, b * P:(b + 1) * P], VM[:, b, hh * P:(hh + 1) * P],
                                                start=b == 0, stop=b == 1)
                    last.then_inc(o_done, 1)

                attention(16, 2, scores_m, values_m)
                pe.wait_ge(o_taken, m.at("otk"))
                for hh in range(HEADS):
                    for qb in range(4):
                        last = nc.tensor.transpose(PS[:, hh, qb * P:(qb + 1) * P], OM[:, qb, hh * P:(hh + 1) * P], IDENT[:])
                    last.then_inc(ot_done, 1)
                m.add("lo", HEADS)
                pe.wait_ge(lo_ready, m.at("lo"))
                for _ in range(HEADS):
                    slot = unit_in()
                    set_in(slot)
                    for b in range(KB):
                        last = products(bank(3 * slot + b // 4), slot, b, OMHI[:, b % 4, :], OMLO[:, b % 4, :], b % 4 == 0, b % 4 == 3)
                    unit_out(last)
                statistics(T)
                statistics(T)
                chunk(HHI, HLO, ready=True)
                chunk(HHI, HLO)
                with m.loop(pe, FF - 1, units=2, use0=1, use1=1):
                    chunk(HHI, HLO)
                    chunk(HHI, HLO)
                m.add("lo", FF)
                pe.wait_ge(lo_ready, m.at("lo"))
                pe.sem_inc(passed, 1)
                with m.loop(pe, KB // 2, units=2 * DOWN_UNITS, use0=1, use1=1):
                    for p in range(2):
                        set_in(p)
                        for k in range(FF):
                            if k % KB == 0:
                                slot = unit_in()
                            last = products(bank(3 * p), slot, k % KB, FHI[:, k, :], FLO[:, k, :], k == 0, k == FF - 1)
                            if k % KB == KB - 1 or k == FF - 1:
                                unit_out(last)
                statistics(T)
                statistics(T)

            def modulation():
                pe.wait_ge(mod_taken, m.at("modt", 1))
                m.add("modt")
                for u in range(KB):
                    s = u % RAW_SLOTS
                    if s == 0:
                        m.add("raw")
                    pe.wait_ge(landed[s], 16 * first_mod + m.at("raw") * 16)
                    for k in range(KB):
                        last = nc.tensor.matmul(PS[:, 5, 2 * u:2 * u + 2], RAW[:, s, k * P:(k + 1) * P], CV[:, k, :], start=k == 0, stop=k == KB - 1)
                    last.then_inc(raw_used[s], 1)
                nc.tensor.matmul(PS[:, 5, 2 * KB:2 * KB + 2], IDENT[:], CV[:, 0, :], start=True, stop=True).then_inc(mod_done, 1)

            pe.wait_ge(sv_ready, 1)
            modulation()

            def chunk2(hi, lo, full, ready=False):
                slot = unit_in()
                set_in(slot)
                parts = ((bank(3 * slot), slice(0, T)), (bank(3 * slot + 1, TC), slice(T, TA)))[:2 if full else 1]
                for k in range(KB):
                    if ready:
                        m.add("lo")
                        pe.wait_ge(lo_ready, m.at("lo"))
                    w = slice(k * P, (k + 1) * P)
                    for o, c in parts:
                        nc.tensor.matmul(o, WH[:, slot, w], hi[:, k, c], start=k == 0, stop=False, skip_group_check=True)
                        nc.tensor.matmul(o, WH[:, slot, w], lo[:, k, c], start=False, stop=False, skip_group_check=True)
                    for o, c in parts:
                        last = nc.tensor.matmul(o, WL[:, slot, w], hi[:, k, c], start=False, stop=k == KB - 1, skip_group_check=True)
                unit_out(last)

            def chunks2(count, hi, lo, full):
                with m.loop(pe, count // 2, units=2, use0=1, use1=1):
                    chunk2(hi, lo, full)
                    chunk2(hi, lo, full)

            def heads(bufs, full, diff):
                nq = 6 if full else 4
                kh, kl, qh, ql, vh, vl, ptl = (bufs[n] for n in ("kh", "kl", "qh", "ql", "vh", "vl", "ptl"))
                m.add("qks")
                pe.wait_ge(qk_staged, m.at("qks"))

                def keys(qb):
                    return range(6) if qb < 4 else range(4, 6)

                def scores(n):
                    half, qb = (n % 2, n // 2) if diff else (n // nq, n % nq)
                    rows = slice(half * HD, half * HD + HD)
                    o = 2 * (n % 2) * T
                    q = slice(qb * P, (qb + 1) * P)
                    for k0, k1 in ((0, T), (T, TA)) if qb < 4 else ((T, TA),):
                        for x, (lq, rk) in enumerate(((qh, kh), (qh, kl), (ql, kh))):
                            last = nc.tensor.matmul(FLAT[:, o:o + k1 - k0], lq[rows, q], rk[rows, k0:k1], start=x == 0, stop=x == 2)
                        o += k1 - k0
                    last.then_inc(s_done, 1)

                def transposed(src, qb):
                    for b in range(len(keys(qb))):
                        last = nc.tensor.transpose(FLAT[:, 4 * T + b * P:4 * T + (b + 1) * P], src[:, b * P:(b + 1) * P], IDENT[:])
                    last.then_inc(pt_done, 1)

                def values(i):
                    par = 0 if diff else i % 2
                    if diff:
                        m.add("of")
                        if i >= 2:
                            pe.wait_ge(of_taken, m.at("of", -2))
                    else:
                        m.add("lo")
                        pe.wait_ge(lo_ready, m.at("lo", -2))
                    ks = keys(2 * i % nq)
                    for b, kb in enumerate(ks):
                        for x, (lv, rp) in enumerate(((vh, PTH), (vh, ptl), (vl, PTH))):
                            last = nc.tensor.matmul(PS[:, 6 + i % 2, 0:2 * P], lv[:, kb * P:(kb + 1) * P], rp[:, par, b, :, :].rearrange("p q n -> p (q n)"),
                                                    start=b == 0 and x == 0, stop=b == len(ks) - 1 and x == 2)
                    last.then_inc(o_done, 1)

                def v_in():
                    m.add("vs")
                    pe.wait_ge(v_staged, m.at("vs"))

                scores(0)
                scores(1)
                if diff:
                    for qb in range(nq):
                        for n in (2 * qb, 2 * qb + 1):
                            m.add("exp")
                            if n + 2 < 2 * nq:
                                pe.wait_ge(exp_done, m.at("exp"))
                                scores(n + 2)
                        m.add("comb")
                        pe.wait_ge(combined, m.at("comb"))
                        if qb:
                            pe.wait_ge(ptl_ready, m.at("ptl"))
                        transposed(COMB[:, qb % 2, :], qb)
                        m.add("ptl")
                        if qb == 1:
                            v_in()
                        if qb % 2:
                            pe.wait_ge(ptl_ready, m.at("ptl"))
                            values(qb // 2)
                    pe.wait_ge(of_taken, m.at("of"))
                    for c0, c1 in ((0, T), (T, TA)):
                        last = nc.tensor.matmul(FLAT[:, 4 * T + c0:4 * T + c1], ONES[:], OSQ[:, c0:c1], start=True, stop=True)
                    last.then_inc(stat_done, 1)
                    return
                for n in range(2 * nq):
                    m.add("sc")
                    pe.wait_ge(scaled, m.at("sc"))
                    if n:
                        pe.wait_ge(ptl_ready, m.at("ptl"))
                    transposed(PB[:, n % 2, :], n % nq)
                    m.add("ptl")
                    if n + 2 < 2 * nq:
                        scores(n + 2)
                    if n == 2 and bufs is SECOND:
                        v_in()
                    if n % 2 == 0 and n:
                        values(n // 2 - 1)
                pe.wait_ge(ptl_ready, m.at("ptl"))
                values(nq - 1)

            def v_to_tokens(chunks_):
                for n, c in enumerate(chunks_):
                    if n:
                        m.add("vtr")
                        pe.wait_ge(vt_ready, m.at("vtr"))
                    for b in range(6):
                        last = nc.tensor.transpose(FLAT[:, b * P:(b + 1) * P], U2[:, c, b * P:(b + 1) * P], IDENT[:])
                    last.then_inc(vt_done, 1)
                m.add("vtr")
                pe.wait_ge(vt_ready, m.at("vtr"))

            for l in range(DEPTH):
                full = l == 0
                statistics(TA)
                if l == 0:
                    modulation()
                chunk2(H2HI, H2LO, True, ready=True)
                chunk2(H2HI, H2LO, True)
                chunks2(IN2 - 2, H2HI, H2LO, True)
                sets_idle()
                if l == 0:
                    with m.loop(pe, 5, hsq=1):
                        m.add("hsq")
                        pe.wait_ge(hsq_ready, m.at("hsq"))
                        for c0, c1 in ((0, T), (T, TA)):
                            last = nc.tensor.matmul(FLAT[:, 6 * T + c0:6 * T + c1], HEAD_ONES, SQ[:, 0, c0:c1], start=True, stop=True)
                        last.then_inc(stat_done, 1)
                    v_to_tokens([5] + list(range(14, 18)))
                    m.add("vs")
                    pe.wait_ge(v_staged, m.at("vs"))
                    with m.loop(pe, 4, qks=1, sc=12, ptl=12, lo=6):
                        heads(FIRST, True, False)
                    m.add("qks")
                    pe.wait_ge(lo_ready, m.at("lo"))
                    pe.sem_inc(passed, 1)
                    m.add("exp", 4 * 12)
                    with m.loop(pe, 4, qks=1, vs=1, exp=12, comb=6, ptl=6, of=3, lo=1):
                        heads(SECOND, True, True)
                        m.add("lo")
                    m.add("sc", 4 * 6)
                    m.add("qks")
                else:
                    v_to_tokens([5] + list(range(14, 18)))
                    m.add("vs")
                    pe.wait_ge(v_staged, m.at("vs"))
                    with m.loop(pe, 4, qks=1, sc=8, ptl=8, lo=4):
                        heads(FIRST, False, False)
                    m.add("qks")
                    with m.loop(pe, 4, qks=1, vs=1, sc=8, ptl=8, lo=4):
                        heads(SECOND, False, False)
                    m.add("qks")
                pe.wait_ge(lo_ready, m.at("lo"))
                pe.sem_inc(passed, 1)
                chunks2(KB, H2HI, H2LO, full)
                statistics(TA if full else T)
                statistics(TA if full else T)
                m.add("lo", KB)
                pe.wait_ge(lo_ready, m.at("lo"))
                pe.sem_inc(passed, 1)
                with m.loop(pe, QUARTERS, units=2 * KB, use0=KB, use1=KB, lo=KB):
                    chunks2(KB, H2HI, H2LO, full)
                    m.add("lo", KB)
                    pe.wait_ge(lo_ready, m.at("lo"))
                    pe.sem_inc(passed, 1)
                    chunks2(KB, GHI, GLO, full)
                statistics(TA if full else T)

        @block.scalar
        def _(act):
            m = Marks(*MARKS)
            A = nc.scalar.activation

            def unit_wait():
                m.add("units")
                act.wait_ge(units_done, m.at("units"))
                return (m.n["units"] - 1) % SLOTS

            def take(dst, n=T):
                p = unit_wait()
                m.add(f"use{p}")
                A(dst, PS[:, 3 * p:3 * p + 1, 0:n], ACT.Copy).then_inc(taken[p], 1)

            def square_slot(k):
                if k >= 2:
                    act.wait_ge(sq_taken, m.at("sqt", max(1, k - 2)))
                elif k == 0 and not first[0]:
                    act.wait_ge(sq_taken, m.at("sqt"))
                return SQ[:, k % 2, :]

            first = [True]

            def squares(src, n):
                for k in range(KB):
                    dst = square_slot(k)
                    src(k, dst, n)
                first[0] = False
                m.add("sqt", KB - 1)

            def root(n):
                m.add("stat")
                act.wait_ge(stat_done, m.at("stat"))
                A(RS[:, 0:n], FLAT[:, 6 * T:6 * T + n], ACT.Sqrt, bias=COL[:, 0:1], scale=1.0 / D).then_inc(root_ready, 1)

            def of_y(k, dst, n):
                p = unit_wait()
                m.add(f"use{p}")
                A(Y[:, k, :], bank(3 * p), ACT.Copy)
                A(dst[:, 0:n], bank(3 * p), ACT.Square).then_inc(taken[p], 1)

            def of_x(k, dst, n):
                m.add("x")
                act.wait_ge(x_ready, m.at("x"))
                A(dst[:, 0:n], X[:, k, :], ACT.Square).then_inc(sq_ready, 1)

            def high(dst, src, sem_=None):
                m.add("val")
                act.wait_ge(val_ready, m.at("val"))
                A(dst, src, ACT.Copy).then_inc(hi_ready, 1)

            def norm_high(n=T):
                for k in range(KB):
                    high(HHI[:, k, :], TMP[:, k % 2, 0:n])

            def attention(count, kblocks, source, scale):
                n_keys = kblocks * P

                def exps(n):
                    m.add("max")
                    act.wait_ge(max_ready, m.at("max"))
                    A(PB[:, n % 2, 0:n_keys], source(n), ACT.Exp, bias=MX[:, 2 + n % 2:3 + n % 2], scale=scale,
                      accum_out=DEN[:, n % 2:n % 2 + 1]).then_inc(exp_done, 1)

                exps(0)
                for n in range(count):
                    if n + 1 < count:
                        exps(n + 1)
                    m.add("pt")
                    act.wait_ge(pt_done, m.at("pt"))
                    A(PTS[:, n % 2, 0:n_keys], FLAT[:, 4 * T:4 * T + n_keys], ACT.Copy).then_inc(pts_ready, 1)

            act.dma_start(MEM[:], mem).then_inc(mem_in, 16)
            act.wait_ge(consts_in, 16 * 10)
            A(CV[:], CV[:], ACT.Silu).then_inc(sv_ready, 1)
            act.wait_ge(ang_ready, 1)
            A(RT[:], SIN[:], ACT.Sin, scale=0.5).then_inc(sin_ready, 1)
            A(COS[:], SIN[:], ACT.Sin).then_inc(sin_ready, 1)
            act.wait_ge(mem_in, 16)
            act.wait_ge(tables_ready, 1)

            def of_mem(k, dst, n):
                A(dst[:, 0:n], MEM[:, k, :], ACT.Square).then_inc(sq_ready, 1)

            squares(of_mem, TC)
            root(TC)

            def of_x0(k, dst, n):
                A(dst[:, 0:n], X[:, k, :], ACT.Square).then_inc(sq_ready, 1)

            squares(of_x0, T)
            root(T)
            m.add("mem", 16)
            with m.loop(act, DEPTH, **LAYER["act"]):
                m.add("layer")
                act.wait_ge(layer_ready, m.at("layer"))
                act.dma_start(POOLW[:], poolw[bass.ds(m.at("layer", -1), 1), :, :, :].rearrange("l p b n -> p (l b) n")).then_inc(pool_in, 16)
                norm_high()
                with m.loop(act, MIX_IN // 2, units=2, use0=1, use1=1) as i:
                    take(U[:, bass.ds(2 * i, 1), :])
                    take(U[:, bass.ds(2 * i + 1, 1), :])
                for c in range(POOL):
                    high(BHI[:, POOL + c, :], U[:, C_BX + c, :])
                for c in range(POOL):
                    m.add("mixed")
                    act.wait_ge(pool_mixed, m.at("mixed"))
                    A(BHI[:, c, :], bank(c), ACT.Identity, scale=PL[:, C_SCALE + c:C_SCALE + c + 1]).then_inc(hi_ready, 1)
                for c in range(QKV):
                    m.add("vt")
                    act.wait_ge(vt_done, m.at("vt"))
                    A(U[:, C_V + c, :], bank((3, 4, 5, 6, 7, 3)[c]), ACT.Copy).then_inc(vt_ready, 1)
                attention(16, 6, lambda n: PB[:, n % 2, :], HD ** -0.5)
                for jj in range(2):
                    m.add("otd")
                    act.wait_ge(ot_done, m.at("otd"))
                    A(BHI[:, 2 * POOL + jj, :].rearrange("p (i r) -> p r i", r=4), bank(jj).rearrange("p (r i) -> p r i", r=4),
                      ACT.Copy).then_inc(hi_ready, 1)
                act.dma_start(MEM[:], mem).then_inc(mem_in, 16)
                for k in range(KB):
                    high(NHI[:, k, :], MEM[:, k, :])
                with m.loop(act, KB, units=4, use0=2, use1=2, merge=1) as i:
                    for g in range(3):
                        p = unit_wait()
                        m.add(f"use{p}")
                        A(GATE[:, g, :], bank(3 * p), ACT.Sigmoid).then_inc(taken[p], 1)
                    unit_wait()
                    m.add("use1")
                    m.add("merge")
                    act.wait_ge(merge_done, m.at("merge"))
                    A(MHI[:, bass.ds(i, 1), :], MT[:, 0:1, :], ACT.Copy).then_inc(hi_ready, 1)
                squares(of_y, T)
                root(T)
                squares(of_x, T)
                for c in range(KB):
                    take(KV[:, c:c + 1, :], TC)
                root(T)
                norm_high()
                for c in range(HEADS):
                    take(QM[:, c:c + 1, :])
                for c in range(2):
                    m.add("vt")
                    act.wait_ge(vt_done, m.at("vt"))
                    A(VM[:, c, :], bank(4 + c), ACT.Copy).then_inc(vt_ready, 1)
                attention(16, 2, lambda n: FLAT[:, 2 * (n % 2) * T:2 * (n % 2) * T + TC], P ** -0.5)
                for hh in range(HEADS):
                    m.add("otd")
                    act.wait_ge(ot_done, m.at("otd"))
                    A(OMHI[:, hh, :], bank(hh), ACT.Copy).then_inc(hi_ready, 1)

                def of_mo(k, dst, n):
                    if k % 2 == 0:
                        p = unit_wait()
                        m.add(f"use{p}")
                    p = (m.n["units"] - 1) % SLOTS
                    A(Y[:, k, :], bank(3 * p + k % 2), ACT.Copy)
                    sq = A(dst[:, 0:n], bank(3 * p + k % 2), ACT.Square)
                    sq.then_inc(taken[p] if k % 2 else sq_ready, 1)

                squares(of_mo, T)
                root(T)
                squares(of_x, T)
                root(T)
                norm_high()
                with m.loop(act, FF, units=2, use0=1, use1=1, conv=1) as i:
                    take(UA[:, 0:1, 8:8 + T])
                    m.add("conv")
                    act.wait_ge(conv_ready, m.at("conv"))
                    A(FC[:, 0, :], FC[:, 0, :], ACT.Silu).then_inc(silu_ready, 1)
                    m.add("units")
                    m.add("use1")
                    act.wait_ge(taken[1], m.at("use1", 1))
                    A(FHI[:, bass.ds(i, 1), :], FT[:, 0:1, :], ACT.Copy).then_inc(hi_ready, 1)

                act.dma_start(CROW[:].rearrange("p v n -> p (v n)"), crow.partition_broadcast(P)).then_inc(crow_in, 16)
                m.add("crow")
                act.wait_ge(crow_in, m.at("crow") * 16)
                A(CROW[:], CROW[:], ACT.Silu).then_inc(crow_ready, 1)

                def of_down(k, dst, n):
                    for u in range(k * MOD_CHUNK, (k + 1) * MOD_CHUNK):
                        if u >= 4:
                            act.wait_ge(mod_used, m.at("modu", u - 3))
                        act.dma_start(MODW[u % 4][:].unsqueeze(1), modw[bass.ds(m.at("layer", -1) * MOD_LAYER + u, 1), :, :].rearrange("u p n -> p u n")).then_inc(modw_in[u % 4], 16)
                    m.add("units", DOWN_UNITS)
                    act.wait_ge(units_done, m.at("units"))
                    m.add(f"use{k % 2}")
                    A(Y[:, k, :], bank(3 * (k % 2)), ACT.Copy)
                    A(dst[:, 0:n], bank(3 * (k % 2)), ACT.Square).then_inc(taken[k % 2], 1)

                squares(of_down, T)
                m.add("modu", MOD_LAYER)
                root(T)
                squares(of_x, T)
                root(T)

            act.dma_start(CTX[:], ctx).then_inc(in2, 16)
            act.dma_start(PAR2[:], params2).then_inc(in2, 16)
            act.dma_start(SM[:], small2.partition_broadcast(P)).then_inc(in2, 16)
            act.wait_ge(lam_ready, 1)
            A(LM[:, 2:4], LM[:, 0:2], ACT.Exp).then_inc(lam_ready, 1)

            def spans(full):
                return ((0, slice(0, T)), (1, slice(T, TA)))[:2 if full else 1]

            def squares_x(full, wait):
                for k in range(KB):
                    dst = square_slot(k)
                    if wait:
                        m.add("x")
                        act.wait_ge(x_ready, m.at("x"))
                    for v, c in spans(full):
                        last = A(dst[:, c], (CTX if v else X)[:, k, :], ACT.Square)
                    last.then_inc(sq_ready, 1)
                m.add("sqt", KB - 1)

            def norm_high2(l, part, full):
                for k in range(KB):
                    m.add("val")
                    act.wait_ge(val_ready, m.at("val"))
                    for v, c in spans(full):
                        last = A(H2HI[:, k, c], TMP[:, k % 2, c], ACT.Identity, bias=MOD[:, l * MODS + part * KB + k, v:v + 1])
                    last.then_inc(hi_ready, 1)

            def take2(dst, full):
                n = TA if full else T
                p = unit_wait()
                m.add(f"use{p}")
                A(dst, FLAT[:, 3 * p * T:3 * p * T + n].unsqueeze(1), ACT.Copy).then_inc(taken[p], 1)

            m.add("o", DEPTH * 32)

            def high_parts(pairs, ready):
                for dst, src in pairs:
                    last = A(dst[:].unsqueeze(1), src, ACT.Copy)
                last.then_inc(ready, 1)

            def exps(n, n_keys, masked, sink):
                m.add("max")
                act.wait_ge(max_ready, m.at("max"))
                if sink is not None:
                    A(ES[:, n % 2:n % 2 + 1], sink, ACT.Exp, bias=MX[:, 2 + n % 2:3 + n % 2])
                src = PB[:, n % 2, 0:n_keys] if masked else FLAT[:, 2 * (n % 2) * T:2 * (n % 2) * T + n_keys]
                A(PB[:, n % 2, 0:n_keys], src, ACT.Exp, bias=MX[:, 2 + n % 2:3 + n % 2], scale=HD ** -0.5,
                  accum_out=DEN[:, n % 2:n % 2 + 1]).then_inc(exp_done, 1)

            def transposed_high(par, q, n_keys):
                m.add("pt")
                act.wait_ge(pt_done, m.at("pt"))
                A(PTH[:, par, 0:n_keys // P, q, :], FLAT[:, 4 * T:4 * T + n_keys].rearrange("p (b n) -> p b n", n=P), ACT.Copy).then_inc(pts_ready, 1)

            def heads(full, masked, block, following, sink=None):
                nq = 6 if full else 4

                def n_keys(n):
                    return TA if n % nq < 4 else TC

                def scale(n):
                    m.add("r")
                    act.wait_ge(r_ready, m.at("r"))
                    A(PB[:, n % 2, 0:n_keys(n)], PB[:, n % 2, 0:n_keys(n)], ACT.Identity, scale=MX[:, 4 + n % 2:5 + n % 2]).then_inc(scaled, 1)

                def output(i):
                    m.add("o")
                    act.wait_ge(o_done, m.at("o"))
                    half, c = i // (nq // 2), i % (nq // 2) * 2 * P
                    rows = slice(half * HD, half * HD + HD)
                    A(H2HI[rows, block, c:c + 2 * P], PS[rows, 6 + i % 2:7 + i % 2, 0:2 * P], ACT.Copy).then_inc(hi_ready, 1)

                last = 2 * nq - 1
                exps(0, n_keys(0), masked, sink and sink(0))
                scale(0)
                for n in range(last + 1):
                    if n < last:
                        exps(n + 1, n_keys(n + 1), masked, sink and sink((n + 1) // nq))
                    if n == last - 1:
                        high_parts(following, qk_high)
                    transposed_high(n // 2 % 2, n % 2, n_keys(n))
                    if n < last:
                        scale(n + 1)
                    if n % 2 and n >= 3:
                        output((n - 3) // 2)
                output(nq - 1)

            def heads_diff(block, following):
                def n_keys(qb):
                    return TA if qb < 4 else TC

                def output(i):
                    m.add("o")
                    act.wait_ge(o_done, m.at("o"))
                    A(OF[:, 2 * i * P:2 * (i + 1) * P], PS[:, 6 + i % 2, 0:2 * P], ACT.Copy)
                    A(OSQ[:, 2 * i * P:2 * (i + 1) * P], PS[:, 6 + i % 2, 0:2 * P], ACT.Square).then_inc(of_taken, 1)

                for n in range(2):
                    exps(n, TA, False, None)
                for qb in range(6):
                    m.add("r")
                    act.wait_ge(r_ready, m.at("r"))
                    A(COMB[:, qb % 2, 0:n_keys(qb)], PB[:, 0, 0:n_keys(qb)], ACT.Identity, scale=MX[:, 4:5]).then_inc(scaled, 1)
                    m.add("comb")
                    if qb < 5:
                        act.wait_ge(combined, m.at("comb"))
                        for n in (2 * qb + 2, 2 * qb + 3):
                            exps(n, n_keys(qb + 1), False, None)
                    if qb == 4:
                        high_parts(following, qk_high)
                    if qb % 2 == 0 and qb:
                        output(qb // 2 - 1)
                    transposed_high(0, qb % 2, n_keys(qb))
                output(2)
                m.add("stat")
                act.wait_ge(stat_done, m.at("stat"))
                A(OSQ[:], FLAT[:, 4 * T:4 * T + TA], ACT.Sqrt, bias=COL[:, 0:1], scale=1.0 / P).then_inc(root_ready, 1)
                m.add("val")
                act.wait_ge(val_ready, m.at("val"))
                A(H2HI[:, block, :], OF[:].unsqueeze(1), ACT.Copy).then_inc(hi_ready, 1)

            def second_qk(j):
                return (SECOND["qh"], U2[:, bass.ds(j + 6, 1), :]), (SECOND["kh"], U2[:, bass.ds(j + 10, 1), :])

            def first_heads(full, masked, sink=None):
                m.add("roped")
                act.wait_ge(roped, m.at("roped", DEPTH * 2 * QKV))
                high_parts(((FIRST["qh"], U2[:, 0:1, :]), (FIRST["kh"], U2[:, 4:5, :])), qk_high)
                high_parts(((FIRST["vh"], U2[:, 5:6, :]),), v_high)
                n = 12 if full else 8
                with m.loop(act, 4, max=n, r=n, pt=n, o=n // 2) as j:
                    heads(full, masked, bass.ds(j, 1), ((FIRST["qh"], U2[:, bass.ds(j + 1, 1), :]),), sink)

            def v_to_tokens(chunks_):
                for c in chunks_:
                    m.add("vt")
                    act.wait_ge(vt_done, m.at("vt"))
                    A(U2[:, c, :], FLAT[:, 0:TA], ACT.Copy).then_inc(vt_ready, 1)

            for l in range(DEPTH):
                full = l == 0
                if l == 0:
                    squares_x(True, False)
                else:
                    squares_x(True, True)
                root(TA)
                norm_high2(l, 0, True)
                act.dma_start(C2[:], rope2[:, 0:T]).then_inc(in2, 16)
                act.dma_start(S2[:], rope2[:, T:2 * T]).then_inc(in2, 16)
                if l:
                    act.dma_start(BAND[:], band[:, 0:BW]).then_inc(in2, 16)
                    act.dma_start(CMASK[:], band[:, BW:BW + HD]).then_inc(in2, 16)
                with m.loop(act, IN2 // 2, units=2, use0=1, use1=1) as i:
                    take2(U2[:, bass.ds(2 * i, 1), :], True)
                    take2(U2[:, bass.ds(2 * i + 1, 1), :], True)
                if l == 0:
                    with m.loop(act, 5, stat=1, rr=1) as c:
                        act.wait_ge(root_row, m.at("rr", 1))
                        m.add("rr")
                        A(SQ[:, 0:1, :], U2[:, bass.ds(c, 1), :], ACT.Square).then_inc(hsq_ready, 1)
                        m.add("stat")
                        act.wait_ge(stat_done, m.at("stat"))
                        A(RS[:], FLAT[:, 6 * T:6 * T + TA], ACT.Sqrt, bias=COL[:, 0:1], scale=1.0 / HD).then_inc(root_ready, 1)
                    v_to_tokens([5] + list(range(14, 18)))
                    first_heads(True, False)
                    high_parts(second_qk(0), qk_high)
                    with m.loop(act, 4, max=12, r=6, comb=6, pt=6, o=3, stat=1, val=1) as j:
                        high_parts(((SECOND["vh"], U2[:, bass.ds(j + 14, 1), :]),), v_high)
                        heads_diff(bass.ds(j + 4, 1), second_qk(j + 1))
                else:
                    act.wait_ge(rows_in, 16)
                    v_to_tokens([5] + list(range(14, 18)))
                    first_heads(False, True, lambda half: SK[:, half:half + 1])
                    high_parts(second_qk(0), qk_high)
                    with m.loop(act, 4, max=8, r=8, pt=8, o=4, bias=1) as j:
                        act.wait_ge(bias_used, m.at("bias", 1))
                        m.add("bias")
                        for h in range(2):
                            for half in range(2):
                                act.dma_start(BIAS[half * HD:(half + 1) * HD, h, :].rearrange("p (d c) -> p d c", c=HD),
                                              skewed(half)[bass.ds(2 * j + h, 1), :, :, :].rearrange("h q d c -> (h q) d c")).then_inc(bias_in, 16)
                        high_parts(((SECOND["vh"], U2[:, bass.ds(j + 14, 1), :]),), v_high)
                        heads(False, True, bass.ds(j + 4, 1), second_qk(j + 1))

                def of_y2(k, dst, n):
                    p = unit_wait()
                    m.add(f"use{p}")
                    A(Y2[:, k, 0:n], FLAT[:, 3 * p * T:3 * p * T + n], ACT.Copy)
                    A(dst[:, 0:n], FLAT[:, 3 * p * T:3 * p * T + n], ACT.Square).then_inc(taken[p], 1)

                n2 = TA if full else T
                squares(of_y2, n2)
                root(n2)
                squares_x(full, True)
                root(n2)
                norm_high2(l, 3, full)
                with m.loop(act, QUARTERS, units=2 * KB, use0=KB, use1=KB, val=KB):
                    with m.loop(act, KB // 2, units=2, use0=1, use1=1, val=2) as i:
                        for p in range(2):
                            unit_wait()
                            m.add(f"use{p}")
                            A(TMP[:, p, 0:n2], FLAT[:, 3 * p * T:3 * p * T + n2], ACT.Relu).then_inc(relu_ready, 1)
                            m.add("val")
                            act.wait_ge(val_ready, m.at("val"))
                            A(GHI[:, bass.ds(2 * i + p, 1), 0:n2], TMP[:, p:p + 1, 0:n2], ACT.Copy).then_inc(hi_ready, 1)
                    m.add("units", KB)
                    m.add("use0", KB // 2)
                    m.add("use1", KB // 2)

                def of_y3(k, dst, n):
                    if k == 0:
                        m.add("y", 1)
                        act.wait_ge(y_ready, m.at("y"))
                    A(dst[:, 0:n], Y2[:, k, 0:n], ACT.Square).then_inc(sq_ready, 1)

                squares(of_y3, n2)
                root(n2)

        @block.vector
        def _(dve):
            m = Marks(*MARKS)
            TT = nc.vector.tensor_tensor
            def TTR(out, in0, in1, scale, init, op0, op1, accum):
                nc.vector.tensor_tensor_reduce(out=out, in0=in0, in1=in1, scale=scale, scalar=init, op0=op0, op1=op1, accum_out=accum)
            TS = nc.vector.tensor_scalar
            STT = nc.vector.scalar_tensor_tensor

            def par(c):
                return PL[:, c:c + 1]

            def add_squares(k, n, arrived):
                if k == 0:
                    return
                if k > 1:
                    dve.drain()
                arrived(k)
                if k == 1:
                    TT(ACC[:, 0:n], SQ[:, 0, 0:n], SQ[:, 1, 0:n], ALU.add).then_inc(sq_taken, 1)
                else:
                    TT(ACC[:, 0:n], ACC[:, 0:n], SQ[:, k % 2, 0:n], ALU.add).then_inc(sq_taken, 1)

            def sq_arrived(k):
                m.add("sq", 2 if k == 1 else 1)
                dve.wait_ge(sq_ready, m.at("sq"))

            def y_arrived(k):
                for j in ((0, 1) if k == 1 else (k,)):
                    m.add(f"use{j % 2}")
                for p in range(2) if k == 1 else (k % 2,):
                    dve.wait_ge(taken[p], m.at(f"use{p}", 1))

            def root_inverse(n):
                m.add("root")
                dve.wait_ge(root_ready, m.at("root"))
                nc.vector.reciprocal(RS[:, 0:n], RS[:, 0:n])
                dve.drain()

            def low(dst, src, hi):
                m.add("hi")
                dve.wait_ge(hi_ready, m.at("hi"))
                TT(dst, src, hi.bitcast(F32), ALU.subtract).then_inc(lo_ready, 1)

            def norm_apply(gain):
                for k in range(KB + 1):
                    if k < KB:
                        dve.drain()
                        STT(TMP[:, k % 2, 0:T], X[:, k, :], par(gain + k), RS[:, 0:T], ALU.mult, ALU.mult).then_inc(val_ready, 1)
                    if k:
                        low(HLO[:, k - 1, :], TMP[:, (k - 1) % 2, 0:T], HHI[:, k - 1, :])

            def residual(gain):
                for k in range(KB + 1):
                    if k < KB:
                        STT(TMP[:, k % 2, 0:T], Y[:, k, :], par(gain + k), RS[:, 0:T], ALU.mult, ALU.mult)
                        dve.drain()
                        TT(X[:, k, :], X[:, k, :], TMP[:, k % 2, 0:T], ALU.add).then_inc(x_ready, 1)
                    if k >= 1:
                        add_squares(k - 1, T, sq_arrived)

            def attention(count, keys, maximum, scale, dv, dst):
                def outputs(n):
                    m.add("o")
                    dve.wait_ge(o_done, m.at("o"))
                    nc.vector.reciprocal(MX[:, 4 + n % 2:5 + n % 2], DEN[:, n % 2:n % 2 + 1])
                    dve.drain()
                    TS(dst(n), PS[:, 6 + n % 2, 0:dv], MX[:, 4 + n % 2:5 + n % 2], None, ALU.mult).then_inc(o_taken, 1)

                for n in range(count):
                    m.add("s")
                    dve.wait_ge(s_done, m.at("s"))
                    dve.sem_inc(passed, 1)
                    maximum(n)
                    dve.drain()
                    TS(MX[:, 2 + n % 2:3 + n % 2], MX[:, 1:2], -scale, None, ALU.mult).then_inc(max_ready, 1)
                    dve.drain()
                    if n:
                        outputs(n - 1)
                outputs(count - 1)

            MJ = TMP[:].rearrange("p b n -> p (b n)")[:, 0:D]
            nc.vector.memset(MX[:], 0.0).then_inc(taken[0], 1)
            nc.vector.memset(DEN[:], 0.0).then_inc(taken[1], 1)
            dve.wait_ge(consts_in, 16 * 10)
            POS, ANG, TURN = COS[:], PU[:, 0, 0:T], PU[:, 1, 0:T]
            nc.vector.tensor_copy(POS, SIN[:].bitcast(I32))
            dve.drain()
            TS(ANG, POS, COL[:, 1:2], None, ALU.mult)
            dve.drain()
            TS(TURN, ANG, 1.0 / TWO_PI, MAGIC, ALU.mult, ALU.add)
            dve.drain()
            TS(TURN, TURN, -MAGIC, None, ALU.add)
            dve.drain()
            for part in TURN_PARTS:
                STT(ANG, TURN, -part, ANG, ALU.mult, ALU.add)
                dve.drain()
            TS(SIN[:], ANG, PI_IN, -PI_IN, ALU.min, ALU.max).then_inc(ang_ready, 1)
            dve.wait_ge(sin_ready, 2)
            TS(SIN[:], COS[:], COL[:, 2:3], None, ALU.mult)
            TT(RT[:], RT[:], RT[:], ALU.mult)
            dve.drain()
            TS(COS[:], RT[:], -2.0, 1.0, ALU.mult, ALU.add).then_inc(tables_ready, 1)
            dve.drain()
            for k in range(KB):
                add_squares(k, TC, sq_arrived)
            m.add("root")
            dve.wait_ge(root_ready, m.at("root"))
            nc.vector.reciprocal(MR[:], RS[:, 0:TC])
            dve.drain()
            for k in range(KB):
                add_squares(k, T, sq_arrived)
            root_inverse(T)
            m.add("layer")
            with m.loop(dve, DEPTH, **LAYER["dve"]):
                nc.vector.tensor_copy(PL[:], PAR[:, bass.ds(m.at("layer", -1), 1), :]).then_inc(layer_ready, 1)
                m.add("layer")
                dve.drain()
                norm_apply(G_MIX)
                use = {0: m.n["use0"], 1: m.n["use1"]}

                def chunk_in(c):
                    m.n[f"use{c % 2}"] = use[c % 2] + c // 2 + 1
                    dve.wait_ge(taken[c % 2], m.at(f"use{c % 2}", 1))

                dve.drain()
                nc.vector.memset(PU[:, :, 0:16], 0.0)
                nc.vector.memset(CB[:, :, 0:2], 0.0)
                for c in range(POOL):
                    chunk_in(c)
                    nc.vector.tensor_copy(PU[:, 0, 16:], U[:, c, :])
                    dve.drain()
                    for w in range(c + 2):
                        s = 1 << w
                        TT(PU[:, w + 1, 16:], PU[:, w, 16:], PU[:, w, 16 - s:16 - s + T], ALU.add)
                        dve.drain()
                    edge = (96, 64, 32)[c]
                    rows = ((slice(0, 96), c + 1), (slice(96, P), c + 2)) if edge == 96 else \
                        ((slice(0, 64), c + 1), (slice(64, P), c + 2)) if edge == 64 else \
                        ((slice(0, P), c + 2), (slice(0, 32), c + 1))
                    for r, w in rows:
                        STT(U[r, c, :], PU[r, w, 16:], COL[r, 4 + c:5 + c], PU[r, 0, 16:], ALU.mult, ALU.subtract)
                        dve.drain()
                        TT(PU[r, w, 16:32], PU[r, w, 16:32], INV16[r, c, :], ALU.mult)
                        dve.drain()
                        TT(U[r, c, 0:16], PU[r, w, 16:32], PU[r, 0, 16:32], ALU.subtract)
                        dve.drain()
                    dve.drain().then_inc(pooled, 1)
                for c in range(POOL):
                    chunk_in(C_BC + c)
                    TT(CB[:, 0, 2:], U[:, C_BC + c, :], U[:, C_BX + c, :], ALU.mult)
                    dve.drain()
                    TS(CB[:, 1, 2:], CB[:, 0, 2:], par(C_CONVB + 2 * POOL + c), None, ALU.mult)
                    for tap in (1, 0):
                        dve.drain()
                        STT(CB[:, 1, 2:], CB[:, 0, tap:tap + T], par(C_CONVB + tap * POOL + c), CB[:, 1, 2:], ALU.mult, ALU.add)
                    dve.drain()
                    TT(U[:, C_BX + c, :], CB[:, 1, 2:], U[:, C_BB + c, :], ALU.mult).then_inc(val_ready, 1)
                    dve.drain()
                swap = [(i + 8) % 16 for i in range(16)] + list(range(16, 32))
                for c in range(2 * QKV):
                    chunk_in(C_Q + c)
                    dve.sem_inc(passed, 1)
                    u = U[:, C_Q + c, :]
                    nc.vector.stream_shuffle(RT[:], u, swap)
                    dve.drain()
                    TT(RT[:], RT[:], SIN[:], ALU.mult)
                    TT(u, u, COS[:], ALU.mult)
                    dve.drain()
                    TT(u, u, RT[:], ALU.add).then_inc(roped, 1)
                    dve.drain()
                for p in range(2):
                    m.n[f"use{p}"] = use[p] + MIX_IN // 2
                m.add("units", MIX_IN)
                for c in range(POOL):
                    low(BLO[:, POOL + c, :], U[:, C_BX + c, :], BHI[:, POOL + c, :])
                for c in range(POOL):
                    m.add("hi")
                    dve.wait_ge(hi_ready, m.at("hi"))
                    STT(BLO[:, c, :], bank(c), par(C_SCALE + c), BHI[:, c, :].bitcast(F32), ALU.mult, ALU.subtract).then_inc(lo_ready, 1)

                def maximum(n):
                    r = n // 2 % 4
                    c0 = 2 * (n % 2) * T
                    TTR(PB[:, n % 2, 0:T], FLAT[:, c0:c0 + T], MASK0[:, 3 - r:3 - r + T], 1.0, NEG, ALU.add, ALU.max, MX[:, 0:1])
                    dve.drain()
                    TTR(PB[:, n % 2, T:TA], FLAT[:, c0 + T:c0 + TA], MASK12[:], 1.0, MX[:, 0:1], ALU.add, ALU.max, MX[:, 1:2])

                attention(16, 6, maximum, HD ** -0.5, HD,
                          lambda n: OTOK[:, n // 2 % 4, (n // 8) * P + n % 2 * HD:(n // 8) * P + n % 2 * HD + HD])
                for jj in range(2):
                    low(BLO[:, 2 * POOL + jj, :].rearrange("p (i r) -> p r i", r=4), bank(jj).rearrange("p (r i) -> p r i", r=4),
                        BHI[:, 2 * POOL + jj, :].rearrange("p (i r) -> p r i", r=4))
                m.add("mem", 16)
                dve.wait_ge(mem_in, m.at("mem", 16))
                for k in range(KB):
                    STT(MEM[:, k, :], MEM[:, k, :], par(G_KV + k), MR[:], ALU.mult, ALU.mult).then_inc(val_ready, 1)
                for k in range(KB):
                    m.add("hi")
                    dve.wait_ge(hi_ready, m.at("hi"))
                    TT(NLO[:, k, :], MEM[:, k, :], NHI[:, k, :].bitcast(F32), ALU.subtract).then_inc(mem_ready, 1)
                with m.loop(dve, KB, use0=2, use1=2, units=4, hi=1) as i:
                    m.add("use0", 2)
                    m.add("use1")
                    dve.wait_ge(taken[0], m.at("use0", 1))
                    dve.wait_ge(taken[1], m.at("use1", 1))
                    m.add("units", 4)
                    dve.wait_ge(units_done, m.at("units"))
                    TT(MT[:, 0, :], bank(3), GATE[:, 0, :], ALU.mult)
                    TT(MT[:, 1, :], bank(4), GATE[:, 1, :], ALU.mult)
                    dve.drain()
                    TT(MT[:, 0, :], MT[:, 0, :], MT[:, 1, :], ALU.add)
                    dve.drain()
                    TT(MT[:, 1, :], bank(5), GATE[:, 2, :], ALU.mult).then_inc(taken[1], 1)
                    m.add("use1")
                    dve.drain()
                    TT(MT[:, 0, :], MT[:, 0, :], MT[:, 1, :], ALU.add).then_inc(merge_done, 1)
                    low(MLO[:, bass.ds(i, 1), :], MT[:, 0:1, :], MHI[:, bass.ds(i, 1), :])
                    dve.drain()
                def post(gain, next_gain):
                    root_inverse(T)
                    residual(gain)
                    root_inverse(T)
                    if next_gain is not None:
                        norm_apply(next_gain)

                def y_squares():
                    for k in range(KB):
                        add_squares(k, T, y_arrived)

                y_squares()
                root_inverse(T)
                residual(G_MIXP)
                m.add("use0", 4)
                m.add("use1", 4)
                m.add("units", KB + KB)
                root_inverse(T)
                norm_apply(G_MEM)
                m.add("use0", 2)
                m.add("use1", 2)
                m.add("units", HEADS)

                def maximum_m(n):
                    c0 = 2 * (n % 2) * T
                    nc.vector.reduce_max(MX[:, 1:2], FLAT[:, c0:c0 + TC], AX.X)

                attention(16, 2, maximum_m, P ** -0.5, P, lambda n: OM[:, n % 4, (n // 4) * P:(n // 4 + 1) * P])
                for hh in range(HEADS):
                    low(OMLO[:, hh, :], bank(hh), OMHI[:, hh, :])

                def mo_arrived(k):
                    if k == 1:
                        m.add("sq")
                        dve.wait_ge(sq_ready, m.at("sq"))
                    if k % 2:
                        m.add(f"use{k // 2 % 2}")
                        dve.wait_ge(taken[k // 2 % 2], m.at(f"use{k // 2 % 2}", 1))
                    else:
                        m.add("sq")
                        dve.wait_ge(sq_ready, m.at("sq"))

                for k in range(KB):
                    add_squares(k, T, mo_arrived)
                m.add("units", HEADS)
                post(G_MEMP, G_FFN)
                dve.drain()
                nc.vector.memset(UA[:, 0, 0:8], 0.0)
                with m.loop(dve, FF, use0=1, use1=1, units=2, silu=1, hi=1) as i:
                    m.add("use0")
                    dve.wait_ge(taken[0], m.at("use0", 1))
                    TS(FC[:, 0, :], UA[:, 0, 8:8 + T], PL[:, bass.ds(i + C_CONVF + 2 * FF, 1)], None, ALU.mult)
                    dve.drain()
                    STT(FC[:, 0, :], UA[:, 0, 7:7 + T], PL[:, bass.ds(i + C_CONVF + FF, 1)], FC[:, 0, :], ALU.mult, ALU.add)
                    dve.drain()
                    STT(FC[:, 0, :], UA[:, 0, 6:6 + T], PL[:, bass.ds(i + C_CONVF, 1)], FC[:, 0, :], ALU.mult, ALU.add).then_inc(conv_ready, 1)
                    m.add("silu")
                    dve.wait_ge(silu_ready, m.at("silu"))
                    m.add("units", 2)
                    dve.wait_ge(units_done, m.at("units"))
                    TT(FT[:, 0, :], FC[:, 0, :], bank(3), ALU.mult).then_inc(taken[1], 1)
                    m.add("use1")
                    low(FLO[:, bass.ds(i, 1), :], FT[:, 0:1, :], FHI[:, bass.ds(i, 1), :])
                    dve.drain()
                m.add("units", DOWN_UNITS * KB)
                m.add("crow")
                dve.wait_ge(crow_ready, m.at("crow"))
                for k in range(KB):
                    for u in range(k * MOD_CHUNK, (k + 1) * MOD_CHUNK):
                        if u % 4 == 0:
                            m.add("modw")
                        dve.wait_ge(modw_in[u % 4], m.at("modw") * 16)
                        dve.sem_inc(passed, 1)
                        TTR(MJ, MODW[u % 4][:], CROW[:, 0, :], 1.0, 0.0, ALU.mult, ALU.add, MODL[:, u, 0:1])
                        dve.drain()
                        TTR(MJ, MODW[u % 4][:], CROW[:, 1, :], 1.0, 0.0, ALU.mult, ALU.add, MODL[:, u, 1:2])
                        dve.drain().then_inc(mod_used, 1)
                    add_squares(k, T, y_arrived)
                nc.vector.tensor_copy(MOD[:, bass.ds(m.at("layer", -2) * MOD_LAYER, MOD_LAYER), :], MODL[:])
                post(G_FFNP, None)

            dve.drain()
            dve.wait_ge(in2, 48)
            for p in range(2):
                TTR(RT2[:, 0:HD], SM[:, 2 * p * HD:(2 * p + 1) * HD], SM[:, (2 * p + 1) * HD:(2 * p + 2) * HD], 1.0, 0.0, ALU.mult, ALU.add, LM[:, p:p + 1])
                dve.drain()
            TS(SINK8[:], SM[:, 4 * HD:4 * HD + 8], HD ** 0.5, None, ALU.mult)
            TS(QKG[:, 2:3], QKG[:, 2:3], 1.0 - LAMBDA0, None, ALU.mult)
            nc.vector.memset(ZERO[:], 0.0)
            dve.drain().then_inc(lam_ready, 1)
            dve.wait_ge(lam_ready, 2)
            TT(LM[:, 4:5], LM[:, 3:4], LM[:, 2:3], ALU.subtract)
            dve.drain()
            TS(LM[:, 4:5], LM[:, 4:5], -LAMBDA0, None, ALU.add)
            nc.vector.memset(DEN[:], 0.0).then_inc(mod_taken, 1)
            TT(MOD[:, 0:MOD_DVE, :], MOD[:, 0:MOD_DVE, :], BMOD[:, 0:MOD_DVE].unsqueeze(2).to_broadcast([P, MOD_DVE, 2]), ALU.add)
            dve.drain()

            def with_gains(l):
                for part, g, shift in ((1, 0, 1.0), (2, 1, 0.0), (4, 2, 1.0), (5, 3, 0.0)):
                    mod = MOD[:, l * MODS + part * KB:l * MODS + (part + 1) * KB, :]
                    STT(mod, mod, shift, NG[:, l, g, :].unsqueeze(2).to_broadcast([P, KB, 2]), ALU.add, ALU.mult)
                dve.drain()

            with_gains(0)

            def mod_rows(i):
                m.add("modd")
                dve.wait_ge(mod_done, m.at("modd"))
                c = slice(MOD_DVE + i * KB, MOD_DVE + (i + 1) * KB)
                TT(MOD[:, c, :], PS[:, 5, 0:2 * KB].rearrange("p (k v) -> p k v", v=2), BMOD[:, c].unsqueeze(2).to_broadcast([P, KB, 2]),
                   ALU.add).then_inc(mod_taken, 1)
                dve.drain()

            def spans(full):
                return ((0, slice(0, T)), (1, slice(T, TA)))[:2 if full else 1]

            def xpart(v):
                return CTX if v else X

            def norm_apply2(l, part, full):
                for k in range(KB + 1):
                    if k < KB:
                        dve.drain()
                        for v, c in spans(full):
                            last = STT(TMP[:, k % 2, c], xpart(v)[:, k, :], MOD[:, l * MODS + (part + 1) * KB + k, v:v + 1], RS[:, c], ALU.mult, ALU.mult)
                        last.then_inc(val_ready, 1)
                    if k:
                        m.add("hi")
                        dve.wait_ge(hi_ready, m.at("hi"))
                        for v, c in spans(full):
                            last = STT(H2LO[:, k - 1, c], TMP[:, (k - 1) % 2, c], MOD[:, l * MODS + part * KB + k - 1, v:v + 1],
                                       H2HI[:, k - 1, c].bitcast(F32), ALU.add, ALU.subtract)
                        last.then_inc(lo_ready, 1)

            def residual2(l, part, full, stats=True):
                for k in range(KB + 1):
                    if k < KB:
                        for v, c in spans(full):
                            STT(TMP[:, k % 2, c], Y2[:, k, c], MOD[:, l * MODS + part * KB + k, v:v + 1], RS[:, c], ALU.mult, ALU.mult)
                        dve.drain()
                        for v, c in spans(full):
                            last = TT(xpart(v)[:, k, :], xpart(v)[:, k, :], TMP[:, k % 2, c], ALU.add)
                        last.then_inc(x_ready, 1)
                    if k and stats:
                        add_squares(k - 1, TA if full else T, sq_arrived)
                    else:
                        dve.drain()

            m.add("exp", DEPTH * 32)
            m.add("pts", DEPTH * 32)

            def turn(c):
                u = U2[:, c, 0:T]
                dve.sem_inc(passed, 1)
                nc.vector.stream_shuffle(RT2[:], u, [(i + 16) % 32 for i in range(32)])
                dve.drain()
                TT(RT2[:], RT2[:], S2[:], ALU.mult)
                TT(u, u, C2[:], ALU.mult)
                dve.drain()
                TT(u, u, RT2[:], ALU.add)
                dve.drain()

            def low_parts(parts, mark, highs, staged):
                m.add(mark)
                dve.wait_ge(highs, m.at(mark))
                for dst, src, hi in parts:
                    last = TT(dst[:].unsqueeze(1), src, hi[:].bitcast(F32).unsqueeze(1), ALU.subtract)
                last.then_inc(staged, 1)

            def negative_max(n, n_keys, bias=None, sink=None):
                c0 = 2 * (n % 2) * T
                m.add("s")
                dve.wait_ge(s_done, m.at("s"))
                if bias is None:
                    nc.vector.reduce_max(MX[:, 1:2], FLAT[:, c0:c0 + n_keys], AX.X)
                else:
                    dve.sem_inc(passed, 1)
                    TTR(PB[:, n % 2, 0:T], FLAT[:, c0:c0 + T], bias, 1.0, NEG, ALU.add, ALU.max, MX[:, 0:1])
                    dve.drain()
                    TTR(PB[:, n % 2, T:TA], FLAT[:, c0 + T:c0 + TA], ZERO[:], 1.0, MX[:, 0:1], ALU.add, ALU.max, MX[:, 1:2])
                dve.drain()
                if sink is not None:
                    TT(MX[:, 1:2], MX[:, 1:2], sink, ALU.max)
                    dve.drain()
                TS(MX[:, 2 + n % 2:3 + n % 2], MX[:, 1:2], -HD ** -0.5, None, ALU.mult).then_inc(max_ready, 1)
                dve.drain()

            def transposed_low(bufs, par, q, n_keys):
                m.add("pts")
                dve.wait_ge(pts_ready, m.at("pts"))
                b = n_keys // P
                TT(bufs["ptl"][:, par, 0:b, q, :], FLAT[:, 4 * T:4 * T + n_keys].rearrange("p (b n) -> p b n", n=P),
                   PTH[:, par, 0:b, q, :].bitcast(F32), ALU.subtract).then_inc(ptl_ready, 1)

            def heads(bufs, full, block, following, bias=None, sink=None, after_scores=None):
                nq = 6 if full else 4

                def n_keys(n):
                    return TA if n % nq < 4 else TC

                def maximum(n):
                    half, qb = n // nq, n % nq
                    negative_max(n, n_keys(n), bias and bias(half, qb), sink and sink(half))

                def inverse(n):
                    m.add("exp")
                    dve.wait_ge(exp_done, m.at("exp"))
                    d = DEN[:, n % 2:n % 2 + 1]
                    if sink is not None:
                        TT(d, d, ES[:, n % 2:n % 2 + 1], ALU.add)
                        dve.drain()
                    nc.vector.reciprocal(MX[:, 4 + n % 2:5 + n % 2], d).then_inc(r_ready, 1)

                def output(i):
                    m.add("hi")
                    dve.wait_ge(hi_ready, m.at("hi"))
                    half, c = i // (nq // 2), i % (nq // 2) * 2 * P
                    rows = slice(half * HD, half * HD + HD)
                    TT(H2LO[rows, block, c:c + 2 * P], PS[rows, 6 + i % 2:7 + i % 2, 0:2 * P], H2HI[rows, block, c:c + 2 * P].bitcast(F32),
                       ALU.subtract).then_inc(lo_ready, 1)

                last = 2 * nq - 1
                maximum(0)
                maximum(1)
                inverse(0)
                for n in range(last + 1):
                    if n < last:
                        inverse(n + 1)
                    if n == last - 1:
                        low_parts(following, "qkh", qk_high, qk_staged)
                    transposed_low(bufs, n // 2 % 2, n % 2, n_keys(n))
                    if n + 2 <= last:
                        maximum(n + 2)
                        if n + 2 == last and after_scores is not None:
                            dve.drain().then_inc(after_scores, 1)
                    if n % 2 and n >= 3:
                        output((n - 3) // 2)
                output(nq - 1)
                dve.drain()

            def heads_diff(block, following):
                def n_keys(qb):
                    return TA if qb < 4 else TC

                for n in range(2):
                    negative_max(n, TA)
                for qb in range(6):
                    m.add("exp", 2)
                    dve.wait_ge(exp_done, m.at("exp"))
                    nc.vector.reciprocal(MX[:, 4:6], DEN[:])
                    dve.drain()
                    TS(MX[:, 5:6], MX[:, 5:6], LM[:, 4:5], None, ALU.mult).then_inc(r_ready, 1)
                    dve.drain()
                    if qb < 5:
                        negative_max(2 * qb + 2, n_keys(qb + 1))
                    m.add("sc")
                    dve.wait_ge(scaled, m.at("sc"))
                    c = COMB[:, qb % 2, 0:n_keys(qb)]
                    STT(c, PB[:, 1, 0:n_keys(qb)], MX[:, 5:6], c, ALU.mult, ALU.add).then_inc(combined, 1)
                    if qb < 5:
                        negative_max(2 * qb + 3, n_keys(qb + 1))
                    else:
                        low_parts(following, "qkh", qk_high, qk_staged)
                    transposed_low(SECOND, 0, qb % 2, n_keys(qb))
                m.add("root")
                dve.wait_ge(root_ready, m.at("root"))
                nc.vector.reciprocal(OSQ[:], OSQ[:])
                dve.drain()
                STT(OF[:], OF[:], QKG[:, 2:3], OSQ[:], ALU.mult, ALU.mult).then_inc(val_ready, 1)
                m.add("hi")
                dve.wait_ge(hi_ready, m.at("hi"))
                TT(H2LO[:, block, :], OF[:].unsqueeze(1), H2HI[:, block, :].bitcast(F32), ALU.subtract).then_inc(lo_ready, 1)
                dve.drain()

            def second_qk(j):
                return ((SECOND["ql"], U2[:, bass.ds(j + 6, 1), :], SECOND["qh"]), (SECOND["kl"], U2[:, bass.ds(j + 10, 1), :], SECOND["kh"]))

            def second_v(j):
                low_parts(((SECOND["vl"], U2[:, bass.ds(j + 14, 1), :], SECOND["vh"]),), "vh", v_high, v_staged)

            def first_qkv():
                low_parts(((FIRST["ql"], U2[:, 0:1, :], FIRST["qh"]), (FIRST["kl"], U2[:, 4:5, :], FIRST["kh"])), "qkh", qk_high, qk_staged)
                low_parts(((FIRST["vl"], U2[:, 5:6, :], FIRST["vh"]),), "vh", v_high, v_staged)

            def first_q(j):
                return ((FIRST["ql"], U2[:, bass.ds(j + 1, 1), :], FIRST["qh"]),)

            for l in range(DEPTH):
                full = l == 0
                n2 = TA if full else T
                if l == 0:
                    for k in range(KB):
                        add_squares(k, TA, sq_arrived)
                    mod_rows(0)
                root_inverse(TA)
                norm_apply2(l, 0, True)
                if l == 0:
                    mod_rows(1)
                    with_gains(1)
                m.add("in2", 64 if l else 32)
                dve.wait_ge(in2, m.at("in2", 48))
                use = {0: m.n["use0"], 1: m.n["use1"]}
                for c in range(5) if l else range(6, 14):
                    m.n[f"use{c % 2}"] = use[c % 2] + c // 2 + 1
                    dve.wait_ge(taken[c % 2], m.at(f"use{c % 2}", 1))
                    turn(c)
                for p in range(2):
                    m.n[f"use{p}"] = use[p] + IN2 // 2
                    dve.wait_ge(taken[p], m.at(f"use{p}", 1))
                m.add("units", IN2)
                if l == 0:
                    nc.vector.memset(MX[:, 6:7], 0.0).then_inc(root_row, 1)
                    with m.loop(dve, 5, root=1) as c:
                        m.add("root")
                        dve.wait_ge(root_ready, m.at("root"))
                        nc.vector.reciprocal(RS[:], RS[:])
                        dve.drain()
                        STT(U2[:, bass.ds(c, 1), :], U2[:, bass.ds(c, 1), :], PAR2[:, bass.ds(c + (2 * KB * 4 + MOD_UNITS + 3), 1)],
                            RS[:].unsqueeze(1), ALU.mult, ALU.mult).then_inc(root_row, 1)
                        dve.drain()
                    for c in range(5):
                        turn(c)
                    dve.drain().then_inc(roped, 1)
                    first_qkv()
                    with m.loop(dve, 4, qkh=1, s=12, exp=12, pts=12, hi=6) as j:
                        heads(FIRST, True, bass.ds(j, 1), first_q(j))
                    low_parts(second_qk(0), "qkh", qk_high, qk_staged)
                    m.add("sc", 4 * 12)
                    with m.loop(dve, 4, qkh=1, vh=1, s=12, exp=12, sc=6, pts=6, root=1, hi=1) as j:
                        second_v(j)
                        heads_diff(bass.ds(j + 4, 1), second_qk(j + 1))
                else:
                    dve.drain().then_inc(roped, 1)
                    first_qkv()
                    with m.loop(dve, 4, qkh=1, s=8, exp=8, pts=8, hi=4) as j:
                        for half in range(2):
                            nc.vector.tensor_copy(SK[:, half:half + 1], SM[:, bass.ds(j + (4 * HD + 4 * half), 1)])
                            nc.vector.tensor_copy(SK[:, 2 + half:3 + half], SINK8[:, bass.ds(j + 4 * half, 1)])
                        dve.drain()
                        heads(FIRST, False, bass.ds(j, 1), first_q(j), lambda half, qb: BAND[:, (3 - qb) * P:(3 - qb) * P + T],
                              lambda half: SK[:, 2 + half:3 + half])
                    low_parts(second_qk(0), "qkh", qk_high, qk_staged)
                    nc.vector.memset(MX[:, 6:7], 0.0).then_inc(bias_used, 1)
                    with m.loop(dve, 4, qkh=1, vh=1, s=8, exp=8, pts=8, hi=4, bias=64) as j:
                        second_v(j)
                        m.add("bias", 64)
                        dve.wait_ge(bias_in, m.at("bias"))
                        for h in range(2):
                            STT(BIAS[:, h, :].rearrange("p (d c) -> p d c", c=HD), BIAS[:, h, :].rearrange("p (d c) -> p d c", c=HD), HD ** 0.5,
                                CMASK[:].unsqueeze(1).to_broadcast([P, DR, HD]), ALU.mult, ALU.add)
                        dve.drain()
                        heads(SECOND, False, bass.ds(j + 4, 1), second_qk(j + 1),
                              lambda half, qb: BIAS[:, half, (6 - 2 * qb) * HD:(6 - 2 * qb) * HD + T], after_scores=bias_used)
                m.add("units", KB)
                for k in range(KB):
                    add_squares(k, n2, y_arrived)
                root_inverse(n2)
                residual2(l, 2, full)
                root_inverse(n2)
                norm_apply2(l, 3, full)
                dve.drain()
                nc.vector.memset(Y2[:], 0.0)
                dve.drain()
                with m.loop(dve, QUARTERS, units=2 * KB, use0=KB, use1=KB, relu=KB, hi=KB):
                    with m.loop(dve, KB // 2, units=2, use0=1, use1=1, relu=2, hi=2) as i:
                        for p in range(2):
                            m.add("units")
                            m.add(f"use{p}")
                            m.add("relu")
                            dve.wait_ge(relu_ready, m.at("relu"))
                            STT(TMP[:, p, 0:n2], FLAT[:, 3 * p * T:3 * p * T + n2], 0.0, TMP[:, p, 0:n2], ALU.max, ALU.mult).then_inc(taken[p], 1)
                            dve.drain().then_inc(val_ready, 1)
                            m.add("hi")
                            dve.wait_ge(hi_ready, m.at("hi"))
                            TT(GLO[:, bass.ds(2 * i + p, 1), 0:n2], TMP[:, p:p + 1, 0:n2], GHI[:, bass.ds(2 * i + p, 1), 0:n2].bitcast(F32),
                               ALU.subtract).then_inc(lo_ready, 1)
                            dve.drain()
                    with m.loop(dve, KB // 2, units=2, use0=1, use1=1) as i:
                        for p in range(2):
                            m.add("units")
                            m.add(f"use{p}")
                            dve.wait_ge(units_done, m.at("units"))
                            y = Y2[:, bass.ds(2 * i + p, 1), 0:n2]
                            TT(y, y, FLAT[:, 3 * p * T:3 * p * T + n2].unsqueeze(1), ALU.add).then_inc(taken[p], 1)
                    dve.drain()
                dve.drain().then_inc(y_ready, 1)
                for k in range(KB):
                    add_squares(k, n2, sq_arrived)
                root_inverse(n2)
                residual2(l, 5, full, stats=l == 0)


def kernel(**inputs):
    import numpy as np
    import concourse.bacc as bacc
    from concourse.bass_utils import run_bass_kernel_spmd

    a = {k: np.asarray(v) for k, v in inputs.items()}
    f4 = np.float32

    def chunks(w):
        k, n = w.shape
        return np.ascontiguousarray(w.reshape(k // P, P, n // P, P).transpose(2, 1, 0, 3))

    units = []
    for l in range(DEPTH):
        w_in = chunks(a["w_in"][l])
        units += [w_in[c] for c in range(MIX_IN)]
        branch = [chunks(a[n][l]) for n in ("w_branch_a", "w_branch_b", "w_branch_c")]
        for c in range(KB):
            units += [w_in[MIX_IN + g * KB + c] for g in range(3)]
            units.append(np.concatenate([w[c] for w in branch], axis=1))
        units += list(chunks(a["w_out"][l])) + list(chunks(a["w_mkv"][l])) + list(chunks(a["w_mq"][l]))
        mo = chunks(a["w_mo"][l])
        units += [np.concatenate([mo[2 * u], mo[2 * u + 1]], axis=1) for u in range(HEADS)]
        up = chunks(a["w_up"][l])
        for j in range(FF):
            units += [up[j], up[FF + j]]
        down = chunks(a["w_down"][l])
        pad = np.zeros((P, DOWN_UNITS * KB - FF, P), f4)
        for c in range(KB):
            padded = np.concatenate([down[c], pad], axis=1)
            units += [padded[:, u * KB:(u + 1) * KB] for u in range(DOWN_UNITS)]
    w_mod = np.concatenate([chunks(w) for w in a["w_mod_2"]])
    units += list(w_mod[MOD_DVE:])
    modw = w_mod[:MOD_DVE].transpose(0, 3, 2, 1).reshape(MOD_DVE, P, D)
    pairs = np.concatenate([np.r_[j * HD:(j + 1) * HD, (j + 4) * HD:(j + 5) * HD] for j in range(4)])
    order = np.r_[pairs, 4 * P:IN2 * P]
    rows = np.r_[pairs, 4 * P:KB * P]
    for l in range(DEPTH):
        units += list(chunks(a["w_in_2"][l][:, order])) + list(chunks(a["w_out_2"][l][rows]))
        up, down = chunks(a["w_mlp_in_2"][l]), chunks(a["w_mlp_out_2"][l])
        for q in range(QUARTERS):
            units += list(up[q * KB:(q + 1) * KB]) + list(down[:, :, q * KB:(q + 1) * KB])
    stream = np.stack(units).reshape(len(units), P, D)

    def feature_major(v):
        return np.ascontiguousarray(v.T.reshape(-1, P, v.shape[0]).transpose(1, 0, 2))

    def columns(v):
        return v.reshape(-1, P).T

    par = np.stack([np.concatenate([columns(a[n][l]) for n in (
        "norm_mix_pre", "norm_mix_post", "norm_mem_pre", "norm_mem_post", "norm_memkv", "norm_ffn_pre", "norm_ffn_post",
        "pool_scale", "conv_b_w", "conv_ffn_w")], axis=1) for l in range(DEPTH)], axis=1)

    gq, gk = (np.tile(a["qk_norm_a_2"][0, i], 2)[:, None] for i in range(2))
    params2 = np.concatenate([columns(a["norm_g_2"]), columns(a["b_mod_2"]), gq, gk, columns(a["diff_subln_2"]), gq, gq, gq, gq, gk,
                              np.kron(np.eye(2), np.ones((HD, HD))).astype(f4)], axis=1)
    small2 = np.concatenate([a["diff_lambda_2"][0].ravel(), a["sink_c_2"][0]])
    w = 2 * HD - 1
    rpb = np.zeros((2 * HEADS, DR + 1, w), f4)
    rpb[:, :, 48:48 + 31] = a["rpb_d_2"][0]

    gd = 3 * D // 8 // 4
    diag = np.zeros((DEPTH, POOL * P, POOL * P), f4)
    for g in range(4):
        diag[:, g * gd:(g + 1) * gd, g * gd:(g + 1) * gd] = a["pool_w"][:, g]
    poolw = np.stack([diag[:, k * P:(k + 1) * P, c * P:(c + 1) * P] for c, k in (
        (0, 0), (0, 1), (1, 0), (1, 1), (1, 2), (2, 1), (2, 2))], axis=2)

    consts = np.zeros((P, 2 * P + 64), f4)
    consts[:, :P] = np.eye(P)
    consts[:, P:2 * P] = 1.0
    col = consts[:, 2 * P:2 * P + 16]
    col[:, 0] = EPS
    rot = HD // 4
    inv = (f4(500000.0) ** (-np.arange(0, rot, 2, dtype=f4) / f4(rot))).astype(f4)
    for p in range(P):
        d = p % HD
        if d < rot:
            col[p, 1] = inv[d % (rot // 2)]
            col[p, 2] = -1.0 if d < rot // 2 else 1.0
    for c in range(POOL):
        for p in range(P):
            w = (2, 4, 8, 16)[(c * P + p) // gd]
            col[p, 4 + c] = 1.0 / w
            consts[p, 2 * P + 16 + 16 * c:2 * P + 32 + 16 * c] = 1.0 / np.minimum(np.arange(16) + 1, w)
    i = np.arange(P)[:, None]
    j = np.arange(T + 3)[None]
    gap = 4 * i - (j - 3)
    k = np.arange(P)[None]
    masks = np.concatenate([np.where((gap >= 0) & (gap <= 128), 0, NEG), np.where(k <= i, 0, NEG),
                            np.where((k <= i) & ((i - k) % 4 == 0), 0, NEG)], axis=1).astype(f4)

    t = np.arange(T)
    inv2 = (f4(10000.0) ** (-np.arange(16, dtype=f4) / f4(16))).astype(f4)
    d = np.arange(P) % HD
    pos = np.stack([t // 64, t % 64]).astype(f4)[d // 32]
    ang = (pos * inv2[d % 16][:, None]).astype(f4)
    rope2 = np.concatenate([np.cos(ang), np.sin(ang) * np.where(d // 16 % 2, 1, -1)[:, None]], axis=1).astype(f4)
    jj = np.arange(BW)[None]
    cq = (np.arange(P) % 64)[:, None]
    ck = np.arange(64)[None]
    cs = np.clip(cq - 8, 0, 48)
    band = np.concatenate([np.where(abs(jj - 3 * P - i) <= 128, 0, NEG), np.where((ck >= cs) & (ck < cs + 16), 0, NEG)], axis=1).astype(f4)

    ins = {
        "stream": stream, "modw": modw, "crow": np.concatenate([a["c_2"][0], a["c_ctx_2"]]), "x": feature_major(a["x"][0]), "ctx": feature_major(a["ctx_2"][0]), "params2": params2,
        "cvec": np.stack([columns(a["c_2"][0]), columns(a["c_ctx_2"])], axis=2), "small2": small2, "rope2": rope2, "band": band, "rpb": rpb, "mem": feature_major(a["mem"][0]),
        "params1": par, "positions": a["positions"][0], "consts": consts, "poolw": poolw, "masks": masks,
    }
    nc = bacc.Bacc("TRN2", target_bir_lowering=False, num_devices=1)
    t = np.arange(T)
    inv2 = (f4(10000.0) ** (-np.arange(16, dtype=f4) / f4(16))).astype(f4)
    d = np.arange(P) % HD
    pos = np.stack([t // 64, t % 64]).astype(f4)[d // 32]
    ang = (pos * inv2[d % 16][:, None]).astype(f4)
    rope2 = np.concatenate([np.cos(ang), np.sin(ang) * np.where(d // 16 % 2, 1, -1)[:, None]], axis=1).astype(f4)
    jj = np.arange(BW)[None]
    cq = (np.arange(P) % 64)[:, None]
    ck = np.arange(64)[None]
    cs = np.clip(cq - 8, 0, 48)
    band = np.concatenate([np.where(abs(jj - 3 * P - i) <= 128, 0, NEG), np.where((ck >= cs) & (ck < cs + 16), 0, NEG)], axis=1).astype(f4)

    ins = {n: np.ascontiguousarray(v) for n, v in ins.items()}
    args = {n: nc.dram_tensor("in_" + n, v.shape, mybir.dt.from_np(v.dtype), kind="ExternalInput").ap() for n, v in ins.items()}
    out = nc.dram_tensor("out", (D, T), F32, kind="ExternalOutput").ap()
    build(nc, out=out, **args)
    r = run_bass_kernel_spmd(nc, [{"in_" + n: v for n, v in ins.items()}], core_ids=[0])
    return np.ascontiguousarray(r.results[0]["out"].T)[None]
```
